# Optimizing a Trainium2 kernel written in Bass

```python
import math
import jax, jax.numpy as jnp
from jax import lax
import numpy as np

D_MODEL = 1024
BATCH = 1
SEQ = 512
DEPTH = 2

HEAD_DIM = 64
ROPE_THETA = 10000.0
EPS = 1e-6
NEG_INF = -1e30
Q_BLOCK = 128
MLA_HEADS = 4
MLA_Q_RANK = 256
MLA_KV_RANK = 128
MLA_NOPE = 64
MLA_ROPE = 32
MLA_V = 64
SWA_HEADS = 4
SWA_KV_HEADS = 2
SWA_WINDOW = 128
DIFF_HEADS = 4
DIFF_QK = 32
DIFF_V = 2 * DIFF_QK
HY_CH = 256
HY_ORDER = 2
HY_DIRS = 2
HY_SHORT = 3
HY_EMB = 33
HY_BANDS = (HY_EMB - 1) // 2
HY_FFN = 64
HY_TARGET = 1e-2
HY_MIN_DECAY = math.log(HY_TARGET) / 1.5
HY_MAX_DECAY = math.log(HY_TARGET) / 0.3
MLA_COLS = MLA_Q_RANK + MLA_KV_RANK + MLA_ROPE
SWA_COLS = (SWA_HEADS + 2 * SWA_KV_HEADS) * HEAD_DIM
DIFF_COLS = DIFF_HEADS * (4 * DIFF_QK + DIFF_V)
HY_COLS = (HY_ORDER + 1) * HY_CH
IN_COLS = MLA_COLS + SWA_COLS + DIFF_COLS + HY_COLS
D_MIX = MLA_HEADS * MLA_V + SWA_HEADS * HEAD_DIM + DIFF_HEADS * DIFF_V + HY_CH
N_GROUPS = 4
EXPERTS_PER_GROUP = 8
N_EXPERTS = N_GROUPS * EXPERTS_PER_GROUP
TOP_K = 2
D_EXPERT = 256
MOE_BLOCK = 128

kernel_name = 'hybrid_parallel_heads_hier_moe_encoder'

def rms_norm(x, g):
    x32 = x.astype(jnp.float32)
    y = x32 * lax.rsqrt(jnp.mean(x32 * x32, axis=-1, keepdims=True) + EPS)
    return (y * g.astype(jnp.float32)).astype(x.dtype)

def rope(x, positions):
    half = x.shape[-1] // 2
    inv_freq = jnp.exp(-math.log(ROPE_THETA) * jnp.arange(half, dtype=jnp.float32) / half)
    ang = positions.astype(jnp.float32)[:, None, :, None] * inv_freq
    cos, sin = jnp.cos(ang), jnp.sin(ang)
    x32 = x.astype(jnp.float32)
    x1, x2 = x32[..., :half], x32[..., half:]
    return jnp.concatenate([x1 * cos - x2 * sin, x1 * sin + x2 * cos], axis=-1).astype(x.dtype)

def to_heads(t, n_heads):
    B, S, _ = t.shape
    return t.reshape(B, S, n_heads, -1).transpose(0, 2, 1, 3)

def from_heads(t):
    B, H, S, d = t.shape
    return t.transpose(0, 2, 1, 3).reshape(B, S, H * d)

def query_blocks(q):
    B, H, S, d = q.shape
    return jnp.moveaxis(q.reshape(B, H, S // Q_BLOCK, Q_BLOCK, d), 2, 0)

def merge_query_blocks(o):
    nb, B, H, qb, d = o.shape
    return jnp.moveaxis(o, 0, 2).reshape(B, H, nb * qb, d)

def dense_attention(q, k, v, scale):
    def attend(qi):
        s = jnp.einsum('bhqd,bhkd->bhqk', qi, k).astype(jnp.float32) * scale
        p = jax.nn.softmax(s, axis=-1)
        return jnp.einsum('bhqk,bhkd->bhqd', p.astype(v.dtype), v)
    return merge_query_blocks(lax.map(attend, query_blocks(q)))

def mla_mixer(cols, positions, q_norm, kv_norm, w_uq, w_ukv):
    c_q, c_kv, k_pe = jnp.split(cols, [MLA_Q_RANK, MLA_Q_RANK + MLA_KV_RANK], axis=-1)
    q = to_heads(rms_norm(c_q, q_norm) @ w_uq, MLA_HEADS)
    kv = to_heads(rms_norm(c_kv, kv_norm) @ w_ukv, MLA_HEADS)
    q_nope, q_pe = q[..., :MLA_NOPE], q[..., MLA_NOPE:]
    k_nope, v = kv[..., :MLA_NOPE], kv[..., MLA_NOPE:]
    k_pe = rope(k_pe[:, None], positions)
    q = jnp.concatenate([q_nope, rope(q_pe, positions)], axis=-1)
    k = jnp.concatenate([k_nope, jnp.broadcast_to(k_pe, k_nope.shape[:-1] + (MLA_ROPE,))], axis=-1)
    o = dense_attention(q, k, v, (MLA_NOPE + MLA_ROPE) ** -0.5)
    return from_heads(o)

def band_blocks(t):
    B, H, S, d = t.shape
    nb = S // SWA_WINDOW
    tp = jnp.pad(t, ((0, 0), (0, 0), (SWA_WINDOW, SWA_WINDOW), (0, 0)))
    tp = tp.reshape(B, H, nb + 2, SWA_WINDOW, d)
    return jnp.concatenate([tp[:, :, :-2], tp[:, :, 1:-1], tp[:, :, 2:]], axis=3)

def swa_mixer(cols, positions, sink):
    B, S, _ = cols.shape
    W = SWA_WINDOW
    nb = S // W
    G = SWA_HEADS // SWA_KV_HEADS
    q, k, v = jnp.split(cols, [SWA_HEADS * HEAD_DIM, (SWA_HEADS + SWA_KV_HEADS) * HEAD_DIM], axis=-1)
    q = rope(to_heads(q, SWA_HEADS), positions).reshape(B, SWA_KV_HEADS, G, nb, W, HEAD_DIM)
    kb = band_blocks(rope(to_heads(k, SWA_KV_HEADS), positions))
    vb = band_blocks(to_heads(v, SWA_KV_HEADS))
    s = jnp.einsum('bhgnqd,bhnkd->bhgnqk', q, kb).astype(jnp.float32) * HEAD_DIM ** -0.5
    qi = jnp.arange(W)[:, None]
    kj = jnp.arange(3 * W)[None, :]
    band = jnp.abs(kj - W - qi) <= W
    kpos = (jnp.arange(nb)[:, None] - 1) * W + jnp.arange(3 * W)[None, :]
    valid = band[None] & ((kpos >= 0) & (kpos < S))[:, None, :]
    s = jnp.where(valid, s, NEG_INF)
    sink32 = sink.astype(jnp.float32).reshape(1, SWA_KV_HEADS, G, 1, 1, 1)
    m = jnp.maximum(jnp.max(s, axis=-1, keepdims=True), sink32)
    e = jnp.exp(s - m)
    p = e / (jnp.sum(e, axis=-1, keepdims=True) + jnp.exp(sink32 - m))
    o = jnp.einsum('bhgnqk,bhnkd->bhgnqd', p.astype(vb.dtype), vb)
    return from_heads(o.reshape(B, SWA_HEADS, S, HEAD_DIM))

def diff_mixer(cols, positions, lam_vecs, norm_g, lambda_init):
    B, S, _ = cols.shape
    q, k, v = jnp.split(cols, [DIFF_HEADS * 2 * DIFF_QK, DIFF_HEADS * 4 * DIFF_QK], axis=-1)
    q = q.reshape(B, S, DIFF_HEADS, 2, DIFF_QK)
    k = k.reshape(B, S, DIFF_HEADS, 2, DIFF_QK)
    q1 = rope(q[..., 0, :].transpose(0, 2, 1, 3), positions)
    q2 = rope(q[..., 1, :].transpose(0, 2, 1, 3), positions)
    k1 = rope(k[..., 0, :].transpose(0, 2, 1, 3), positions)
    k2 = rope(k[..., 1, :].transpose(0, 2, 1, 3), positions)
    v = to_heads(v, DIFF_HEADS)
    lv = lam_vecs.astype(jnp.float32)
    lam = jnp.exp(jnp.sum(lv[0] * lv[1])) - jnp.exp(jnp.sum(lv[2] * lv[3])) + lambda_init
    scale = DIFF_QK ** -0.5

    def attend(qs):
        q1i, q2i = qs
        p1 = jax.nn.softmax(jnp.einsum('bhqd,bhkd->bhqk', q1i, k1).astype(jnp.float32) * scale, axis=-1)
        p2 = jax.nn.softmax(jnp.einsum('bhqd,bhkd->bhqk', q2i, k2).astype(jnp.float32) * scale, axis=-1)
        return jnp.einsum('bhqk,bhkd->bhqd', (p1 - lam * p2).astype(v.dtype), v)

    o = merge_query_blocks(lax.map(attend, (query_blocks(q1), query_blocks(q2))))
    o = rms_norm(o, norm_g) * (1.0 - lambda_init)
    return from_heads(o)

def hyena_filters(L, w1, b1, w2, b2, w3, b3, w4, sin_freq):
    t = jnp.linspace(0.0, 1.0, L, dtype=jnp.float32)
    w = 2.0 * math.pi * jnp.arange(L, dtype=jnp.float32) / L
    f = jnp.linspace(1e-4, HY_BANDS - 1, HY_BANDS, dtype=jnp.float32)
    z = jnp.concatenate([t[:, None], jnp.cos(w[:, None] * f), -jnp.sin(w[:, None] * f)], axis=-1)
    z = z.astype(w1.dtype)
    h = jnp.sin(sin_freq[0] * (z @ w1 + b1))
    h = jnp.sin(sin_freq[1] * (h @ w2 + b2))
    h = jnp.sin(sin_freq[2] * (h @ w3 + b3))
    h = (h @ w4).astype(jnp.float32).reshape(L, HY_DIRS, HY_ORDER, HY_CH)
    decay = jnp.linspace(HY_MIN_DECAY, HY_MAX_DECAY, HY_CH, dtype=jnp.float32)
    window = jnp.exp(-t[:, None] * jnp.abs(decay))
    return h * window[:, None, None, :]

def two_sided_filter(h_fwd, h_bwd):
    C = h_fwd.shape[-1]
    filt = jnp.concatenate([h_fwd[:1] + h_bwd[:1], h_fwd[1:], jnp.zeros((1, C), h_fwd.dtype), h_bwd[:0:-1]], axis=0)
    return filt * lax.rsqrt(jnp.sum(filt * filt, axis=0, keepdims=True) + EPS)

def fft_long_conv(u, filt, bias):
    L = u.shape[1]
    u32 = u.astype(jnp.float32)
    U = jnp.fft.rfft(u32, n=2 * L, axis=1)
    F = jnp.fft.rfft(filt, axis=0)
    y = jnp.fft.irfft(U * F[None], n=2 * L, axis=1)[:, :L]
    return (y + u32 * bias.astype(jnp.float32)).astype(u.dtype)

def hyena_mixer(cols, conv_w, conv_b, w1, b1, w2, b2, w3, b3, w4, sin_freq, bias):
    B, S, C_in = cols.shape
    u = lax.conv_general_dilated(cols, conv_w[:, None, :], (1,), [(HY_SHORT // 2, HY_SHORT // 2)],
                                 dimension_numbers=('NWC', 'WIO', 'NWC'),
                                 feature_group_count=C_in) + conv_b
    v, x1, x2 = jnp.split(u, HY_ORDER + 1, axis=-1)
    filters = hyena_filters(S, w1, b1, w2, b2, w3, b3, w4, sin_freq)
    z = v
    for o, gate in enumerate((x1, x2)):
        z = gate * fft_long_conv(z, two_sided_filter(filters[:, 0, o], filters[:, 1, o]), bias[o])
    return z

def grouped_expert_ffn(ht, expert_idx, gate, w_gate, w_up, w_down):
    T, D = ht.shape
    E = w_gate.shape[0]
    A = T * TOP_K
    flat_e = expert_idx.reshape(A)
    flat_tok = jnp.repeat(jnp.arange(T, dtype=jnp.int32), TOP_K)
    flat_g = gate.reshape(A)
    order = jnp.argsort(flat_e)
    se = flat_e[order]
    counts = jnp.bincount(flat_e, length=E)
    padded = (counts + MOE_BLOCK - 1) // MOE_BLOCK * MOE_BLOCK
    pad_end = jnp.cumsum(padded)
    pad_start = pad_end - padded
    start = jnp.cumsum(counts) - counts
    dest = pad_start[se] + (jnp.arange(A, dtype=jnp.int32) - start[se])
    n_blocks = (A + E * (MOE_BLOCK - 1) + MOE_BLOCK - 1) // MOE_BLOCK
    P = n_blocks * MOE_BLOCK
    slot_tok = jnp.full((P,), T, jnp.int32).at[dest].set(flat_tok[order])
    slot_gate = jnp.zeros((P,), flat_g.dtype).at[dest].set(flat_g[order])
    block_expert = jnp.minimum(
        jnp.searchsorted(pad_end, jnp.arange(n_blocks, dtype=jnp.int32) * MOE_BLOCK, side='right'), E - 1)
    h_pad = jnp.concatenate([ht, jnp.zeros((1, D), ht.dtype)], axis=0)
    xb = h_pad[slot_tok].reshape(n_blocks, MOE_BLOCK, D)

    def expert_block(args):
        xe, e = args
        return (jax.nn.silu(xe @ w_gate[e]) * (xe @ w_up[e])) @ w_down[e]

    yb = lax.map(expert_block, (xb, block_expert)).reshape(P, D)
    y = jnp.zeros((T + 1, D), ht.dtype).at[slot_tok].add(yb * slot_gate[:, None].astype(yb.dtype))
    return y[:T]

def hier_moe(h, rg_w, rg_b, re_w, re_b, w_gate, w_up, w_down):
    B, S, D = h.shape
    T = B * S
    ht = h.reshape(T, D)
    pg = jax.nn.softmax((ht @ rg_w + rg_b).astype(jnp.float32), axis=-1)
    pg_top, g_sel = lax.top_k(pg, 1)
    le = (ht @ re_w + re_b).astype(jnp.float32).reshape(T, N_GROUPS, EXPERTS_PER_GROUP)
    idx = jnp.broadcast_to(g_sel[:, :, None], (T, 1, EXPERTS_PER_GROUP))
    le_sel = jnp.take_along_axis(le, idx, axis=1)[:, 0]
    top_v, top_i = lax.top_k(le_sel, TOP_K)
    expert_idx = g_sel * EXPERTS_PER_GROUP + top_i
    gate = pg_top * jax.nn.softmax(top_v, axis=-1)
    return grouped_expert_ffn(ht, expert_idx, gate, w_gate, w_up, w_down).reshape(B, S, D)

def setup_inputs(seed: int = 0) -> dict:
    key = jax.random.key(seed)
    ks = iter(jax.random.split(key, 48))

    def nrm(shape, scale):
        return scale * jax.random.normal(next(ks), shape, jnp.float32)

    L, D = DEPTH, D_MODEL
    return {
        'x': nrm((BATCH, SEQ, D), 1.0),
        'c': nrm((BATCH, D), 1.0),
        'positions': jnp.broadcast_to(jnp.arange(SEQ, dtype=jnp.int32), (BATCH, SEQ)),
        'ln1_g': 1.0 + nrm((L, D), 0.02),
        'ln2_g': 1.0 + nrm((L, D), 0.02),
        'ada_w': nrm((L, D, 6 * D), 0.5 * D ** -0.5),
        'ada_b': nrm((L, 6 * D), 0.02),
        'w_in': nrm((L, D, IN_COLS), D ** -0.5),
        'mla_q_norm': 1.0 + nrm((L, MLA_Q_RANK), 0.02),
        'mla_kv_norm': 1.0 + nrm((L, MLA_KV_RANK), 0.02),
        'mla_w_uq': nrm((L, MLA_Q_RANK, MLA_HEADS * (MLA_NOPE + MLA_ROPE)), MLA_Q_RANK ** -0.5),
        'mla_w_ukv': nrm((L, MLA_KV_RANK, MLA_HEADS * (MLA_NOPE + MLA_V)), MLA_KV_RANK ** -0.5),
        'swa_sink': nrm((L, SWA_HEADS), 0.5),
        'diff_lambda': nrm((L, 4, DIFF_QK), 0.1),
        'diff_norm_g': 1.0 + nrm((L, DIFF_V), 0.02),
        'hy_conv_w': nrm((L, HY_SHORT, HY_COLS), HY_SHORT ** -0.5),
        'hy_conv_b': nrm((L, HY_COLS), 0.02),
        'hy_w1': nrm((L, HY_EMB, HY_FFN), HY_EMB ** -0.5),
        'hy_b1': nrm((L, HY_FFN), 0.02),
        'hy_w2': nrm((L, HY_FFN, HY_FFN), HY_FFN ** -0.5),
        'hy_b2': nrm((L, HY_FFN), 0.02),
        'hy_w3': nrm((L, HY_FFN, HY_FFN), HY_FFN ** -0.5),
        'hy_b3': nrm((L, HY_FFN), 0.02),
        'hy_w4': nrm((L, HY_FFN, HY_DIRS * HY_ORDER * HY_CH), HY_FFN ** -0.5),
        'hy_sin_freq': 1.0 + nrm((L, 3, HY_FFN), 0.02),
        'hy_bias': nrm((L, HY_ORDER, HY_CH), 0.1),
        'w_out': nrm((L, D_MIX, D), D_MIX ** -0.5),
        'router_g_w': nrm((L, D, N_GROUPS), D ** -0.5),
        'router_g_b': nrm((L, N_GROUPS), 0.01),
        'router_e_w': nrm((L, D, N_EXPERTS), D ** -0.5),
        'router_e_b': nrm((L, N_EXPERTS), 0.01),
        'moe_w_gate': nrm((L, N_EXPERTS, D, D_EXPERT), D ** -0.5),
        'moe_w_up': nrm((L, N_EXPERTS, D, D_EXPERT), D ** -0.5),
        'moe_w_down': nrm((L, N_EXPERTS, D_EXPERT, D), D_EXPERT ** -0.5),
        'final_g': 1.0 + nrm((D,), 0.02),
    }

def reference(x, c, positions, ln1_g, ln2_g, ada_w, ada_b, w_in, mla_q_norm, mla_kv_norm,
              mla_w_uq, mla_w_ukv, swa_sink, diff_lambda, diff_norm_g, hy_conv_w, hy_conv_b,
              hy_w1, hy_b1, hy_w2, hy_b2, hy_w3, hy_b3, hy_w4, hy_sin_freq, hy_bias, w_out,
              router_g_w, router_g_b, router_e_w, router_e_b, moe_w_gate, moe_w_up, moe_w_down,
              final_g):
    c_act = jax.nn.silu(c)
    split_at = [MLA_COLS, MLA_COLS + SWA_COLS, MLA_COLS + SWA_COLS + DIFF_COLS]
    for l in range(DEPTH):
        mod = (c_act @ ada_w[l] + ada_b[l])[:, None, :]
        sh1, sc1, g1, sh2, sc2, g2 = jnp.split(mod, 6, axis=-1)
        h = rms_norm(x, ln1_g[l]) * (1.0 + sc1) + sh1
        cols = h @ w_in[l]
        c_a, c_b, c_c, c_d = jnp.split(cols, split_at, axis=-1)
        y_a = mla_mixer(c_a, positions, mla_q_norm[l], mla_kv_norm[l], mla_w_uq[l], mla_w_ukv[l])
        y_b = swa_mixer(c_b, positions, swa_sink[l])
        lambda_init = 0.8 - 0.6 * math.exp(-0.3 * l)
        y_c = diff_mixer(c_c, positions, diff_lambda[l], diff_norm_g[l], lambda_init)
        y_d = hyena_mixer(c_d, hy_conv_w[l], hy_conv_b[l], hy_w1[l], hy_b1[l], hy_w2[l], hy_b2[l],
                          hy_w3[l], hy_b3[l], hy_w4[l], hy_sin_freq[l], hy_bias[l])
        mix = jnp.concatenate([y_a, y_b, y_c, y_d], axis=-1)
        x = x + g1 * (mix @ w_out[l])
        h = rms_norm(x, ln2_g[l]) * (1.0 + sc2) + sh2
        x = x + g2 * hier_moe(h, router_g_w[l], router_g_b[l], router_e_w[l], router_e_b[l],
                              moe_w_gate[l], moe_w_up[l], moe_w_down[l])
    return rms_norm(x, final_g)


_drawn_inputs = setup_inputs


def setup_inputs(seed=0):
    import zlib

    import numpy as np

    out = dict(_drawn_inputs(seed))
    spreads = {}
    factors = {'ln1_g': 2.891,
     'ln2_g': 3.076,
     'mla_q_norm': 8.0,
     'mla_kv_norm': 8.0,
     'swa_sink': 64.0,
     'diff_norm_g': 8.0,
     'router_g_b': 7.176,
     'router_e_b': 5.769,
     'final_g': 8.101}
    for name, (base, spread) in spreads.items():
        noise = np.random.default_rng([zlib.crc32(name.encode()), seed]).standard_normal(out[name].shape)
        drawn = base * np.exp(spread * noise) if base else spread * noise
        out[name] = __import__('jax').numpy.asarray(drawn.astype(out[name].dtype))
    for name, factor in factors.items():
        out[name] = (out[name] * factor).astype(out[name].dtype)
    return out
```

```python
from contextlib import ExitStack
import math

import numpy as np
import concourse.bass as bass
from concourse import mybir

F32 = mybir.dt.float32
I32 = mybir.dt.int32
ALU = mybir.AluOpType
ACT = mybir.ActivationFunctionType
X = mybir.AxisListType.X

P = 128
DEPTH, D, S = 2, 1024, 512
NT = S // P
KT = D // P
EPS = 1e-6
NEG = -1e30
MAGIC = 1.5 * 2.0 ** 23

A_COLS, B_COLS, C_COLS, D_COLS = 416, 512, 768, 768
IN_COLS = A_COLS + B_COLS + C_COLS + D_COLS
NH = 4
MLA_SCALE = 96.0 ** -0.5
SWA_SCALE = 0.125
DIFF_SCALE = 32.0 ** -0.5
CH = 256

SLOT = 6144
ADA = 768
N_ADA = 6 * D // ADA
NE, NG, EPG, F = 32, 4, 8, 256
CAP = 64
EXTRA = 2 * S // CAP - 1
EMPTY = 4096.0


def host_constants():
    t = np.arange(S, dtype=np.float64)
    k = np.arange(S, dtype=np.float64)
    ang = 2 * np.pi * ((t[:, None] * k[None, :]) % (2 * S)) / (2 * S)
    cos, sin = np.cos(ang), np.sin(ang)
    alt = 1.0 - 2.0 * (np.arange(S) % 2)
    sin_f = sin[:, :P].copy()
    sin_f[:, 0] = alt
    sin_i = sin[:P, :].copy()
    sin_i[0, :] = alt
    tl = np.linspace(0.0, 1.0, S, dtype=np.float32)
    w = (2.0 * math.pi * np.arange(S, dtype=np.float32) / S).astype(np.float32)
    f = np.linspace(1e-4, 15, 16, dtype=np.float32)
    wf = (w[:, None] * f).astype(np.float32)
    z = np.concatenate([tl[:, None], np.cos(wf), -np.sin(wf)], axis=-1)
    decay = np.linspace(math.log(1e-2) / 1.5, math.log(1e-2) / 0.3, CH, dtype=np.float32)
    window = np.exp(-tl[:, None] * np.abs(decay))
    q = np.arange(P)
    mask = np.zeros((P, 3 * P))
    mask[:, :P] = np.where(q[None, :] >= q[:, None], 0.0, NEG)
    mask[:, 2 * P:] = np.where(q[None, :] <= q[:, None], 0.0, NEG)
    inv = [np.exp(-math.log(10000.0) * np.arange(h, dtype=np.float32) / h) for h in (16, 32)]
    lam = [[0.8 - 0.6 * math.exp(-0.3 * l), 1.0 - (0.8 - 0.6 * math.exp(-0.3 * l))] for l in range(DEPTH)]
    tri = (q[:, None] < q[None, :]) * 1.0
    grid = np.arange(NE * 7)
    block_id = (grid // 7) * 8 + grid % 7 + 1
    block_at = (grid % 7 + 1) * float(CAP)
    desc = np.arange(EPG, 0, -1)
    misc = np.concatenate([np.arange(NE), desc])
    out = {"k_cos": cos, "k_sin": sin, "k_sin_f": sin_f, "k_sin_i": sin_i, "k_z": z.T, "k_window": window,
           "k_mask": mask, "k_inv": np.concatenate(inv)[None], "k_lam": np.array(lam), "k_tri": tri,
           "k_ident": np.eye(P), "k_misc": misc[None], "k_blocks": np.stack([block_id, block_at]), "k_empty": np.full((P, S * NE // P), EMPTY)}
    return {n: np.ascontiguousarray(a, dtype=np.float32) for n, a in out.items()}


def trunk(nc, a, out):
    h2_rows = nc.dram_tensor("h2_rows", (S, D), F32, kind="Internal").ap()
    slots_of = nc.dram_tensor("slots_of", (S * NE, 1), F32, kind="Internal").ap()
    pair_rows = nc.dram_tensor("pair_rows", (2 * S, D), F32, kind="Internal").ap()

    ctx = ExitStack()
    with ctx:
        def sb(name, shape, dt=F32):
            return ctx.enter_context(nc.sbuf_tensor(name, shape, dt))

        layer_sems = []

        def sem(name, per_layer=True):
            s = ctx.enter_context(nc.semaphore(name))
            if per_layer:
                layer_sems.append(s)
            return s

        ARENA = 2 * SLOT
        ARENA_WORDS = 18432
        big = sb("big", [P, ARENA + ARENA_WORDS])
        x_tok = sb("x_tok", [P, NT, D])
        mod = sb("mod", [P, 4, D])
        ht_r = sb("ht_r", [P, 4096])
        mix_r = sb("mix_r", [P, 3072])
        ydT = sb("ydT", [P, 2, S])
        pr_r = sb("pr_r", [P, 2560])
        c_rep = sb("c_rep", [P, KT, P])
        res_tmp = sb("res_tmp", [P, 512])
        rope_t = sb("rope_t", [P, NT, 96])
        ident = sb("ident", [P, P])
        ones = sb("ones", [P, P])
        tri = sb("tri", [P, P])
        mask = sb("mask", [P, 3 * P])
        small = sb("small", [P, 672])
        gather_i = sb("gather_i", [P, 2], I32)
        scatter_i = sb("scatter_i", [P, 2], I32)
        over_i = sb("over_i", [1, 16], I32)
        tot_i = sb("tot_i", [1, 2], I32)

        def at(buf, off, *dims, rows=P):
            n = int(np.prod(dims))
            v = buf[0:rows, off:off + n]
            if len(dims) == 1:
                return v
            names = "abcd"[:len(dims)]
            return v.rearrange(f"p ({' '.join(names)}) -> p {' '.join(names)}", **{names[i]: dims[i] for i in range(len(dims))})

        small_at = [0]

        def sm(n, rows=P):
            o = small_at[0]
            small_at[0] += n
            assert small_at[0] <= 672, small_at
            return small[0:rows, o:o + n]

        def slot(s, *dims):
            return at(big, s * SLOT, *dims)

        def ar(off, *dims, rows=P):
            return at(big, ARENA + off, *dims, rows=rows)

        cosm, sinm = ar(0, NT, S), ar(2048, NT, S)
        sin_f, sin_i = ar(4096, NT, P), ar(4608, S)
        fc, fd, fcn = ar(5120, NT, S), ar(7168, NT, S), ar(9216, S)
        fsum, fdif = ar(9728, NT, S), ar(11776, NT, S)
        yre, yim = ar(9728, NT, CH), ar(10752, NT, CH)
        cm = ar(11776, 2, 2, S)
        vxT = ar(13824, 4, S)
        vx_tok = ar(15872, NT, 2 * CH)
        sq_sum, sq_dif = ar(13824, NT, S), ar(15872, NT, S)
        cols_b, cols_c = ar(0, NT, B_COLS), ar(2048, NT, C_COLS)
        kv_tok, cT, k_tok = ar(5120, NT, S), ar(7168, 3, S), ar(8704, NT, NH, 96)
        qT_a, kT_a = ar(10240, NH, S), ar(12288, NH, S)
        rope_b = ar(14336, NT, 384)
        w_uq, w_ukv = ar(14336, 2, 384), ar(14336 + 768, S)
        qT_b, kT_b = ar(15872, NH, S), ar(15872 + 2048, S)
        rope_c, kT_c = ar(7168, NT, S), ar(7168 + 2048, 2, S)
        qT_c = at(ht_r, 0, 8, S)
        hT = at(ht_r, 0, KT, S)
        mixT = at(ht_r, 0, 6, S)
        w4, zT = at(ht_r, 0, D, rows=64), at(ht_r, 1024, S, rows=33)
        bias_b, s_b, window = at(ht_r, 1536, S), at(ht_r, 2048, S), at(ht_r, 2560, NT, CH)
        sh1, gsc1, ln1 = (at(mix_r, 1024 * j, D) for j in range(3))
        cols_a = at(mix_r, 0, NT, A_COLS)
        mix_tok = at(mix_r, 0, NT, 768)
        h_tok = at(pr_r, 0, 2, D)
        f_tmp = at(pr_r, 2048, S)
        mlp_y, mlp_k, mlp_h = (at(pr_r, 512 * j, S, rows=64) for j in range(3))
        q_tok = at(pr_r, 0, NT, 384)
        rp = [at(pr_r, 1536 + 256 * j, 256) for j in range(4)]
        prob, probT = at(pr_r, 0, 3, S), at(pr_r, 1536, 2, S)
        ln2 = ar(12288, D)
        xg, yg = at(ht_r, 0, 2, D), at(ht_r, 2048, 2, D)
        xT = at(pr_r, 0, 2, KT * CAP)
        sil, act_h, act_T = at(pr_r, 1024, 2, F), at(pr_r, 1536, 2, F), at(pr_r, 2048, 2, P)
        pair = ar(12288, 2, 2, D)
        comb = ar(12288 + 4096, D)
        rt = [0]

        def rb(*dims, rows=P):
            o = rt[0]
            rt[0] += int(np.prod(dims))
            assert rt[0] <= 3072, rt
            return at(mix_r, o, *dims, rows=rows)

        lgT = rb(S, rows=36)
        lg = rb(NT, 36)
        m1, m2 = rb(NT, NE), rb(NT, NE)
        msum = rb(NT, NE)
        cum = rb(NT, NE)
        r_tmp = rb(NT, NE)
        r_tmp2 = rb(NT, EPG)
        og, o1, o2, le = rb(NT, NG), rb(NT, EPG), rb(NT, EPG), rb(NT, EPG)
        rd = rb(NT, NG)
        gmax, pg, v1, v2, vd = (rb(NT) for _ in range(5))
        wgt = rb(2, NT)
        dest_f = rb(2, NT)
        slot_f, gidx_f, hi_f = rb(NE), rb(NE), rb(NE)
        cnt = rb(NE)
        flag, pos, pick = rb(NE * 7), rb(NE * 7), rb(NE * 7)
        o_code = rb(2)
        block_id, block_at = rb(NE * 7), rb(NE * 7)
        o_idx = rb(4)
        r_w = rb(KT, 36)
        dest_i = sb("dest_i", [P, 2, NT], I32)
        slot_i = sb("slot_i", [P, NE], I32)
        gslot_i = sb("gslot_i", [P, NE], I32)

        c_act = sm(KT)
        hw1, hw2, hw3 = sm(64, 33), sm(64, 64), sm(64, 64)
        hb, hf = sm(3, 64), sm(3, 64)
        conv_w, conv_b = sm(18), sm(6)
        lred, lexp, lam_b, neglam = sm(2), sm(2), sm(2), sm(1)
        gd, gn = sm(64), sm(3)
        sink = sm(NH)
        nss, nrs, ns2 = sm(NT), sm(NT), sm(NT)
        css, crs = sm(2 * NT), sm(2 * NT)
        lv = sm(P)
        mx, nm, rs = lv[:, 0:64], lv[:, 64:P], sm(64)
        c_sb, pos_f = lv[:, 0:KT], rs[:, 0:NT]
        esink, den = sm(16), sm(16)
        kap = sm(16)
        dss, drs = sm(16), sm(16)
        invf = sm(48)
        r_b = sm(1, 36)
        tok_id = sm(2 * NT)
        part_id = sm(1)
        over_tot, neghalf = sm(2), sm(1)
        misc = sb("misc", [P, NE + EPG])
        pos_i = sb("pos_i", [P, NT], I32)
        iota_e = misc[:, 0:NE]
        desc8 = misc[:, NE:NE + EPG]

        bank = [ctx.enter_context(nc.psum_tensor(f"bank{i}", [P, 512], F32)) for i in range(8)]

        first_load = sem("first_load", False)
        layer_done = sem("layer_done", False)
        layer_go = sem("layer_go", False)
        fin_sq, fin_mid, fin_rs, fin_row = (sem(n, False) for n in "fin_sq fin_mid fin_rs fin_row".split())
        out_row = [sem(f"out_row{i}", False) for i in range(2)]
        table_dma = sem("table_dma", False)
        gathered = [sem(f"gathered{i}", False) for i in range(2)]
        scattered = [sem(f"scattered{i}", False) for i in range(2)]
        over_gathered, over_scattered = sem("over_gathered", False), sem("over_scattered", False)

        ready_v, ready_a = sem("ready_v"), sem("ready_a")
        taken_v, taken_a = sem("taken_v"), sem("taken_a")
        v_step, a_step, g_step = sem("v_step"), sem("a_step"), sem("g_step")
        slot_full = [sem(f"slot_full{i}") for i in range(4)]
        hy_in, dft_in, mod_in, ln2_in, mla_w_in, fill_in, rw_in, tab_in, ov_i = (
            sem(n) for n in "hy_in dft_in mod_in ln2_in mla_w_in fill_in rw_in tab_in ov_i".split())
        sin_in, mlp_ready = sem("sin_in"), sem("mlp_ready")
        filt_ready, sq_ready, fscale = sem("filt_ready"), sem("sq_ready"), sem("fscale")
        nss_ready, nrs_ready, hrow_ready = sem("nss_ready"), sem("nrs_ready"), sem("hrow_ready")
        conv_mid, y_ready = sem("conv_mid"), sem("y_ready")
        css_ready, crs_ready, cn_ready = sem("css_ready"), sem("crs_ready"), sem("cn_ready")
        kpe_ready, ktok_ready, qr_ready, ropeb_ready, ropec_ready, padded = (
            sem(n) for n in "kpe_ready ktok_ready qr_ready ropeb_ready ropec_ready padded".split())
        nm_ready, swa_s, prob_b, diff_ready, lam_pre, lam_exp = (
            sem(n) for n in "nm_ready swa_s prob_b diff_ready lam_pre lam_exp".split())
        dss_ready, drs_ready, mix_ready, x_ready = (sem(n) for n in "dss_ready drs_ready mix_ready x_ready".split())
        h2_stored = [sem("h2_stored0"), sem("h2_stored1")]
        e_in, e_out, m_ready, dest_ready, slots_ready, code_ready = (
            sem(n) for n in "e_in e_out m_ready dest_ready slots_ready code_ready".split())
        xt_done, xt_ready, gu_done, silu_ready, acth_ready, at_done, actT_ready, y_done, yg_lo, yg_hi = (
            sem(n) for n in "xt_done xt_ready gu_done silu_ready acth_ready at_done actT_ready y_done yg_lo yg_hi".split())
        ov_w, ov_i2, ov_x, ov_xt, ov_gu, ov_sil, ov_act, ov_at, ov_aT, ov_y, ov_ya, ov_yv, ov_t, ov_done = (
            sem("ov_" + n) for n in "w i2 x xt gu sil act at aT y ya yv t done".split())
        moe_done, pair_in, pair_used = sem("moe_done"), [sem("pair_in0"), sem("pair_in1")], sem("pair_used")
        gidx_ready, sidx_ready = sem("gidx_ready", False), sem("sidx_ready", False)
        waited = sem("waited")
        ones_set, ang_ready, rope_ready, tables_ready = (sem(n, False) for n in ("ones_set", "ang_ready", "rope_ready", "tables_ready"))
        c_ready, rep_ready, sines_ready, iota_ready, final_in = (
            sem(n, False) for n in "c_ready rep_ready sines_ready iota_ready final_in".split())

        class Steps:

            def __init__(self, eng, s):
                self.eng, self.s, self.n = eng, s, 0

            def __call__(self, ins):
                ins.then_inc(self.s, 1)
                self.n += 1
                self.eng.wait_ge(self.s, self.n)

        number = {}

        class Products:

            def __init__(self, pe, group, first, taken):
                self.pe, self.group, self.first, self.taken, self.n = pe, group, first, taken, 0

            def bank(self, name):
                if self.n >= 4:
                    self.pe.wait_ge(self.taken, self.n - 3)
                number[name] = (self.group, self.n)
                self.n += 1
                return bank[self.first + (self.n - 1) % 4]

        class Reader:
            def __init__(self, eng, first, ready):
                self.eng, self.first, self.ready, self.n = eng, first, ready, 0

            def take(self, name):
                assert number[name][1] == self.n, (name, number[name], self.n)
                self.n += 1
                self.eng.wait_ge(self.ready, self.n)
                return bank[self.first + (self.n - 1) % 4]

        def done(eng, name):
            g, n = number[name]
            eng.wait_ge(ready_v if g == "v" else ready_a, n + 1)

        def taken(eng, name):
            g, n = number[name]
            eng.wait_ge(taken_v if g == "v" else taken_a, n + 1)

        outs, maps = [], []
        for h in range(NH):
            for qt in range(NT):
                outs.append(("a", h, qt, [len(maps)]))
                maps.append(("a", h, qt, 0))
        for h in range(NH):
            for qt in range(NT):
                outs.append(("b", h, qt, [len(maps)]))
                maps.append(("b", h, qt, 0))
        for h in range(NH):
            for qt in range(NT):
                outs.append(("c", h, qt, [len(maps), len(maps) + 1]))
                maps += [("c", h, qt, 0), ("c", h, qt, 1)]
        out_of = {m: o for o, v in enumerate(outs) for m in v[3]}
        MOD_AFTER = {3: 3, 8: 4, 13: 5, 18: 6, 23: 7}
        steps, given = [], 0
        for o, v in enumerate(outs):
            while given < min(v[3][-1] + 3, len(maps)):
                steps.append(("S", given))
                given += 1
            steps.append(("T", o))
            if o:
                steps.append(("PV", o - 1))
            if o in MOD_AFTER:
                steps.append(("M", MOD_AFTER[o]))
        steps.append(("PV", len(outs) - 1))

        def band(n):
            return (P if n == 0 else 0), (2 * P if n == NT - 1 else 3 * P)

        def mod_parts(c):
            parts = []
            for half, (lo, n) in enumerate(((0, 512), (512, 256))):
                g0 = c * ADA + lo
                g = g0
                while g < g0 + n:
                    e = min(g0 + n, (g // D + 1) * D)
                    parts.append((half, g - g0, e - g0, g // D, g % D, g % D + e - g))
                    g = e
            return parts

        CHUNKS = [("ada", 0), ("ada", 1), ("ada", 2), ("in", "d"), ("in", "a"), ("in", "b"), ("in", "c"),
                  ("ada", 3), ("ada", 4), ("ada", 5), ("ada", 6), ("ada", 7), ("out", 0), ("out", 1)]
        chunk_at = {c: (n % 2, n // 2) for n, c in enumerate(CHUNKS)}
        col0 = {"a": (0, A_COLS), "b": (A_COLS, B_COLS), "c": (A_COLS + B_COLS, C_COLS),
                "d": (A_COLS + B_COLS + C_COLS, D_COLS)}
        USES = len(CHUNKS) // 2

        def chunk_slot(c):
            return chunk_at[c][0]

        def chunk_wait(eng, c):
            s, n = chunk_at[c]
            eng.wait_ge(slot_full[s], 16 * (n + 1))

        def chunk_used(eng, c):
            kind, which = c
            if kind == "ada":
                done(eng, f"m{which}1")
            elif kind == "out":
                done(eng, f"w{which}{NT - 1}")
            else:
                done(eng, {"d": "d5", "a": "a30", "b": "b30", "c": "c3512"}[which])

        def expert_full(s, i):
            return 16 * (USES if s < 2 else 0) + 48 + 48 * i

        def expert_slot(s):
            wg = slot(s, 3, KT, F)[:, 0]
            wu = slot(s, 3, KT, F)[:, 1]
            wd = at(big, s * SLOT + 4096, 2, D)
            return wg, wu, wd

        def row(ap2):
            return ap2.partition_broadcast(P) if len(ap2.shape) == 1 else ap2.broadcast_to([P, ap2.shape[1]])

        def of_layer(name, l):
            v = a[name]
            names = " ".join("bcde"[:len(v.shape) - 1])
            s = v[bass.ds(l, 1)]
            return s.rearrange(f"a {names} -> (a {names.split(' ')[0]}) {' '.join(names.split(' ')[1:])}".rstrip())

        def row_of(name, l):
            return a[name][bass.ds(l, 1)]

        ctx.enter_context(nc.allow_non_contiguous_dma(reason="vectors of a few KB with one element on a partition"))
        block = ctx.enter_context(nc.Block())

        @block.tensor
        def _(pe):
            pe.wait_ge(first_load, 16 * 8)
            pe.wait_ge(ones_set, 1)
            pe.wait_ge(rep_ready, 1)

            def mm(o, l, r, start=True, stop=True):
                return nc.tensor.matmul(o, l, r, start=start, stop=stop)

            def layer(l):
                V = Products(pe, "v", 0, taken_v)
                A = Products(pe, "a", 4, taken_a)

                def mod_sum(c):
                    chunk_wait(pe, ("ada", c))
                    w = at(big, chunk_slot(("ada", c)) * SLOT, KT, ADA)
                    for half, (lo, n) in enumerate(((0, 512), (512, 256))):
                        b = V.bank(f"m{c}{half}")
                        for k in range(KT):
                            last = mm(b[:, 0:n], c_rep[:, k, :], w[:, k, lo:lo + n], k == 0, k == KT - 1)
                        last.then_inc(ready_v, 1)

                pe.wait_ge(hy_in, 16 * 12)
                for j, (w, n) in enumerate(((hw1, 33), (hw2, 64), (hw3, 64))):
                    if j:
                        pe.wait_ge(mlp_ready, j)
                    b = V.bank(f"f{j}")
                    mm(b[0:64, :], w, zT if j == 0 else mlp_h).then_inc(ready_v, 1)
                pe.wait_ge(mlp_ready, 3)
                for t in range(NT):
                    for d in range(2):
                        b = V.bank(f"h{t}{d}")
                        mm(b[:, :], mlp_h[:, t * P:(t + 1) * P], w4[:, d * S:(d + 1) * S]).then_inc(ready_v, 1)
                pe.wait_ge(sq_ready, NT)
                b = V.bank("fn")
                for t in range(NT):
                    mm(b[:, :], ones[:, :], sq_sum[:, t], t == 0, False)
                    last = mm(b[:, :], ones[:, :], sq_dif[:, t], False, t == NT - 1)
                last.then_inc(ready_v, 1)
                pe.wait_ge(dft_in, 64)
                pe.wait_ge(filt_ready, NT)

                def dft(name, w, col, n, rhs):
                    b = V.bank(name)
                    for kt in range(NT):
                        last = mm(b[0:n, :], w[:, kt, col:col + n], rhs[:, kt, :], kt == 0, kt == NT - 1)
                    last.then_inc(ready_v, 1)

                for m in range(NT):
                    dft(f"fc{m}", cosm, m * P, P, fsum)
                dft("fcn", sin_f, 0, 1, fsum)
                for m in range(NT):
                    dft(f"fd{m}", sinm, m * P, P, fdif)
                for c in range(3):
                    mod_sum(c)

                def transpose_rows(first):
                    for t in range(NT):
                        pe.wait_ge(hrow_ready, first + t + 1)
                        for half in range(2):
                            b = A.bank(f"hT{first + t}{half}")
                            for j in range(4):
                                k = 4 * half + j
                                rows = h_tok[:, t % 2, :].rearrange("p (c k) -> p k c", k=KT)[:, k]
                                last = nc.tensor.transpose(b[:, j * P:(j + 1) * P], rows, ident[:, :])
                            last.then_inc(ready_a, 1)

                transpose_rows(0)
                taken(pe, "hT31")

                chunk_wait(pe, ("in", "d"))
                w = at(big, chunk_slot(("in", "d")) * SLOT, KT, D_COLS)
                for m in range(6):
                    b = V.bank(f"d{m}")
                    for k in range(KT):
                        last = mm(b[:, :], w[:, k, m * P:(m + 1) * P], hT[:, k, :], k == 0, k == KT - 1)
                    last.then_inc(ready_v, 1)

                def project(g, tiles=range(NT)):
                    c = ("in", g)
                    chunk_wait(pe, c)
                    n = col0[g][1]
                    w = at(big, chunk_slot(c) * SLOT, KT, n)
                    for t in tiles:
                        for lo in range(0, n, 512):
                            m = min(512, n - lo)
                            b = A.bank(f"{g}{t}{lo}")
                            for k in range(KT):
                                last = mm(b[:, 0:m], hT[:, k, t * P:(t + 1) * P], w[:, k, lo:lo + m], k == 0, k == KT - 1)
                            last.then_inc(ready_a, 1)

                project("a")
                taken(pe, "d3")
                for t in range(NT):
                    b = A.bank(f"vx{t}")
                    for c in range(4):
                        last = nc.tensor.transpose(b[:, c * P:(c + 1) * P], vxT[:, c, t * P:(t + 1) * P], ident[:, :])
                    last.then_inc(ready_a, 1)
                for o in range(2):
                    taken(pe, "vx3" if o == 0 else "y03")
                    for m in range(NT):
                        b = V.bank(f"u{o}{m}")
                        for part, w in enumerate((cosm, sin_f if m == 0 else sinm)):
                            col = 0 if part and m == 0 else m * P
                            for kt in range(NT):
                                last = mm(b[:, part * CH:(part + 1) * CH], w[:, kt, col:col + P], vx_tok[:, kt, 0:CH],
                                          kt == 0, kt == NT - 1)
                        last.then_inc(ready_v, 1)
                    if o == 0:
                        for t in range(NT):
                            b = V.bank(f"y{o}{t}")
                            for kt in range(NT):
                                if t == 0:
                                    pe.wait_ge(y_ready, kt + 1)
                                mm(b[:, 0:CH], cosm[:, kt, t * P:(t + 1) * P], yre[:, kt, :], kt == 0, False)
                                w = sin_i[:, t * P:(t + 1) * P] if kt == 0 else sinm[:, kt, t * P:(t + 1) * P]
                                last = mm(b[:, 0:CH], w, yim[:, kt, :], False, kt == NT - 1)
                            last.then_inc(ready_v, 1)
                    else:
                        for c in range(2):
                            b = V.bank(f"y{o}{c}")
                            for kt in range(NT):
                                if c == 0:
                                    pe.wait_ge(y_ready, NT + kt + 1)
                                mm(b[:, :], yre[:, kt, c * P:(c + 1) * P], cosm[:, kt, :], kt == 0, False)
                                w = sin_i if kt == 0 else sinm[:, kt, :]
                                last = mm(b[:, :], yim[:, kt, c * P:(c + 1) * P], w, False, kt == NT - 1)
                            last.then_inc(ready_v, 1)
                project("b")
                pe.wait_ge(cn_ready, 1)
                for j in range(3):
                    b = A.bank(f"ct{j}")
                    for t in range(NT):
                        last = nc.tensor.transpose(b[:, t * P:(t + 1) * P], cols_a[:, t, j * P:(j + 1) * P], ident[:, :])
                    last.then_inc(ready_a, 1)
                taken(pe, "ct2")
                pe.wait_ge(mla_w_in, 32)
                for t in range(NT):
                    b = A.bank(f"q{t}")
                    for j in range(2):
                        last = mm(b[:, 0:384], cT[:, j, t * P:(t + 1) * P], w_uq[:, j, :], j == 0, j == 1)
                    last.then_inc(ready_a, 1)
                    b = A.bank(f"kv{t}")
                    mm(b[:, :], cT[:, 2, t * P:(t + 1) * P], w_ukv).then_inc(ready_a, 1)
                project("c", range(2))
                pe.wait_ge(ktok_ready, 1)
                for h in range(NH):
                    b = A.bank(f"kTa{h}")
                    for t in range(NT):
                        last = nc.tensor.transpose(b[0:96, t * P:(t + 1) * P], k_tok[:, t, h, :], ident[:, :])
                    last.then_inc(ready_a, 1)
                project("c", range(2, NT))
                pe.wait_ge(qr_ready, NT)
                for h in range(NH):
                    b = A.bank(f"qTa{h}")
                    for t in range(NT):
                        last = nc.tensor.transpose(b[0:96, t * P:(t + 1) * P], q_tok[:, t, h * 96:(h + 1) * 96], ident[:, :])
                    last.then_inc(ready_a, 1)
                pe.wait_ge(ropeb_ready, NT)
                b = A.bank("kTb")
                for t in range(NT):
                    last = nc.tensor.transpose(b[:, t * P:(t + 1) * P], rope_b[:, t, 256:384], ident[:, :])
                last.then_inc(ready_a, 1)
                for h in range(NH):
                    b = A.bank(f"qTb{h}")
                    for t in range(NT):
                        last = nc.tensor.transpose(b[0:64, t * P:(t + 1) * P], rope_b[:, t, h * 64:(h + 1) * 64], ident[:, :])
                    last.then_inc(ready_a, 1)
                pe.wait_ge(ropec_ready, NT)
                for j in range(4):
                    b = A.bank(f"cT{j}")
                    for t in range(NT):
                        last = nc.tensor.transpose(b[:, t * P:(t + 1) * P], rope_c[:, t, j * P:(j + 1) * P], ident[:, :])
                    last.then_inc(ready_a, 1)

                taken(pe, "cT3")
                for what, n in steps:
                    if what == "S":
                        g, h, qt, m = maps[n]
                        q = slice(qt * P, (qt + 1) * P)
                        if g == "a":
                            mm(A.bank(f"S{n}")[:, :], qT_a[0:96, h, q], kT_a[0:96, h, :]).then_inc(ready_a, 1)
                        elif g == "c":
                            i = 2 * h + m
                            mm(A.bank(f"S{n}")[:, :], qT_c[:, i, q], kT_c[:, i // 4, :]).then_inc(ready_a, 1)
                        else:
                            lo, hi = band(qt)
                            keys = slice((qt - 1) * P + lo, (qt - 1) * P + hi)
                            mm(V.bank(f"S{n}")[:, lo:hi], qT_b[:, h, q], kT_b[:, keys]).then_inc(ready_v, 1)
                    elif what == "T":
                        g, h, qt, ms = outs[n]
                        if g == "a":
                            taken(pe, f"S{ms[0]}")
                        elif g == "b":
                            pe.wait_ge(prob_b, ms[0] - 15)
                        else:
                            pe.wait_ge(diff_ready, n - 2 * NH * NT + 1)
                        b = A.bank(f"T{n}")
                        nb = NT if g != "b" else (band(qt)[1] - band(qt)[0]) // P
                        for j in range(nb):
                            last = nc.tensor.transpose(b[:, j * P:(j + 1) * P], prob[:, ms[0] % 3, j * P:(j + 1) * P], ident[:, :])
                        last.then_inc(ready_a, 1)
                    elif what == "PV":
                        g, h, qt, ms = outs[n]
                        taken(pe, f"T{n}")
                        b = V.bank(f"O{n}")
                        if g == "b":
                            lo, hi = band(qt)
                            tiles = range((qt * P - P + lo) // P, (qt * P - P + hi) // P)
                        else:
                            tiles = range(NT)
                        for j, kt in enumerate(tiles):
                            v = {"a": kv_tok[:, kt, h * P:(h + 1) * P], "b": cols_b[:, kt, 384:512],
                                 "c": cols_c[:, kt, 512 + h // 2 * P:512 + (h // 2 + 1) * P]}[g]
                            last = mm(b[:, 0:P], probT[:, n % 2, j * P:(j + 1) * P], v, j == 0, j == len(tiles) - 1)
                        last.then_inc(ready_v, 1)
                    else:
                        mod_sum(n)
                pe.wait_ge(mix_ready, 1)
                for j in range(6):
                    b = A.bank(f"xT{j}")
                    for t in range(NT):
                        last = nc.tensor.transpose(b[:, t * P:(t + 1) * P], mix_tok[:, t, j * P:(j + 1) * P], ident[:, :])
                    last.then_inc(ready_a, 1)
                taken(pe, "xT5")
                for half in range(2):
                    c = ("out", half)
                    chunk_wait(pe, c)
                    w = at(big, chunk_slot(c) * SLOT, KT, 512)
                    for t in range(NT):
                        b = V.bank(f"w{half}{t}")
                        for k in range(KT):
                            src = mixT[:, k, t * P:(t + 1) * P] if k < 6 else ydT[:, k - 6, t * P:(t + 1) * P]
                            last = mm(b[:, :], src, w[:, k, :], k == 0, k == KT - 1)
                        last.then_inc(ready_v, 1)
                transpose_rows(NT)

                taken(pe, f"hT{2 * NT - 1}1")
                pe.wait_ge(rw_in, 16 * 4)
                b = A.bank("lgT")
                for k in range(KT):
                    last = mm(b[0:36, :], r_w[:, k, :], hT[:, k, :], k == 0, k == KT - 1)
                last.then_inc(ready_a, 1)
                taken(pe, "lgT")
                b = V.bank("lg")
                for t in range(NT):
                    last = nc.tensor.transpose(b[:, t * 36:(t + 1) * 36], lgT[:, t * P:(t + 1) * P], ident[0:36, 0:36])
                last.then_inc(ready_v, 1)
                pe.wait_ge(m_ready, 1)
                ms = msum.rearrange("p t e -> p (t e)")
                b = V.bank("before")
                mm(b[:, 0:P], tri[:, :], ms)
                mm(b[:, P:2 * P], ones[:, :], ms).then_inc(ready_v, 1)
                pe.wait_ge(code_ready, 1)
                b = V.bank("over")
                nc.tensor.transpose(b[0:1, 0:P], o_code[:, 0:1], ident[:, :]).then_inc(ready_v, 1)

                pe.wait_ge(taken_v, V.n)
                pe.wait_ge(taken_a, A.n)

                def x_transpose(b, count):
                    for k in range(KT):
                        rows = xg[0:CAP, b, :].rearrange("p (c k) -> p k c", k=KT)[:, k]
                        last = nc.tensor.transpose(bank[b][:, k * CAP:(k + 1) * CAP], rows, ident[0:CAP, 0:CAP])
                    return last

                def gate_up(b, s):
                    wg, wu, _ = expert_slot(s)
                    for k in range(KT):
                        xk = xT[:, b, k * CAP:(k + 1) * CAP]
                        mm(bank[2 + b][0:CAP, 0:F], xk, wg[:, k, :], k == 0, k == KT - 1)
                        last = mm(bank[2 + b][CAP:P, 0:F], xk, wu[:, k, :], k == 0, k == KT - 1)
                    return last

                def act_transpose(b):
                    for j in range(2):
                        rows = act_h[0:CAP, b, :].rearrange("p (f j) -> p j f", j=2)[:, j]
                        last = nc.tensor.transpose(bank[4 + b][:, j * CAP:(j + 1) * CAP], rows, ident[0:CAP, 0:CAP])
                    return last

                def down(b, s):
                    _, _, wd = expert_slot(s)
                    for j in range(2):
                        hk = act_T[:, b, j * CAP:(j + 1) * CAP]
                        mm(bank[6 + b][0:CAP, :], hk, wd[:, j, 0:512], j == 0, j == 1)
                        last = mm(bank[6 + b][CAP:P, :], hk, wd[:, j, 512:1024], j == 0, j == 1)
                    return last

                gathers = [NE // 2 * 16 * l, NE // 2 * 16 * l]

                def expert(i, s, more):
                    b = s % 2
                    pe.wait_ge(xt_ready, 4 * i + s + 1)
                    pe.wait_ge(slot_full[s], expert_full(s, i))
                    if not (isinstance(i, int) and i == 0 and s < 2):
                        pe.wait_ge(acth_ready, 4 * i + s - 1)
                    gate_up(b, s).then_inc(gu_done, 1)
                    if more:
                        nb = (s + 1) % 2
                        k = 2 * i + (s + 1) // 2
                        pe.wait_ge(gathered[nb], gathers[nb] + 16 * (k + 1))
                        if not (isinstance(i, int) and i == 0 and s < 1):
                            pe.wait_ge(xt_ready, 4 * i + s)
                        pe.sem_inc(waited, 1)
                        x_transpose(nb, k).then_inc(xt_done, 1)
                    pe.wait_ge(acth_ready, 4 * i + s + 1)
                    if not (isinstance(i, int) and i == 0 and s < 2):
                        pe.wait_ge(actT_ready, 4 * i + s - 1)
                    pe.sem_inc(waited, 1)
                    act_transpose(b).then_inc(at_done, 1)
                    pe.wait_ge(actT_ready, 4 * i + s + 1)
                    if not (isinstance(i, int) and i == 0 and s < 2):
                        pe.wait_ge(yg_lo, 4 * i + s - 1)
                        pe.wait_ge(yg_hi, 4 * i + s - 1)
                    down(b, s).then_inc(y_done, 1)

                pe.wait_ge(gathered[0], gathers[0] + 16)
                pe.sem_inc(waited, 1)
                x_transpose(0, 0).then_inc(xt_done, 1)
                for s in range(4):
                    expert(0, s, True)
                with pe.Fori(1, NE // 4 - 1) as i:
                    for s in range(4):
                        expert(i, s, True)
                for s in range(4):
                    expert(NE // 4 - 1, s, s < 3)

                pe.wait_ge(yg_lo, NE)
                pe.wait_ge(yg_hi, NE)
                n_over = pe.value_load(tot_i[0:1, 0:1], min_val=0, max_val=EXTRA)
                n_before = pe.value_load(tot_i[0:1, 1:2], min_val=0, max_val=EXTRA * DEPTH)
                with pe.Fori(0, EXTRA) as r:
                    with pe.If(r < n_over):
                        pe.wait_ge(over_gathered, (n_before + r + 1) * 16)
                        pe.sem_inc(waited, 1)
                        x_transpose(0, 0).then_inc(ov_xt, 1)
                        pe.wait_ge(ov_x, r + 1)
                        pe.wait_ge(ov_w, 48 * r + 48)
                        gate_up(0, 0).then_inc(ov_gu, 1)
                        pe.wait_ge(ov_act, r + 1)
                        pe.sem_inc(waited, 1)
                        act_transpose(0).then_inc(ov_at, 1)
                        pe.wait_ge(ov_aT, r + 1)
                        down(0, 0).then_inc(ov_y, 1)
                    with pe.Else():
                        pe.nop()
                pe.drain().then_inc(layer_done, 1)

            with pe.Fori(0, DEPTH) as l:
                layer(l)
                pe.wait_ge(layer_go, l + 1)

        @block.sync
        def _(sp):
            sp.dma_start(x_tok[:, :, :], a["x"].rearrange("b (t p) d -> p (b t) d", p=P)).then_inc(first_load, 16)
            sp.dma_start(c_sb, a["c"].rearrange("b (p k) -> p (b k)", k=KT)).then_inc(first_load, 16)
            sp.dma_start(pos_i[:, :], a["positions"].rearrange("b (t p) -> p (b t)", p=P)).then_inc(first_load, 16)
            sp.dma_start(ident[:, :], a["k_ident"]).then_inc(first_load, 16)
            sp.dma_start(tri[:, :], a["k_tri"]).then_inc(first_load, 16)
            sp.dma_start(mask[:, :], a["k_mask"]).then_inc(first_load, 16)
            sp.dma_start(invf, row(a["k_inv"])).then_inc(first_load, 16)
            sp.dma_start(misc[:, :], row(a["k_misc"])).then_inc(first_load, 16)

            with sp.Fori(0, DEPTH) as l:
                for n, (kind, which) in enumerate(CHUNKS):
                    s = n % 2
                    if n >= 2:
                        chunk_used(sp, CHUNKS[n - 2])
                    if kind == "ada":
                        src = of_layer("ada_w", l)[:, which * ADA:(which + 1) * ADA]
                    elif kind == "in":
                        lo, m = col0[which]
                        src = of_layer("w_in", l)[:, lo:lo + m]
                    if kind == "out":
                        src = of_layer("w_out", l)[:, which * 512:(which + 1) * 512]
                        sp.dma_start(slot(s, 12, 512)[:, 0:KT], src.rearrange("(k p) n -> p k n", p=P)).then_inc(slot_full[s], 16)
                    else:
                        m = src.shape[1]
                        sp.dma_start(at(big, s * SLOT, KT, m), src.rearrange("(p k) n -> p k n", k=KT)).then_inc(slot_full[s], 16)

                def load_expert(i, s):
                    wg, wu, wd = expert_slot(s)
                    e = l * NE + 4 * i + s
                    sp.dma_start(wg, a["moe_w_gate"].rearrange("l e d f -> (l e) d f")[bass.ds(e, 1)].rearrange(
                        "a (p k) f -> (a p) k f", k=KT)).then_inc(slot_full[s], 16)
                    sp.dma_start(wu, a["moe_w_up"].rearrange("l e d f -> (l e) d f")[bass.ds(e, 1)].rearrange(
                        "a (p k) f -> (a p) k f", k=KT)).then_inc(slot_full[s], 16)
                    sp.dma_start(wd, a["moe_w_down"].rearrange("l e f d -> (l e) f d")[bass.ds(e, 1)].rearrange(
                        "a (p j) d -> (a p) j d", j=2)).then_inc(slot_full[s], 16)

                for s in range(4):
                    if s < 2:
                        chunk_used(sp, CHUNKS[-2 + s])
                    else:
                        done(sp, f"O{len(outs) - 1}")
                    load_expert(0, s)
                with sp.Fori(1, NE // 4) as i:
                    for s in range(4):
                        sp.wait_ge(y_done, 4 * i + s - 3)
                        load_expert(i, s)

                taken(sp, "over")
                n_over = sp.value_load(tot_i[0:1, 0:1], min_val=0, max_val=EXTRA)
                n_before = sp.value_load(tot_i[0:1, 1:2], min_val=0, max_val=EXTRA * DEPTH)
                table = slots_of.rearrange("(r e) o -> r (e o)", e=NE)
                with sp.Fori(0, EXTRA) as r:
                    with sp.If(r < n_over):
                        code = sp.value_load(over_i[0:1, bass.ds(r, 1)], min_val=1, max_val=8 * NE - 1)
                        e = sp.snap(code // 8, min_val=0, max_val=NE - 1)
                        j = sp.snap(code % 8, min_val=0, max_val=7)
                        ee = sp.snap(l * NE + e, min_val=0, max_val=DEPTH * NE - 1)
                        wg, wu, wd = expert_slot(0)
                        sp.wait_ge(ov_yv, r + 1)
                        sp.dma_start(wg, a["moe_w_gate"].rearrange("l e d f -> (l e) d f")[bass.ds(ee, 1)].rearrange(
                            "a (p k) f -> (a p) k f", k=KT)).then_inc(ov_w, 16)
                        sp.dma_start(wu, a["moe_w_up"].rearrange("l e d f -> (l e) d f")[bass.ds(ee, 1)].rearrange(
                            "a (p k) f -> (a p) k f", k=KT)).then_inc(ov_w, 16)
                        sp.dma_start(wd, a["moe_w_down"].rearrange("l e f d -> (l e) f d")[bass.ds(ee, 1)].rearrange(
                            "a (p j) d -> (a p) j d", j=2)).then_inc(ov_w, 16)
                        sp.dma_start(o_idx[0:CAP, 0:1], table[bass.ds(j * CAP, CAP), bass.ds(e, 1)]).then_inc(ov_i, 16)
                    with sp.Else():
                        sp.nop()

                sp.wait_ge(moe_done, 1)
                for t in range(NT):
                    if t >= 2:
                        sp.wait_ge(pair_used, t - 1)
                    sp.dma_start(pair[:, t % 2], pair_rows.rearrange("(k t p) d -> t p k d", t=NT, p=P)[t]).then_inc(pair_in[t % 2], 16)

                sp.wait_ge(layer_done, 4 * l + 4)
                sp.sem_inc(waited, 1)
                for s in layer_sems:
                    sp.sem_clear(s)
                sp.sem_inc(layer_go, 1)

            for t in range(NT):
                sp.wait_ge(fin_row, t + 1)
                sp.dma_start(out[0, t * P:(t + 1) * P, :], h_tok[:, t % 2, :]).then_inc(out_row[t % 2], 16)
            for i in range(2):
                sp.wait_ge(out_row[i], 16 * NT // 2)

        @block.scalar
        def _(act):
            A_ = nc.scalar.activation
            act.wait_ge(first_load, 16 * 8)
            A_(c_act, c_sb, ACT.Silu).then_inc(c_ready, 1)
            act.wait_ge(ang_ready, 1)
            ang = at(mix_r, 0, NT, 48)
            half = at(mix_r, 192, NT, 48)
            A_(at(mix_r, 384, NT, 48), ang, ACT.Sin)
            A_(half, ang, ACT.Sin, scale=0.5).then_inc(sines_ready, 1)
            act.wait_ge(c_ready, 1)
            act.wait_ge(tables_ready, 1)

            def layer(l):
                step = Steps(act, a_step)
                R = Reader(act, 4, ready_a)
                d = act.dma_start
                for j, (w, name) in enumerate(((hw1, "hy_w1"), (hw2, "hy_w2"), (hw3, "hy_w3"))):
                    d(w, of_layer(name, l)).then_inc(hy_in, 16)
                for j, name in enumerate(("hy_b1", "hy_b2", "hy_b3")):
                    d(hb[:, j:j + 1], row_of(name, l).rearrange("a n -> n a")).then_inc(hy_in, 16)
                d(hf, of_layer("hy_sin_freq", l).rearrange("j n -> n j")).then_inc(hy_in, 16)
                d(zT, a["k_z"]).then_inc(hy_in, 16)
                d(w4, of_layer("hy_w4", l)).then_inc(hy_in, 16)
                d(window, a["k_window"].rearrange("(t p) c -> p t c", p=P)).then_inc(hy_in, 16)
                d(bias_b, a["hy_bias"].rearrange("l o c -> l (o c)")[bass.ds(l, 1)].broadcast_to([P, S])).then_inc(hy_in, 16)
                d(lv, a["diff_lambda"].rearrange("l j n -> l (j n)")[bass.ds(l, 1)].broadcast_to([P, P])).then_inc(hy_in, 16)
                d(cosm, a["k_cos"].rearrange("(t p) k -> p t k", p=P)).then_inc(dft_in, 16)
                d(sinm, a["k_sin"].rearrange("(t p) k -> p t k", p=P)).then_inc(dft_in, 16)
                d(sin_f, a["k_sin_f"].rearrange("(t p) k -> p t k", p=P)).then_inc(dft_in, 16)
                d(sin_i, a["k_sin_i"]).then_inc(dft_in, 16)
                bias = row_of("ada_b", l)
                for j, dst in enumerate((sh1, gsc1, mod[:, 0, :], mod[:, 1, :], mod[:, 2, :], mod[:, 3, :])):
                    d(dst, bias[:, j * D:(j + 1) * D].broadcast_to([P, D])).then_inc(mod_in, 16)
                d(ln1, row_of("ln1_g", l).broadcast_to([P, D])).then_inc(mod_in, 16)
                for j in range(3):
                    d(conv_w[:, 6 * j:6 * j + 6], of_layer("hy_conv_w", l)[j:j + 1].rearrange("a (c p) -> p (a c)", p=P)).then_inc(mod_in, 16)
                d(conv_b, row_of("hy_conv_b", l).rearrange("a (c p) -> p (a c)", p=P)).then_inc(mod_in, 16)
                d(gd, row_of("diff_norm_g", l).broadcast_to([P, 64])).then_inc(mod_in, 16)
                d(gn[:, 0:2], row_of("mla_q_norm", l).rearrange("a (j p) -> p (a j)", p=P)).then_inc(mod_in, 16)
                d(gn[:, 2:3], row_of("mla_kv_norm", l).rearrange("a (j p) -> p (a j)", p=P)).then_inc(mod_in, 16)
                d(sink, row_of("swa_sink", l).broadcast_to([P, NH])).then_inc(mod_in, 16)
                d(lam_b, a["k_lam"][bass.ds(l, 1)].broadcast_to([P, 2])).then_inc(mod_in, 16)

                d(r_b[0:NG, :], row_of("router_g_b", l).rearrange("a n -> n a")).then_inc(mod_in, 16)
                d(r_b[NG:36, :], row_of("router_e_b", l).rearrange("a n -> n a")).then_inc(mod_in, 16)
                d(slots_of.rearrange("(p n) o -> p (n o)", p=P), a["k_empty"]).then_inc(fill_in, 16)

                for j in range(3):
                    act.wait_ge(sin_in, j + 1)
                    A_(mlp_h, mlp_y, ACT.Sin).then_inc(mlp_ready, 1)
                for t in range(NT):
                    act.wait_ge(filt_ready, t + 1)
                    A_(sq_sum[:, t], fsum[:, t], ACT.Square)
                    last = A_(sq_dif[:, t], fdif[:, t], ACT.Square)
                    if t == 0:
                        step(last)
                        last = A_(sq_dif[0:1, 0], sq_sum[0:1, 0], ACT.Copy)
                    last.then_inc(sq_ready, 1)
                act.wait_ge(lam_pre, 1)
                A_(lexp, lred, ACT.Exp).then_inc(lam_exp, 1)

                def norm(first):
                    for t in range(NT):
                        if first:
                            act.wait_ge(x_ready, t + 1)
                        if t >= 2:
                            done(act, f"hT{first + t - 2}1")
                            if first:
                                act.wait_ge(h2_stored[t % 2], 16)
                        A_(h_tok[:, t % 2, :], x_tok[:, t, :], ACT.Square, accum_out=nss[:, t:t + 1]).then_inc(nss_ready, 1)
                        if t >= 1:
                            evac(first + t - 1)
                    evac(first + NT - 1)

                def evac(n):
                    t = n % NT
                    for half in range(2):
                        b = R.take(f"hT{n}{half}")
                        A_(hT[:, 4 * half:4 * half + 4, t * P:(t + 1) * P], b[:, :].rearrange("p (k c) -> p k c", k=4),
                           ACT.Copy).then_inc(taken_a, 1)
                    if n >= NT:
                        act.dma_start(h2_rows[t * P:(t + 1) * P, :], h_tok[:, t % 2, :]).then_inc(h2_stored[t % 2], 16)

                taken(act, "fd3")
                norm(0)

                act.wait_ge(mod_in, 16 * 18)
                for m in range(6):
                    done(act, f"d{m}")
                    dst = vxT[:, m, :] if m < 4 else ydT[:, m - 4, :]
                    A_(dst, bank[number[f"d{m}"][1] % 4][:, :], ACT.Identity, bias=conv_b[:, m:m + 1],
                       scale=conv_w[:, 6 + m:7 + m]).then_inc(conv_mid, 1)
                for t in range(NT):
                    b = R.take(f"a{t}0")
                    A_(cols_a[:, t, :], b[:, 0:A_COLS], ACT.Copy).then_inc(taken_a, 1)
                    taken(act, f"a{t}0")
                    A_(rp_sq[:, 0:256], cols_a[:, t, 0:256], ACT.Square, accum_out=css[:, 2 * t:2 * t + 1])
                    A_(rp_sq[:, 256:384], cols_a[:, t, 256:384], ACT.Square, accum_out=css[:, 2 * t + 1:2 * t + 2]).then_inc(css_ready, 1)
                for t in range(NT):
                    b = R.take(f"vx{t}")
                    A_(vx_tok[:, t, :], b[:, :], ACT.Copy).then_inc(taken_a, 1)
                done(act, "y11")
                d(w_uq, of_layer("mla_w_uq", l).rearrange("(j p) n -> p j n", p=P)).then_inc(mla_w_in, 16)
                d(w_ukv, of_layer("mla_w_ukv", l)).then_inc(mla_w_in, 16)
                for t in range(NT):
                    b = R.take(f"b{t}0")
                    A_(cols_b[:, t, :], b[:, :], ACT.Copy).then_inc(taken_a, 1)
                for j in range(3):
                    b = R.take(f"ct{j}")
                    A_(cT[:, j, :], b[:, :], ACT.Copy, scale=gn[:, j:j + 1]).then_inc(taken_a, 1)
                for t in range(NT):
                    b = R.take(f"q{t}")
                    A_(q_tok[:, t, :], b[:, 0:384], ACT.Copy).then_inc(taken_a, 1)
                    b = R.take(f"kv{t}")
                    A_(kv_tok[:, t, :], b[:, :], ACT.Copy).then_inc(taken_a, 1)

                def cols_c_copy(t):
                    b = R.take(f"c{t}0")
                    A_(cols_c[:, t, 0:512], b[:, :], ACT.Copy).then_inc(taken_a, 1)
                    b = R.take(f"c{t}512")
                    A_(cols_c[:, t, 512:768], b[:, 0:256], ACT.Copy).then_inc(taken_a, 1)

                cols_c_copy(0)
                cols_c_copy(1)
                for h in range(NH):
                    b = R.take(f"kTa{h}")
                    A_(kT_a[0:96, h, :], b[0:96, :], ACT.Copy).then_inc(taken_a, 1)
                cols_c_copy(2)
                cols_c_copy(3)
                for h in range(NH):
                    b = R.take(f"qTa{h}")
                    A_(qT_a[0:96, h, :], b[0:96, :], ACT.Copy).then_inc(taken_a, 1)
                act.wait_ge(padded, 2)
                b = R.take("kTb")
                A_(kT_b, b[:, :], ACT.Copy).then_inc(taken_a, 1)
                for h in range(NH):
                    b = R.take(f"qTb{h}")
                    g = h // 2
                    A_(qT_b[64 * g:64 * g + 64, h, :], b[0:64, :], ACT.Copy).then_inc(taken_a, 1)
                for j in range(2):
                    b = R.take(f"cT{j}")
                    for i in range(4):
                        last = A_(qT_c[32 * i:32 * i + 32, 4 * j + i, :], b[32 * i:32 * i + 32, :], ACT.Copy)
                    last.then_inc(taken_a, 1)
                for j in range(2):
                    b = R.take(f"cT{2 + j}")
                    A_(kT_c[:, j, :], b[:, :], ACT.Copy).then_inc(taken_a, 1)

                for what, n in steps:
                    if what == "S":
                        g, h, qt, m = maps[n]
                        if n >= 3:
                            done(act, f"T{out_of[n - 3]}")
                        if g == "b":
                            w = band(qt)[1] - band(qt)[0]
                            act.wait_ge(swa_s, n - 16 + 1)
                            pr = prob[:, n % 3, 0:w]
                            A_(pr, pr, ACT.Exp, bias=nm[:, n:n + 1], accum_out=rs[:, n:n + 1])
                            A_(esink[:, n - 16:n - 15], sink[:, h:h + 1], ACT.Exp, bias=nm[:, n:n + 1]).then_inc(prob_b, 1)
                        else:
                            b = R.take(f"S{n}")
                            act.wait_ge(nm_ready, n + 1 if g == "a" else n - 16 + 1)
                            A_(prob[:, n % 3, :], b[:, :], ACT.Exp, bias=nm[:, n:n + 1],
                               scale=MLA_SCALE if g == "a" else DIFF_SCALE, accum_out=rs[:, n:n + 1]).then_inc(taken_a, 1)
                    elif what == "T":
                        g, h, qt, ms = outs[n]
                        w = S if g != "b" else band(qt)[1] - band(qt)[0]
                        b = R.take(f"T{n}")
                        if n >= 2:
                            done(act, f"O{n - 2}")
                        A_(probT[:, n % 2, 0:w], b[:, 0:w], ACT.Copy).then_inc(taken_a, 1)
                for j in range(6):
                    b = R.take(f"xT{j}")
                    A_(mixT[:, j, :], b[:, :], ACT.Copy).then_inc(taken_a, 1)
                done(act, f"O{len(outs) - 1}")
                d(ln2, row_of("ln2_g", l).broadcast_to([P, D])).then_inc(ln2_in, 16)
                d(r_w[:, :, 0:NG], of_layer("router_g_w", l).rearrange("(p k) g -> p k g", k=KT)).then_inc(rw_in, 16)
                d(r_w[:, :, NG:36], of_layer("router_e_w", l).rearrange("(p k) g -> p k g", k=KT)).then_inc(rw_in, 16)
                d(block_id, a["k_blocks"][0:1, :].broadcast_to([P, NE * 7])).then_inc(rw_in, 16)
                d(block_at, a["k_blocks"][1:2, :].broadcast_to([P, NE * 7])).then_inc(rw_in, 16)
                norm(NT)
                b = R.take("lgT")
                A_(lgT, b[0:36, :], ACT.Identity, bias=r_b).then_inc(taken_a, 1)
                act.wait_ge(e_in, 1)
                A_(rd, rd, ACT.Exp).then_inc(e_out, 1)
                act.wait_ge(e_in, 2)
                A_(vd, vd, ACT.Exp).then_inc(e_out, 1)
                act.wait_ge(table_dma, 128 * l + 128)
                table = slots_of.rearrange("(r e) o -> r (e o)", e=NE)
                d(slot_f[0:CAP, :], table[0:CAP, :]).then_inc(tab_in, 16)

                def x_evac(b):
                    return A_(xT[:, b, :], bank[b][:, :], ACT.Copy)

                def y_evac(b):
                    return A_(yg[0:CAP, b, 0:512], bank[6 + b][0:CAP, :], ACT.Copy)

                def expert(i, s, more):
                    b = s % 2
                    pre = isinstance(i, int) and i == 0 and s < 2
                    act.wait_ge(gu_done, 4 * i + s + 1)
                    if not pre:
                        act.wait_ge(acth_ready, 4 * i + s - 1)
                    A_(sil[0:CAP, b, :], bank[2 + b][0:CAP, 0:F], ACT.Silu).then_inc(silu_ready, 1)
                    if more:
                        act.wait_ge(xt_done, 4 * i + s + 2)
                        x_evac((s + 1) % 2).then_inc(xt_ready, 1)
                    act.wait_ge(y_done, 4 * i + s + 1)
                    if not pre:
                        act.wait_ge(scattered[b], NE // 2 * 16 * l + 16 * (2 * i + s // 2))
                    y_evac(b).then_inc(yg_lo, 1)

                act.wait_ge(xt_done, 1)
                x_evac(0).then_inc(xt_ready, 1)
                for s in range(4):
                    expert(0, s, True)
                with act.Fori(1, NE // 4 - 1) as i:
                    for s in range(4):
                        expert(i, s, True)
                for s in range(4):
                    expert(NE // 4 - 1, s, s < 3)

                n_over = act.value_load(tot_i[0:1, 0:1], min_val=0, max_val=EXTRA)
                with act.Fori(0, EXTRA) as r:
                    with act.If(r < n_over):
                        act.wait_ge(ov_xt, r + 1)
                        x_evac(0).then_inc(ov_x, 1)
                        act.wait_ge(ov_gu, r + 1)
                        A_(sil[0:CAP, 0, :], bank[2][0:CAP, 0:F], ACT.Silu).then_inc(ov_sil, 1)
                        act.wait_ge(ov_y, r + 1)
                        y_evac(0).then_inc(ov_ya, 1)
                    with act.Else():
                        act.nop()
                act.drain().then_inc(layer_done, 1)

            rp_sq = at(pr_r, 1536, 384)
            with act.Fori(0, DEPTH) as l:
                layer(l)
                act.wait_ge(layer_go, l + 1)
            act.dma_start(gsc1, a["final_g"].rearrange("(a d) -> a d", a=1).broadcast_to([P, D])).then_inc(final_in, 16)
            for t in range(NT):
                if t >= 2:
                    act.wait_ge(out_row[t % 2], 16 * (t // 2))
                A_(h_tok[:, t % 2, :], x_tok[:, t, :], ACT.Square, accum_out=nss[:, t:t + 1]).then_inc(fin_sq, 1)

        @block.gpsimd
        def _(g):
            g.iota(tok_id, [[P, 2 * NT]], base=0, channel_multiplier=1, allow_small_or_imprecise_dtypes=True)
            g.iota(part_id, [[0, 1]], base=1, channel_multiplier=1, allow_small_or_imprecise_dtypes=True)
            g.memset(neghalf, -0.5)
            g.memset(over_tot, 0.0).then_inc(iota_ready, 1)
            g.wait_ge(iota_ready, 1)
            g.wait_ge(c_ready, 1)
            g.tensor_copy(c_rep[:, :, :], c_act.unsqueeze(2).to_broadcast([P, KT, P])).then_inc(rep_ready, 1)

            def layer(l):
                step = Steps(g, g_step)

                def rstd(dst, src, inv_n, mul=1.0):
                    step(g.tensor_scalar(dst, src, inv_n, EPS, ALU.mult, ALU.add))
                    last = g.tensor_tensor(dst, dst, neghalf.to_broadcast(dst.shape), ALU.pow)
                    if mul != 1.0:
                        step(last)
                        last = g.tensor_scalar(dst, dst, mul, None, ALU.mult)
                    return last

                taken(g, "fn")
                rstd(s_b, s_b, 0.5, 2.0 / (2 * S)).then_inc(fscale, 1)
                for t in range(NT):
                    g.wait_ge(nss_ready, t + 1)
                    rstd(nrs[:, t:t + 1], nss[:, t:t + 1], 1.0 / D).then_inc(nrs_ready, 1)
                for o in range(2):
                    for m in range(NT):
                        n = o * NT + m
                        taken(g, f"u{o}{m}")
                        g.tensor_tensor(yre[:, m, :], cm[:, m % 2, 0, 0:CH], cm[:, m % 2, 1, CH:S], ALU.subtract)
                        g.tensor_tensor(yim[:, m, :], cm[:, m % 2, 1, 0:CH], cm[:, m % 2, 0, CH:S], ALU.add).then_inc(y_ready, 1)
                    if o == 0:
                        g.wait_ge(css_ready, NT)
                        step(g.tensor_scalar(crs.rearrange("p (t j) -> p j t", j=2)[:, 0], css.rearrange("p (t j) -> p j t", j=2)[:, 0],
                                             1.0 / 256, EPS, ALU.mult, ALU.add))
                        step(g.tensor_scalar(crs.rearrange("p (t j) -> p j t", j=2)[:, 1], css.rearrange("p (t j) -> p j t", j=2)[:, 1],
                                             1.0 / 128, EPS, ALU.mult, ALU.add))
                        g.tensor_tensor(crs, crs, neghalf.to_broadcast(crs.shape), ALU.pow).then_inc(crs_ready, 1)
                done(g, "y11")
                g.memset(qT_b, 0.0).then_inc(padded, 1)

                taken(g, "kv3")
                g.wait_ge(kpe_ready, NT)
                for t in range(NT):
                    g.tensor_copy(k_tok[:, t, :, 0:64], kv_tok[:, t, :].rearrange("p (h c) -> p h c", h=NH)[:, :, 0:64])
                    last = g.tensor_copy(k_tok[:, t, :, 64:96], cols_a[:, t, 384:416].unsqueeze(1).to_broadcast([P, NH, 32]))
                last.then_inc(ktok_ready, 1)
                done(g, "c3512")
                g.memset(qT_c, 0.0).then_inc(padded, 1)
                g.wait_ge(dss_ready, 1)
                rstd(drs, dss, 1.0 / 64).then_inc(drs_ready, 1)
                for t in range(NT):
                    g.wait_ge(nss_ready, NT + t + 1)
                    rstd(nrs[:, t:t + 1], nss[:, t:t + 1], 1.0 / D).then_inc(nrs_ready, 1)

                g.wait_ge(dest_ready, 1)
                g.wait_ge(fill_in, 16)
                for k in range(2):
                    for t in range(NT):
                        n = k * NT + t
                        g.indirect_dma_start(out=slots_of, out_offset=bass.IndirectOffsetOnAxis(ap=dest_i[:, k, t:t + 1], axis=0),
                                             in_=tok_id[:, n:n + 1], in_offset=None, bounds_check=S * NE - 1,
                                             oob_is_err=False).then_inc(table_dma, 16)
                g.wait_ge(table_dma, 16 * 8 * l + 16 * 8)
                g.wait_ge(slots_ready, 1)
                g.wait_ge(h2_stored[0], 32)
                g.wait_ge(h2_stored[1], 32)

                def gather(i, s):
                    b = s % 2
                    e = 4 * i + s
                    if not (isinstance(i, int) and i == 0 and s < 2):
                        g.wait_ge(xt_done, e - 1)
                    g.sem_inc(waited, 1)
                    g.tensor_copy(gather_i[0:CAP, b:b + 1], gslot_i[0:CAP, bass.ds(e, 1)]).then_inc(gidx_ready, 1)
                    g.wait_ge(gidx_ready, NE * l + e + 1)
                    g.sem_inc(waited, 1)
                    g.indirect_dma_start(out=xg[0:CAP, b, :], out_offset=None, in_=h2_rows,
                                         in_offset=bass.IndirectOffsetOnAxis(ap=gather_i[0:CAP, b:b + 1], axis=0),
                                         bounds_check=S - 1, oob_is_err=False).then_inc(gathered[b], 16)

                def scatter(i, s):
                    b = s % 2
                    e = 4 * i + s
                    if not (isinstance(i, int) and i == 0 and s < 2):
                        g.wait_ge(scattered[b], NE // 2 * 16 * l + 16 * (2 * i + s // 2))
                    g.sem_inc(waited, 1)
                    g.tensor_copy(scatter_i[0:CAP, b:b + 1], slot_i[0:CAP, bass.ds(e, 1)]).then_inc(sidx_ready, 1)
                    g.wait_ge(sidx_ready, NE * l + e + 1)
                    g.wait_ge(yg_lo, e + 1)
                    g.wait_ge(yg_hi, e + 1)
                    g.sem_inc(waited, 1)
                    g.indirect_dma_start(out=pair_rows, out_offset=bass.IndirectOffsetOnAxis(ap=scatter_i[0:CAP, b:b + 1], axis=0),
                                         in_=yg[0:CAP, b, :], in_offset=None, bounds_check=2 * S - 1,
                                         oob_is_err=False).then_inc(scattered[b], 16)

                gather(0, 0)
                gather(0, 1)

                def expert(i, s, more):
                    if more:
                        gather(i + (s + 2) // 4, (s + 2) % 4)
                    scatter(i, s)

                for s in range(4):
                    expert(0, s, True)
                with g.Fori(1, NE // 4 - 1) as i:
                    for s in range(4):
                        expert(i, s, True)
                for s in range(4):
                    expert(NE // 4 - 1, s, s < 2)
                for b in range(2):
                    g.wait_ge(scattered[b], NE // 2 * 16 * l + NE // 2 * 16)
                g.sem_inc(waited, 1)

                n_over = g.value_load(tot_i[0:1, 0:1], min_val=0, max_val=EXTRA)
                n_before = g.value_load(tot_i[0:1, 1:2], min_val=0, max_val=EXTRA * DEPTH)
                g.drain().then_inc(ov_done, 1)
                with g.Fori(0, EXTRA) as r:
                    with g.If(r < n_over):
                        g.wait_ge(ov_i2, r + 1)
                        g.sem_inc(waited, 1)
                        g.indirect_dma_start(out=xg[0:CAP, 0, :], out_offset=None, in_=h2_rows,
                                             in_offset=bass.IndirectOffsetOnAxis(ap=gather_i[0:CAP, 0:1], axis=0),
                                             bounds_check=S - 1, oob_is_err=False).then_inc(over_gathered, 16)
                        g.wait_ge(ov_ya, r + 1)
                        g.wait_ge(ov_yv, r + 2)
                        g.sem_inc(waited, 1)
                        g.indirect_dma_start(out=pair_rows, out_offset=bass.IndirectOffsetOnAxis(ap=scatter_i[0:CAP, 0:1], axis=0),
                                             in_=yg[0:CAP, 0, :], in_offset=None, bounds_check=2 * S - 1,
                                             oob_is_err=False).then_inc(over_scattered, 16)
                        g.wait_ge(over_scattered, (n_before + r + 1) * 16)
                        g.sem_inc(waited, 1)
                        g.drain().then_inc(ov_done, 1)
                    with g.Else():
                        g.nop()
                g.drain().then_inc(moe_done, 1)
                g.drain().then_inc(layer_done, 1)

            with g.Fori(0, DEPTH) as l:
                layer(l)
                g.wait_ge(layer_go, l + 1)
            for t in range(NT):
                g.wait_ge(fin_sq, t + 1)
                g.tensor_scalar(nrs[:, t:t + 1], nss[:, t:t + 1], 1.0 / D, EPS, ALU.mult, ALU.add).then_inc(fin_mid, 1)
                g.wait_ge(fin_mid, t + 1)
                g.tensor_tensor(nrs[:, t:t + 1], nrs[:, t:t + 1], neghalf, ALU.pow).then_inc(fin_rs, 1)

        @block.vector
        def _(v):
            TS, TT, STT = nc.vector.tensor_scalar, nc.vector.tensor_tensor, nc.vector.scalar_tensor_tensor
            INV2PI = 1.0 / (2 * math.pi)
            C1 = 6.28125
            C2 = float(np.float32(round((2 * math.pi - C1) * 2 ** 21)) / 2 ** 21)
            C3 = float(np.float32(2 * math.pi - C1 - C2))
            PI = 3.1415925

            def reduce_angle(step, y, k):
                step(TS(k, y, INV2PI, MAGIC, ALU.mult, ALU.add))
                step(TS(k, k, MAGIC, None, ALU.subtract))
                for c in (C1, C2, C3):
                    step(STT(out=y, in0=k, scalar=-c, in1=y, op0=ALU.mult, op1=ALU.add))
                return TS(y, y, PI, -PI, ALU.min, ALU.max)

            nc.vector.memset(ones[:, :], 1.0).then_inc(ones_set, 1)
            v.wait_ge(first_load, 16 * 8)
            setup = Steps(v, rope_ready)
            setup(nc.vector.tensor_copy(pos_f, pos_i[:, :]))
            ang, turns = at(mix_r, 0, NT, 48), at(mix_r, 192, NT, 48)
            for t in range(NT):
                setup(TS(ang[:, t, :], invf, pos_f[:, t:t + 1], None, ALU.mult))
            reduce_angle(setup, at(mix_r, 0, NT * 48), at(mix_r, 192, NT * 48)).then_inc(ang_ready, 1)
            v.wait_ge(sines_ready, 1)
            sines, halves = at(mix_r, 384, NT, 48), at(mix_r, 192, NT, 48)
            setup(TT(halves, halves, halves, ALU.mult))
            setup(TS(rope_t[:, :, 0:16], halves[:, :, 0:16], -2.0, 1.0, ALU.mult, ALU.add))
            setup(nc.vector.tensor_copy(rope_t[:, :, 16:32], sines[:, :, 0:16]))
            setup(TS(rope_t[:, :, 32:64], halves[:, :, 16:48], -2.0, 1.0, ALU.mult, ALU.add))
            nc.vector.tensor_copy(rope_t[:, :, 64:96], sines[:, :, 16:48]).then_inc(tables_ready, 1)
            v.wait_ge(tables_ready, 1)
            v.wait_ge(iota_ready, 1)

            def layer(l):
                step = Steps(v, v_step)
                V = Reader(v, 0, ready_v)

                def took(ins):
                    ins.then_inc(taken_v, 1)
                    v.wait_ge(taken_v, V.n)

                v.wait_ge(hy_in, 16 * 12)
                step(TS(bias_b, bias_b, 2.0 / (2 * S), None, ALU.mult))
                for j in range(3):
                    b = V.take(f"f{j}")
                    took(TS(mlp_y, b[0:64, :], hb[:, j:j + 1], hf[:, j:j + 1], ALU.add, ALU.mult))
                    reduce_angle(step, mlp_y, mlp_k).then_inc(sin_in, 1)
                v.wait_ge(mod_in, 16 * 18)
                lvv = lv.rearrange("p (a b n) -> p a b n", a=2, b=2)
                lp = f_tmp[:, 0:64].rearrange("p (a n) -> p a n", a=2)
                step(TT(lp, lvv[:, :, 0], lvv[:, :, 1], ALU.mult))
                nc.vector.tensor_reduce(lred, lp, X, ALU.add).then_inc(lam_pre, 1)
                step(TS(gd, gd, lam_b[:, 1:2], None, ALU.mult))
                win = lambda t: window[:, t].unsqueeze(1).to_broadcast([P, 2, CH])
                two = lambda ap: ap.rearrange("p (o c) -> p o c", o=2)
                for t in range(NT):
                    b = V.take(f"h{t}0")
                    took(TT(two(fsum[:, t]), two(b[:, :]), win(t), ALU.mult))
                    b = V.take(f"h{t}1")
                    took(TT(two(f_tmp), two(b[:, :]), win(t), ALU.mult))
                    step(TT(fdif[:, t], fsum[:, t], f_tmp, ALU.subtract))
                    TT(fsum[:, t], fsum[:, t], f_tmp, ALU.add).then_inc(filt_ready, 1)
                v.wait_ge(lam_exp, 1)
                step(TT(neglam, lexp[:, 1:2], lexp[:, 0:1], ALU.subtract))
                step(TT(neglam, neglam, lam_b[:, 0:1], ALU.subtract))
                b = V.take("fn")
                took(nc.vector.tensor_copy(s_b, b[:, :]))
                v.wait_ge(fscale, 1)
                for m in range(NT):
                    b = V.take(f"fc{m}")
                    took(TT(fc[:, m], b[:, :], s_b, ALU.mult))
                    step(TT(fc[:, m], fc[:, m], bias_b, ALU.add))
                b = V.take("fcn")
                took(TT(f_tmp[0:1, :], b[0:1, :], s_b[0:1, :], ALU.mult))
                step(TT(f_tmp[0:1, :], f_tmp[0:1, :], bias_b[0:1, :], ALU.add))
                step(nc.vector.tensor_copy(fcn, fc[:, 0]))
                step(TS(fcn[0:1, :], f_tmp[0:1, :], 0.5, None, ALU.mult))
                step(TS(fc[0:1, 0], fc[0:1, 0], 0.5, None, ALU.mult))
                for m in range(NT):
                    b = V.take(f"fd{m}")
                    took(TT(fd[:, m], b[:, :], s_b, ALU.mult))

                dest = {0: sh1, 1: gsc1, 2: mod[:, 0, :], 3: mod[:, 1, :], 4: mod[:, 2, :], 5: mod[:, 3, :]}

                def mod_take(c):
                    parts = mod_parts(c)
                    for half in range(2):
                        b = V.take(f"m{c}{half}")
                        mine = [p for p in parts if p[0] == half]
                        for _, lo, hi, vec, d0, d1 in mine:
                            dst = dest[vec][:, d0:d1]
                            last = STT(out=dst, in0=b[:, lo:hi], scalar=1.0 if vec in (1, 4) else 0.0, in1=dst,
                                       op0=ALU.add, op1=ALU.add)
                        took(last)

                for c in range(3):
                    mod_take(c)
                step(TT(gsc1, gsc1, ln1, ALU.mult))

                def rows(first, gsc, sh):
                    for t in range(NT):
                        v.wait_ge(nrs_ready, first + t + 1)
                        h = h_tok[:, t % 2, :]
                        step(STT(out=h, in0=x_tok[:, t, :], scalar=nrs[:, t:t + 1], in1=gsc, op0=ALU.mult, op1=ALU.mult))
                        TT(h, h, sh, ALU.add).then_inc(hrow_ready, 1)

                rows(0, gsc1, sh1)
                for m in range(6):
                    b = V.take(f"d{m}")
                    v.wait_ge(conv_mid, m + 1)
                    dst = vxT[:, m, :] if m < 4 else ydT[:, m - 4, :]
                    step(STT(out=dst[:, 1:S], in0=b[:, 0:S - 1], scalar=conv_w[:, m:m + 1], in1=dst[:, 1:S],
                             op0=ALU.mult, op1=ALU.add))
                    took(STT(out=dst[:, 0:S - 1], in0=b[:, 1:S], scalar=conv_w[:, 12 + m:13 + m], in1=dst[:, 0:S - 1],
                             op0=ALU.mult, op1=ALU.add))

                rope_before = []

                def rope(src, dst, heads, half, t, sig):
                    base = 0 if half == 16 else 32
                    cos = rope_t[:, t, base:base + half].unsqueeze(1).to_broadcast([P, heads, half])
                    sin = rope_t[:, t, base + half:base + 2 * half].unsqueeze(1).to_broadcast([P, heads, half])
                    if rope_before:
                        v.wait_ge(*rope_before.pop())
                    rope_before.append((sig, t + 1))
                    tmp = [r[:, 0:heads * half].rearrange("p (h c) -> p h c", h=heads) for r in rp]
                    TT(tmp[0], src[:, :, 0], cos, ALU.mult)
                    TT(tmp[1], src[:, :, 1], sin, ALU.mult)
                    TT(tmp[2], src[:, :, 0], sin, ALU.mult)
                    step(TT(tmp[3], src[:, :, 1], cos, ALU.mult))
                    TT(dst[:, :, 0], tmp[0], tmp[1], ALU.subtract)
                    TT(dst[:, :, 1], tmp[2], tmp[3], ALU.add).then_inc(sig, 1)

                for o in range(2):
                    for m in range(NT):
                        b = V.take(f"u{o}{m}")
                        n = o * NT + m
                        if n >= 2:
                            v.wait_ge(y_ready, n - 1)
                        col = slice(o * CH, (o + 1) * CH)
                        if m == 0:
                            TT(cm[:, 0, 0, 0:CH], b[:, 0:CH], fc[:, 0, col], ALU.mult)
                            TT(cm[:, 0, 0, CH:S], b[:, CH:S], fcn[:, col], ALU.mult)
                        else:
                            TT(two(cm[:, m % 2, 0]), two(b[:, :]), fc[:, m, col].unsqueeze(1).to_broadcast([P, 2, CH]), ALU.mult)
                        took(TT(two(cm[:, m % 2, 1]), two(b[:, :]), fd[:, m, col].unsqueeze(1).to_broadcast([P, 2, CH]), ALU.mult))
                    if o == 0:
                        for t in range(NT):
                            b = V.take(f"y0{t}")
                            took(TT(vx_tok[:, t, 0:CH], b[:, 0:CH], vx_tok[:, t, CH:S], ALU.mult))
                        v.wait_ge(crs_ready, 1)
                        for t in range(NT):
                            TS(cols_a[:, t, 0:256], cols_a[:, t, 0:256], crs[:, 2 * t:2 * t + 1], None, ALU.mult)
                            last = TS(cols_a[:, t, 256:384], cols_a[:, t, 256:384], crs[:, 2 * t + 1:2 * t + 2], None, ALU.mult)
                        last.then_inc(cn_ready, 1)
                        for t in range(NT):
                            kpe = cols_a[:, t, 384:416].rearrange("p (h a c) -> p h a c", h=1, a=2)
                            rope(kpe, kpe, 1, 16, t, kpe_ready)
                    else:
                        for c in range(2):
                            b = V.take(f"y1{c}")
                            took(TT(ydT[:, c], b[:, :], ydT[:, c], ALU.mult))
                for t in range(NT):
                    taken(v, f"q{t}")
                    q = q_tok[:, t, :].rearrange("p (h c) -> p h c", h=NH)[:, :, 64:96].rearrange("p h (a c) -> p h a c", a=2)
                    rope(q, q, NH, 16, t, qr_ready)
                done(v, "kv3")
                for t in range(NT):
                    rope(cols_b[:, t, 0:384].rearrange("p (h a c) -> p h a c", h=6, a=2),
                         rope_b[:, t, :].rearrange("p (h a c) -> p h a c", h=6, a=2), 6, 32, t, ropeb_ready)
                done(v, "kTa3")
                for t in range(NT):
                    taken(v, f"c{t}512")
                    rope(cols_c[:, t, 0:512].rearrange("p (h a c) -> p h a c", h=16, a=2),
                         rope_c[:, t, :].rearrange("p (h a c) -> p h a c", h=16, a=2), 16, 16, t, ropec_ready)

                for what, n in steps:
                    if what == "S":
                        g, h, qt, m = maps[n]
                        if g == "b":
                            b = V.take(f"S{n}")
                            lo, hi = band(qt)
                            done(v, f"T{out_of[n - 3]}")
                            pr = prob[:, n % 3, 0:hi - lo]
                            took(STT(out=pr, in0=b[:, lo:hi], scalar=SWA_SCALE, in1=mask[:, lo:hi], op0=ALU.mult, op1=ALU.add))
                            step(nc.vector.tensor_reduce(mx[:, n:n + 1], pr, X, ALU.max))
                            TS(nm[:, n:n + 1], mx[:, n:n + 1], sink[:, h:h + 1], -1.0, ALU.max, ALU.mult).then_inc(swa_s, 1)
                        else:
                            done(v, f"S{n}")
                            step(nc.vector.tensor_reduce(mx[:, n:n + 1], bank[4 + number[f"S{n}"][1] % 4][:, :], X, ALU.max))
                            TS(nm[:, n:n + 1], mx[:, n:n + 1], -(MLA_SCALE if g == "a" else DIFF_SCALE), None,
                               ALU.mult).then_inc(nm_ready, 1)
                    elif what == "T":
                        g, h, qt, ms = outs[n]
                        if g == "c":
                            o = n - 2 * NH * NT
                            taken(v, f"S{ms[1]}")
                            m1_, m2_ = ms
                            step(nc.vector.reciprocal(mx[:, m2_:m2_ + 1], rs[:, m2_:m2_ + 1]))
                            step(TS(kap[:, o:o + 1], rs[:, m1_:m1_ + 1], neglam, mx[:, m2_:m2_ + 1], ALU.mult, ALU.mult))
                            STT(out=prob[:, m1_ % 3, :], in0=prob[:, m2_ % 3, :], scalar=kap[:, o:o + 1],
                                in1=prob[:, m1_ % 3, :], op0=ALU.mult, op1=ALU.add).then_inc(diff_ready, 1)
                    elif what == "PV":
                        g, h, qt, ms = outs[n]
                        m0 = ms[0]
                        b = V.take(f"O{n}")
                        if g == "b":
                            v.wait_ge(prob_b, m0 - 15)
                            step(TT(den[:, m0 - 16:m0 - 15], rs[:, m0:m0 + 1], esink[:, m0 - 16:m0 - 15], ALU.add))
                            step(nc.vector.reciprocal(mx[:, m0:m0 + 1], den[:, m0 - 16:m0 - 15]))
                        else:
                            taken(v, f"S{m0}")
                            step(nc.vector.reciprocal(mx[:, m0:m0 + 1], rs[:, m0:m0 + 1]))
                        lo = {"a": 64, "b": h // 2 * 64, "c": h % 2 * 64}[g]
                        c = {"a": 0, "b": 256, "c": 512}[g] + 64 * h
                        took(TS(mix_tok[:, qt, c:c + 64], b[:, lo:lo + 64], mx[:, m0:m0 + 1], None, ALU.mult))
                    else:
                        mod_take(n)
                c_out = [mix_tok[:, t, 512:768].rearrange("p (h c) -> p h c", h=NH) for t in range(NT)]
                sq = at(pr_r, 0, NT, NH, 64)
                for t in range(NT):
                    last = TT(sq[:, t], c_out[t], c_out[t], ALU.mult)
                step(last)
                nc.vector.tensor_reduce(dss.rearrange("p (t h) -> p t h", t=NT), sq, X, ALU.add).then_inc(dss_ready, 1)
                v.wait_ge(drs_ready, 1)
                for t in range(NT):
                    last = TT(c_out[t], c_out[t], drs[:, 4 * t:4 * t + 4].unsqueeze(2).to_broadcast([P, NH, 64]), ALU.mult)
                step(last)
                for t in range(NT):
                    last = TT(c_out[t], c_out[t], gd.unsqueeze(1).to_broadcast([P, NH, 64]), ALU.mult)
                last.then_inc(mix_ready, 1)
                for half in range(2):
                    cols = slice(512 * half, 512 * half + 512)
                    for t in range(NT):
                        b = V.take(f"w{half}{t}")
                        tmp = (res_tmp[:, :], f_tmp)[t % 2]
                        took(TT(tmp, b[:, :], mod[:, 0, cols], ALU.mult))
                        last = TT(x_tok[:, t, cols], x_tok[:, t, cols], tmp, ALU.add)
                        if half:
                            last.then_inc(x_ready, 1)
                    if half == 0:
                        v.wait_ge(ln2_in, 16)
                        step(TT(mod[:, 2, :], mod[:, 2, :], ln2, ALU.mult))
                rows(NT, mod[:, 2, :], mod[:, 1, :])

                RED = nc.vector.tensor_reduce
                b = V.take("lg")
                took(nc.vector.tensor_copy(lg, b[:, 0:NT * 36].rearrange("p (t e) -> p t e", t=NT)))
                up = lambda ap, n: ap.unsqueeze(2).to_broadcast([P, NT, n])

                def first_max(src, best, sel, n):
                    step(RED(best, src, X, ALU.max))
                    step(TT(sel, src, up(best, n), ALU.is_equal))
                    step(TT(sel, sel, desc8[:, EPG - n:EPG].unsqueeze(1).to_broadcast([P, NT, n]), ALU.mult))
                    step(RED(pg, sel, X, ALU.max))
                    step(TT(sel, sel, up(pg, n), ALU.is_equal))

                first_max(lg[:, :, 0:NG], gmax, og, NG)
                TT(rd, lg[:, :, 0:NG], up(gmax, NG), ALU.subtract).then_inc(e_in, 1)
                for t in range(NT):
                    last = TT(r_tmp[:, t, :].rearrange("p (g x) -> p g x", g=NG), lg[:, t, NG:36].rearrange("p (g x) -> p g x", g=NG),
                              og[:, t, :].unsqueeze(2).to_broadcast([P, NG, EPG]), ALU.mult)
                step(last)
                step(RED(le, r_tmp.rearrange("p t (g x) -> p t x g", g=NG), X, ALU.add))
                first_max(le, v1, o1, EPG)
                step(STT(out=r_tmp2, in0=o1, scalar=NEG, in1=le, op0=ALU.mult, op1=ALU.add))
                first_max(r_tmp2, v2, o2, EPG)
                TT(vd, v2, v1, ALU.subtract).then_inc(e_in, 1)
                for o, mk in ((o1, m1), (o2, m2)):
                    for t in range(NT):
                        last = TT(mk[:, t, :].rearrange("p (g x) -> p g x", g=NG), o[:, t, :].unsqueeze(1).to_broadcast([P, NG, EPG]),
                                  og[:, t, :].unsqueeze(2).to_broadcast([P, NG, EPG]), ALU.mult)
                step(last)
                TT(msum, m1, m2, ALU.add).then_inc(m_ready, 1)
                v.wait_ge(e_out, 2)
                step(RED(gmax, rd, X, ALU.add))
                step(nc.vector.reciprocal(pg, gmax))
                step(TS(v1, vd, 1.0, None, ALU.add))
                step(nc.vector.reciprocal(v2, v1))
                step(TT(wgt[:, 0], pg, v2, ALU.mult))
                step(TT(wgt[:, 1], wgt[:, 0], vd, ALU.mult))
                b = V.take("before")
                low = b[:, 0:P].rearrange("p (t e) -> p t e", t=NT)
                tot = b[:, P:2 * P].rearrange("p (t e) -> p t e", t=NT)
                step(nc.vector.tensor_copy(cum, low))
                step(RED(cnt, b[:, P:2 * P].rearrange("p (t e) -> p e t", t=NT), X, ALU.add))
                for k in (3, 2, 1):
                    last = TT(cum[:, NT - k:NT], cum[:, NT - k:NT], tot[:, 0:k], ALU.add)
                    if k > 1:
                        step(last)
                took(last)
                step(STT(out=cum, in0=cum, scalar=float(NE), in1=iota_e.unsqueeze(1).to_broadcast([P, NT, NE]), op0=ALU.mult, op1=ALU.add))
                for k, mk in ((0, m1), (1, m2)):
                    step(TT(r_tmp, mk, cum, ALU.mult))
                    step(RED(dest_f[:, k], r_tmp, X, ALU.add))
                nc.vector.tensor_copy(dest_i[:, :, :], dest_f).then_inc(dest_ready, 1)
                v.wait_ge(rw_in, 16 * 4)
                e7 = lambda ap: ap.rearrange("p (e j) -> p e j", j=7)
                step(TT(e7(flag), cnt.unsqueeze(2).to_broadcast([P, NE, 7]), e7(block_at), ALU.is_gt))
                step(nc.vector.tensor_tensor_scan(pos, flag, flag, 0.0, ALU.add, ALU.max))
                step(STT(out=pick, in0=pos, scalar=part_id, in1=flag, op0=ALU.is_equal, op1=ALU.mult))
                step(TT(pick, pick, block_id, ALU.mult))
                RED(o_code[:, 0:1], pick, X, ALU.add).then_inc(code_ready, 1)
                step(nc.vector.tensor_copy(tot_i[0:1, 0:1], pos[0:1, NE * 7 - 1:NE * 7]))
                step(nc.vector.tensor_copy(tot_i[0:1, 1:2], over_tot[0:1, 0:1]))
                step(TT(over_tot[0:1, 0:1], over_tot[0:1, 0:1], pos[0:1, NE * 7 - 1:NE * 7], ALU.add))
                b = V.take("over")
                took(nc.vector.tensor_copy(over_i[0:1, :], b[0:1, 0:16]))

                def indices(src, hi, low, gather, scatter):
                    step(TS(hi, src, float(S), -float(S), ALU.is_ge, ALU.mult))
                    step(TT(low, src, hi, ALU.add))
                    nc.vector.tensor_copy(gather, low)
                    return nc.vector.tensor_copy(scatter, src)

                v.wait_ge(tab_in, 16)
                indices(slot_f[0:CAP], hi_f[0:CAP], gidx_f[0:CAP], gslot_i[0:CAP, :], slot_i[0:CAP, :]).then_inc(slots_ready, 1)

                def times_up(b):
                    return TT(act_h[0:CAP, b, :], sil[0:CAP, b, :], bank[2 + b][CAP:P, 0:F], ALU.mult)

                def act_evac(b):
                    return nc.vector.tensor_copy(act_T[:, b, 0:2 * CAP], bank[4 + b][:, 0:2 * CAP])

                def y_evac(b):
                    return nc.vector.tensor_copy(yg[0:CAP, b, 512:1024], bank[6 + b][CAP:P, :])

                def expert(i, s):
                    b = s % 2
                    pre = isinstance(i, int) and i == 0 and s < 2
                    v.wait_ge(silu_ready, 4 * i + s + 1)
                    if not pre:
                        v.wait_ge(at_done, 4 * i + s - 1)
                    times_up(b).then_inc(acth_ready, 1)
                    v.wait_ge(at_done, 4 * i + s + 1)
                    if not pre:
                        v.wait_ge(y_done, 4 * i + s - 1)
                    act_evac(b).then_inc(actT_ready, 1)
                    v.wait_ge(y_done, 4 * i + s + 1)
                    if not pre:
                        v.wait_ge(scattered[b], NE // 2 * 16 * l + 16 * (2 * i + s // 2))
                    y_evac(b).then_inc(yg_hi, 1)

                for s in range(4):
                    expert(0, s)
                with v.Fori(1, NE // 4) as i:
                    for s in range(4):
                        expert(i, s)
                for b in range(2):
                    v.wait_ge(scattered[b], NE // 2 * 16 * l + NE // 2 * 16)
                nc.vector.tensor_copy(part_id, part_id).then_inc(ov_yv, 1)
                n_over = v.value_load(tot_i[0:1, 0:1], min_val=0, max_val=EXTRA)
                with v.Fori(0, EXTRA) as r:
                    with v.If(r < n_over):
                        v.wait_ge(ov_i, 16 * r + 16)
                        v.wait_ge(ov_done, r + 1)
                        TS(hi_f[0:CAP, 0:1], o_idx[0:CAP, 0:1], float(S), -float(S), ALU.is_ge, ALU.mult).then_inc(ov_t, 1)
                        v.wait_ge(ov_t, 2 * r + 1)
                        TT(gidx_f[0:CAP, 0:1], o_idx[0:CAP, 0:1], hi_f[0:CAP, 0:1], ALU.add).then_inc(ov_t, 1)
                        v.wait_ge(ov_t, 2 * r + 2)
                        nc.vector.tensor_copy(gather_i[0:CAP, 0:1], gidx_f[0:CAP, 0:1])
                        nc.vector.tensor_copy(scatter_i[0:CAP, 0:1], o_idx[0:CAP, 0:1]).then_inc(ov_i2, 1)
                        v.wait_ge(ov_sil, r + 1)
                        times_up(0).then_inc(ov_act, 1)
                        v.wait_ge(ov_at, r + 1)
                        act_evac(0).then_inc(ov_aT, 1)
                        v.wait_ge(ov_y, r + 1)
                        y_evac(0).then_inc(ov_yv, 1)
                    with v.Else():
                        v.nop()
                for t in range(NT):
                    v.wait_ge(pair_in[t % 2], 16 * (t // 2 + 1))
                    step(TS(comb, pair[:, t % 2, 0], wgt[:, 0, t:t + 1], None, ALU.mult))
                    STT(out=comb, in0=pair[:, t % 2, 1], scalar=wgt[:, 1, t:t + 1], in1=comb, op0=ALU.mult, op1=ALU.add).then_inc(pair_used, 1)
                    v.wait_ge(pair_used, t + 1)
                    step(TT(comb, comb, mod[:, 3, :], ALU.mult))
                    step(TT(x_tok[:, t, :], x_tok[:, t, :], comb, ALU.add))
                v.drain().then_inc(layer_done, 1)

            with v.Fori(0, DEPTH) as l:
                layer(l)
                v.wait_ge(layer_go, l + 1)
            v.wait_ge(final_in, 16)
            for t in range(NT):
                v.wait_ge(fin_rs, t + 1)
                h = h_tok[:, t % 2, :]
                STT(out=h, in0=x_tok[:, t, :], scalar=nrs[:, t:t + 1], in1=gsc1, op0=ALU.mult, op1=ALU.mult).then_inc(fin_row, 1)


_INS = ["x", "c", "positions", "ln1_g", "ln2_g", "ada_w", "ada_b", "w_in", "mla_q_norm", "mla_kv_norm",
        "mla_w_uq", "mla_w_ukv", "swa_sink", "diff_lambda", "diff_norm_g", "hy_conv_w", "hy_conv_b",
        "hy_w1", "hy_b1", "hy_w2", "hy_b2", "hy_w3", "hy_b3", "hy_w4", "hy_sin_freq", "hy_bias", "w_out",
        "router_g_w", "router_g_b", "router_e_w", "router_e_b", "moe_w_gate", "moe_w_up", "moe_w_down",
        "final_g"]


def kernel(**inputs):
    import concourse.bacc as bacc
    from concourse.bass_utils import run_bass_kernel_spmd

    nc = bacc.Bacc("TRN2", target_bir_lowering=False, num_devices=1)
    arrays, aps = {}, {}
    for name, arr in [(n, np.ascontiguousarray(inputs[n])) for n in _INS] + list(host_constants().items()):
        arrays[f"in_{name}_dram"] = arr
        aps[name] = nc.dram_tensor(f"in_{name}_dram", arr.shape, mybir.dt.from_np(arr.dtype), kind="ExternalInput").ap()
    out = nc.dram_tensor("out_0_dram", (1, S, D), F32, kind="ExternalOutput").ap()
    trunk(nc, aps, out)
    r = run_bass_kernel_spmd(nc, [arrays], core_ids=[0])
    return r.results[0]["out_0_dram"]
```

```python
from contextlib import ExitStack
import math

import numpy as np
import concourse.bass as bass
from concourse import mybir

F32 = mybir.dt.float32
I32 = mybir.dt.int32
ALU = mybir.AluOpType
ACT = mybir.ActivationFunctionType
X = mybir.AxisListType.X

P = 128
DEPTH, D, S = 2, 1024, 512
NT = S // P
KT = D // P
EPS = 1e-6
NEG = -1e30
MAGIC = 1.5 * 2.0 ** 23

A_COLS, B_COLS, C_COLS, D_COLS = 416, 512, 768, 768
IN_COLS = A_COLS + B_COLS + C_COLS + D_COLS
NH = 4
MLA_SCALE = 96.0 ** -0.5
SWA_SCALE = 0.125
DIFF_SCALE = 32.0 ** -0.5
CH = 256

SLOT = 6144
ADA = 768
N_ADA = 6 * D // ADA
NE, NG, EPG, F = 32, 4, 8, 256
CAP = 64
EXTRA = 2 * S // CAP - 1
EMPTY = 4096.0


def host_constants():
    t = np.arange(S, dtype=np.float64)
    k = np.arange(S, dtype=np.float64)
    ang = 2 * np.pi * ((t[:, None] * k[None, :]) % (2 * S)) / (2 * S)
    cos, sin = np.cos(ang), np.sin(ang)
    alt = 1.0 - 2.0 * (np.arange(S) % 2)
    sin_f = sin[:, :P].copy()
    sin_f[:, 0] = alt
    sin_i = sin[:P, :].copy()
    sin_i[0, :] = alt
    tl = np.linspace(0.0, 1.0, S, dtype=np.float32)
    w = (2.0 * math.pi * np.arange(S, dtype=np.float32) / S).astype(np.float32)
    f = np.linspace(1e-4, 15, 16, dtype=np.float32)
    wf = (w[:, None] * f).astype(np.float32)
    z = np.concatenate([tl[:, None], np.cos(wf), -np.sin(wf)], axis=-1)
    decay = np.linspace(math.log(1e-2) / 1.5, math.log(1e-2) / 0.3, CH, dtype=np.float32)
    window = np.exp(-tl[:, None] * np.abs(decay))
    q = np.arange(P)
    mask = np.zeros((P, 3 * P))
    mask[:, :P] = np.where(q[None, :] >= q[:, None], 0.0, NEG)
    mask[:, 2 * P:] = np.where(q[None, :] <= q[:, None], 0.0, NEG)
    inv = [np.exp(-math.log(10000.0) * np.arange(h, dtype=np.float32) / h) for h in (16, 32)]
    lam = [[0.8 - 0.6 * math.exp(-0.3 * l), 1.0 - (0.8 - 0.6 * math.exp(-0.3 * l))] for l in range(DEPTH)]
    tri = (q[:, None] < q[None, :]) * 1.0
    grid = np.arange(NE * 7)
    block_id = (grid // 7) * 8 + grid % 7 + 1
    block_at = (grid % 7 + 1) * float(CAP)
    desc = np.arange(EPG, 0, -1)
    misc = np.concatenate([np.arange(NE), desc])
    out = {"k_cos": cos, "k_sin": sin, "k_sin_f": sin_f, "k_sin_i": sin_i, "k_z": z.T, "k_window": window,
           "k_mask": mask, "k_inv": np.concatenate(inv)[None], "k_lam": np.array(lam), "k_tri": tri,
           "k_ident": np.eye(P), "k_misc": misc[None], "k_blocks": np.stack([block_id, block_at]), "k_empty": np.full((P, S * NE // P), EMPTY)}
    return {n: np.ascontiguousarray(a, dtype=np.float32) for n, a in out.items()}


def trunk(nc, a, out):
    h2_rows = nc.dram_tensor("h2_rows", (S, D), F32, kind="Internal").ap()
    slots_of = nc.dram_tensor("slots_of", (S * NE, 1), F32, kind="Internal").ap()
    pair_rows = nc.dram_tensor("pair_rows", (2 * S, D), F32, kind="Internal").ap()

    ctx = ExitStack()
    with ctx:
        def sb(name, shape, dt=F32):
            return ctx.enter_context(nc.sbuf_tensor(name, shape, dt))

        layer_sems = []

        def sem(name, per_layer=True):
            s = ctx.enter_context(nc.semaphore(name))
            if per_layer:
                layer_sems.append(s)
            return s

        ARENA = 2 * SLOT
        ARENA_WORDS = 18432
        big = sb("big", [P, ARENA + ARENA_WORDS])
        x_tok = sb("x_tok", [P, NT, D])
        mod = sb("mod", [P, 4, D])
        ht_r = sb("ht_r", [P, 4096])
        mix_r = sb("mix_r", [P, 3072])
        ydT = sb("ydT", [P, 2, S])
        pr_r = sb("pr_r", [P, 3072])
        c_rep = sb("c_rep", [P, KT, 32])
        part = sb("part", [P, ADA])
        rope_t = sb("rope_t", [P, NT, 96])
        ident = sb("ident", [P, P])
        ones = sb("ones", [P, P])
        tri = sb("tri", [P, P])
        mask = sb("mask", [P, 3 * P])
        small = sb("small", [P, 672])
        gather_i = sb("gather_i", [P, 2], I32)
        scatter_i = sb("scatter_i", [P, 2], I32)
        over_i = sb("over_i", [1, 16], I32)
        tot_i = sb("tot_i", [1, 2], I32)

        def at(buf, off, *dims, rows=P):
            n = int(np.prod(dims))
            v = buf[0:rows, off:off + n]
            if len(dims) == 1:
                return v
            names = "abcd"[:len(dims)]
            return v.rearrange(f"p ({' '.join(names)}) -> p {' '.join(names)}", **{names[i]: dims[i] for i in range(len(dims))})

        small_at = [0]

        def sm(n, rows=P):
            o = small_at[0]
            small_at[0] += n
            assert small_at[0] <= 672, small_at
            return small[0:rows, o:o + n]

        def slot(s, *dims):
            return at(big, s * SLOT, *dims)

        def ar(off, *dims, rows=P):
            return at(big, ARENA + off, *dims, rows=rows)

        cosm, sinm = ar(0, NT, S), ar(2048, NT, S)
        sin_f, sin_i = ar(4096, NT, P), ar(4608, S)
        fc, fd, fcn = ar(5120, NT, S), ar(7168, NT, S), ar(9216, S)
        fsum, fdif = ar(9728, NT, S), ar(11776, NT, S)
        yre, yim = ar(9728, NT, CH), ar(10752, NT, CH)
        cm = ar(11776, 2, 2, S)
        vxT = ar(13824, 4, S)
        vx_tok = ar(15872, NT, 2 * CH)
        sq_sum, sq_dif = ar(13824, NT, S), ar(15872, NT, S)
        cols_b, cols_c = ar(0, NT, B_COLS), ar(2048, NT, C_COLS)
        kv_tok, cT, k_tok = ar(5120, NT, S), ar(7168, 3, S), ar(8704, NT, NH, 96)
        qT_a, kT_a = ar(10240, NH, S), ar(12288, NH, S)
        rope_b = ar(14336, NT, 384)
        w_uq, w_ukv = ar(14336, 2, 384), ar(14336 + 768, S)
        qT_b, kT_b = ar(15872, NH, S), ar(15872 + 2048, S)
        rope_c, kT_c = ar(7168, NT, S), ar(7168 + 2048, 2, S)
        qT_c = at(ht_r, 0, 8, S)
        hT = at(ht_r, 0, KT, S)
        mixT = at(ht_r, 0, 6, S)
        w4, zT = at(ht_r, 0, D, rows=64), at(ht_r, 1024, S, rows=33)
        bias_b, s_b, window = at(ht_r, 1536, S), at(ht_r, 2048, S), at(ht_r, 2560, NT, CH)
        sh1, gsc1, ln1 = (at(mix_r, 1024 * j, D) for j in range(3))
        cols_a = at(mix_r, 0, NT, A_COLS)
        mix_tok = at(mix_r, 0, NT, 768)
        h_tok = at(pr_r, 0, 2, D)
        f_tmp = at(pr_r, 2048, S)
        mlp_y, mlp_k, mlp_h = (at(pr_r, 512 * j, S, rows=64) for j in range(3))
        q_tok = at(pr_r, 0, NT, 384)
        rp = [at(pr_r, 1536 + 256 * j, 256) for j in range(4)]
        prob, probT = at(pr_r, 0, 4, S), at(pr_r, 2048, 2, S)
        ln2 = ar(12288, D)
        h2_tok = ar(12288 + D, NT, D)
        xg, yg = at(ht_r, 0, 2, D), at(ht_r, 2048, 2, D)
        xT = at(pr_r, 0, 2, KT * CAP)
        sil, act_h, act_T = at(pr_r, 1024, 2, F), at(pr_r, 1536, 2, F), at(pr_r, 2048, 2, P)
        rank_is, id_of = at(pr_r, 2304, 2, NT, CAP), at(pr_r, 2304 + 2 * NT * CAP, 2, NT, NE)
        pair = ar(5120, NT, 2, D)
        comb = ar(5120 + NT * 2 * D, 2, D)
        rt = [0]

        def rb(*dims, rows=P):
            o = rt[0]
            rt[0] += int(np.prod(dims))
            assert rt[0] <= 3072, rt
            return at(mix_r, o, *dims, rows=rows)

        lgT = rb(S, rows=36)
        lg = rb(NT, 36)
        m1, m2 = rb(NT, NE), rb(NT, NE)
        msum = rb(NT, NE)
        cum = rb(NT, NE)
        r_tmp = rb(NT, NE)
        r_tmp2 = rb(NT, EPG)
        og, o1, o2, le = rb(NT, NG), rb(NT, EPG), rb(NT, EPG), rb(NT, EPG)
        rd = rb(NT, NG)
        gmax, pg, v1, v2, vd = (rb(NT) for _ in range(5))
        wgt = rb(2, NT)
        rank_f = rb(2, NT)
        dest_f = rb(2, NT)
        slot_f, gidx_f, hi_f = rb(NE), rb(NE), rb(NE)
        cnt = rb(NE)
        flag, pos, pick = rb(NE * 7), rb(NE * 7), rb(NE * 7)
        o_code = rb(2)
        block_id, block_at = rb(NE * 7), rb(NE * 7)
        o_idx = rb(4)
        r_w = rb(KT, 36)
        dest_i = sb("dest_i", [P, 2, NT], I32)
        slot_i = sb("slot_i", [P, NE], I32)
        gslot_i = sb("gslot_i", [P, NE], I32)

        c_act = sm(KT)
        hw1, hw2, hw3 = sm(64, 33), sm(64, 64), sm(64, 64)
        hb, hf = sm(3, 64), sm(3, 64)
        conv_w, conv_b = sm(18), sm(6)
        lred, lexp, lam_b, neglam = sm(2), sm(2), sm(2), sm(1)
        gd, gn = sm(64), sm(3)
        sink = sm(NH)
        nss, nrs, f_s = sm(NT), sm(NT), sm(4)
        css, crs = sm(2 * NT), sm(2 * NT)
        lv = sm(P)
        mx, nm, rs = lv[:, 0:64], lv[:, 64:P], sm(64)
        c_sb, pos_f = lv[:, 0:KT], rs[:, 0:NT]
        esink, den = sm(16), sm(16)
        kap = sm(16)

        dss, drs = sm(16), sm(16)
        invf = sm(48)
        r_b = sm(1, 36)
        tok_id = sm(2 * NT)
        part_id = sm(1)
        over_tot, neghalf = sm(2), sm(1)
        misc = sb("misc", [P, NE + EPG])
        pos_i = sb("pos_i", [P, NT], I32)
        iota_e = misc[:, 0:NE]
        desc8 = misc[:, NE:NE + EPG]

        bank = [ctx.enter_context(nc.psum_tensor(f"bank{i}", [P, 512], F32)) for i in range(8)]

        first_load = sem("first_load", False)
        layer_done = sem("layer_done", False)
        layer_go = sem("layer_go", False)
        fin_sq, fin_mid, fin_rs, fin_row = (sem(n, False) for n in "fin_sq fin_mid fin_rs fin_row".split())
        out_row = [sem(f"out_row{i}", False) for i in range(2)]
        table_dma = sem("table_dma", False)
        gathered = [sem(f"gathered{i}", False) for i in range(2)]
        scattered = [sem(f"scattered{i}", False) for i in range(2)]
        over_gathered, over_scattered = sem("over_gathered", False), sem("over_scattered", False)

        ready_v, ready_a = sem("ready_v"), sem("ready_a")
        taken_v, taken_a = sem("taken_v"), sem("taken_a")
        v_step, a_step, g_step = sem("v_step"), sem("a_step"), sem("g_step")
        slot_full = [sem(f"slot_full{i}", False) for i in range(4)]
        x_in, hy_in, vec_in = (sem(n, False) for n in "x_in hy_in vec_in".split())
        dft_in, mod_in, ln2_in, mla_w_in, fill_in, rw_in, hot_ready, ov_i = (
            sem(n) for n in "dft_in mod_in ln2_in mla_w_in fill_in rw_in hot_ready ov_i".split())
        sin_in, mlp_ready = sem("sin_in"), sem("mlp_ready")
        filt_ready, sq_ready, fscale, srep_ready = sem("filt_ready"), sem("sq_ready"), sem("fscale"), sem("srep_ready")
        nss_ready, nrs_ready, hrow_ready = sem("nss_ready"), sem("nrs_ready"), sem("hrow_ready")
        conv_mid, y_ready = sem("conv_mid"), sem("y_ready")
        css_ready, crs_ready, cn_ready = sem("css_ready"), sem("crs_ready"), sem("cn_ready")
        kpe_ready, ktok_ready, qr_ready, ropeb_ready, ropec_ready, padded = (
            sem(n) for n in "kpe_ready ktok_ready qr_ready ropeb_ready ropec_ready padded".split())
        nm_ready, swa_s, prob_b, diff_ready, lam_pre, lam_exp = (
            sem(n) for n in "nm_ready swa_s prob_b diff_ready lam_pre lam_exp".split())
        dss_ready, drs_ready, mix_ready, x_ready = (sem(n) for n in "dss_ready drs_ready mix_ready x_ready".split())
        h2_stored = [sem("h2_stored0"), sem("h2_stored1")]
        e_in, e_out, m_ready, dest_ready, slots_ready, code_ready = (
            sem(n) for n in "e_in e_out m_ready dest_ready slots_ready code_ready".split())
        xt_done, xt_ready, gu_done, silu_ready, acth_ready, at_done, actT_ready, y_done, yg_lo, yg_hi = (
            sem(n) for n in "xt_done xt_ready gu_done silu_ready acth_ready at_done actT_ready y_done yg_lo yg_hi".split())
        ov_w, ov_i2, ov_x, ov_xt, ov_gu, ov_sil, ov_act, ov_at, ov_aT, ov_y, ov_ya, ov_yv, ov_t, ov_done = (
            sem("ov_" + n) for n in "w i2 x xt gu sil act at aT y ya yv t done".split())
        moe_done, pair_in = sem("moe_done"), [sem(f"pair_in{t}") for t in range(NT)]
        gated, summed, scaled, x_new = (sem(n) for n in "gated summed scaled x_new".split())
        gidx_ready, sidx_ready = sem("gidx_ready", False), sem("sidx_ready", False)
        waited = sem("waited")
        ones_set, ang_ready, rope_ready, tables_ready = (sem(n, False) for n in ("ones_set", "ang_ready", "rope_ready", "tables_ready"))
        c_ready, rep_ready, sines_ready, iota_ready, final_in = (
            sem(n, False) for n in "c_ready rep_ready sines_ready iota_ready final_in".split())

        class Steps:

            def __init__(self, eng, s):
                self.eng, self.s, self.n = eng, s, 0

            def __call__(self, ins):
                ins.then_inc(self.s, 1)
                self.n += 1
                self.eng.wait_ge(self.s, self.n)

        number = {}

        class Products:

            def __init__(self, pe, group, first, taken):
                self.pe, self.group, self.first, self.taken, self.n = pe, group, first, taken, 0

            def bank(self, name):
                if self.n >= 4:
                    self.pe.wait_ge(self.taken, self.n - 3)
                number[name] = (self.group, self.n)
                self.n += 1
                return bank[self.first + (self.n - 1) % 4]

        class Reader:
            def __init__(self, eng, first, ready):
                self.eng, self.first, self.ready, self.n = eng, first, ready, 0

            def take(self, name):
                assert number[name][1] == self.n, (name, number[name], self.n)
                self.n += 1
                self.eng.wait_ge(self.ready, self.n)
                return bank[self.first + (self.n - 1) % 4]

        def done(eng, name):
            g, n = number[name]
            eng.wait_ge(ready_v if g == "v" else ready_a, n + 1)

        def taken(eng, name):
            g, n = number[name]
            eng.wait_ge(taken_v if g == "v" else taken_a, n + 1)

        outs, maps = [], []
        for h in range(NH):
            for qt in range(NT):
                outs.append(("a", h, qt, [len(maps)]))
                maps.append(("a", h, qt, 0))
        for h in range(NH):
            for qt in range(NT):
                outs.append(("b", h, qt, [len(maps)]))
                maps.append(("b", h, qt, 0))
        for h in range(NH):
            for qt in range(NT):
                outs.append(("c", h, qt, [len(maps), len(maps) + 1]))
                maps += [("c", h, qt, 0), ("c", h, qt, 1)]
        out_of = {m: o for o, v in enumerate(outs) for m in v[3]}
        MOD_AFTER = {3: 3, 8: 4, 13: 5, 18: 6, 23: 7}
        steps, given = [], 0
        for o, v in enumerate(outs):
            if v[0] == "c":
                steps.append(("K", o))
            while given < min(v[3][-1] + 3, len(maps)):
                steps.append(("S", given))
                given += 1
            steps.append(("T", o))
            if o:
                steps.append(("PV", o - 1))
            if o - 1 in MOD_AFTER:
                steps.append(("M", MOD_AFTER[o - 1]))
            if o in MOD_AFTER:
                steps.append(("P", MOD_AFTER[o]))
        steps.append(("PV", len(outs) - 1))

        def band(n):
            return (P if n == 0 else 0), (2 * P if n == NT - 1 else 3 * P)

        def mod_parts(c):
            parts = []
            for half, (lo, n) in enumerate(((0, 512), (512, 256))):
                g0 = c * ADA + lo
                g = g0
                while g < g0 + n:
                    e = min(g0 + n, (g // D + 1) * D)
                    parts.append((half, g - g0, e - g0, g // D, g % D, g % D + e - g))
                    g = e
            return parts

        CHUNKS = [("ada", 0), ("ada", 1), ("ada", 2), ("in", "d"), ("in", "a"), ("in", "b"), ("in", "c"),
                  ("ada", 3), ("ada", 4), ("ada", 5), ("ada", 6), ("ada", 7), ("out", 0), ("out", 1)]
        chunk_at = {c: (n % 2, n // 2) for n, c in enumerate(CHUNKS)}
        col0 = {"a": (0, A_COLS), "b": (A_COLS, B_COLS), "c": (A_COLS + B_COLS, C_COLS),
                "d": (A_COLS + B_COLS + C_COLS, D_COLS)}
        USES = len(CHUNKS) // 2

        def chunk_slot(c):
            return chunk_at[c][0]

        def slot_base(s, l):
            return l * (16 * (USES if s < 2 else 0) + 48 * NE // 4)

        def chunk_wait(eng, c, l):
            s, n = chunk_at[c]
            eng.wait_ge(slot_full[s], slot_base(s, l) + 16 * (n + 1))

        def chunk_used(eng, c):
            kind, which = c
            if kind == "ada":
                done(eng, f"p{which}1")
            elif kind == "out":
                done(eng, f"w{which}{NT - 1}")
            else:
                done(eng, {"d": "d5", "a": "a30", "b": "b30", "c": "c3512"}[which])

        def expert_full(s, i, l):
            return slot_base(s, l) + 16 * (USES if s < 2 else 0) + 48 + 48 * i

        def expert_slot(s):
            wg = slot(s, 3, KT, F)[:, 0]
            wu = slot(s, 3, KT, F)[:, 1]
            wd = at(big, s * SLOT + 4096, 2, D)
            return wg, wu, wd

        def row(ap2):
            return ap2.partition_broadcast(P) if len(ap2.shape) == 1 else ap2.broadcast_to([P, ap2.shape[1]])

        def of_layer(name, l):
            v = a[name]
            names = " ".join("bcde"[:len(v.shape) - 1])
            s = v[bass.ds(l, 1)]
            return s.rearrange(f"a {names} -> (a {names.split(' ')[0]}) {' '.join(names.split(' ')[1:])}".rstrip())

        def row_of(name, l):
            return a[name][bass.ds(l, 1)]

        ctx.enter_context(nc.allow_non_contiguous_dma(reason="vectors of a few KB with one element on a partition"))
        block = ctx.enter_context(nc.Block())

        @block.tensor
        def _(pe):
            pe.wait_ge(first_load, 16 * 7)
            pe.wait_ge(ones_set, 1)
            pe.wait_ge(rep_ready, 1)

            def mm(o, l, r, start=True, stop=True):
                return nc.tensor.matmul(o, l, r, start=start, stop=stop)

            def layer(l):
                V = Products(pe, "v", 0, taken_v)
                A = Products(pe, "a", 4, taken_a)

                def mod_parts_sum(c):
                    chunk_wait(pe, ("ada", c), l)
                    w = at(big, chunk_slot(("ada", c)) * SLOT, KT, ADA)
                    for half, (lo, n) in enumerate(((0, 512), (512, 256))):
                        b = A.bank(f"p{c}{half}")
                        for k in range(2):
                            for g in range(4):
                                last = mm(b[32 * g:32 * g + 32, 0:n], c_rep[:, 2 * g + k, :], w[:, 2 * g + k, lo:lo + n], k == 0, k == 1)
                        last.then_inc(ready_a, 1)

                def mod_sum(c):
                    for half, (lo, n) in enumerate(((0, 512), (512, 256))):
                        taken(pe, f"p{c}{half}")
                        mm(V.bank(f"m{c}{half}")[:, 0:n], ones[:, :], part[:, lo:lo + n]).then_inc(ready_v, 1)

                pe.wait_ge(hy_in, 16 * 11 * (l + 1))
                pe.sem_inc(waited, 1)
                for j, (w, n) in enumerate(((hw1, 33), (hw2, 64), (hw3, 64))):
                    if j:
                        pe.wait_ge(mlp_ready, j)
                    b = V.bank(f"f{j}")
                    mm(b[0:64, :], w, zT if j == 0 else mlp_h).then_inc(ready_v, 1)
                    if j:
                        mod_sum(j - 1)
                    if j < 2:
                        mod_parts_sum(j)
                pe.wait_ge(mlp_ready, 3)
                for t in range(NT):
                    for d in range(2):
                        b = V.bank(f"h{t}{d}")
                        mm(b[:, :], mlp_h[:, t * P:(t + 1) * P], w4[:, d * S:(d + 1) * S]).then_inc(ready_v, 1)
                pe.wait_ge(sq_ready, NT)
                b = A.bank("fp")
                for i, sq in enumerate((sq_sum, sq_dif)):
                    for t in range(NT):
                        last = mm(b[32 * t:32 * t + 32, :], ones[:, 0:32], sq[:, t], i == 0, i == 1)
                last.then_inc(ready_a, 1)
                mod_parts_sum(2)
                taken(pe, "fp")
                b = V.bank("fn")
                for j in range(4):
                    last = mm(b[:, j:j + 1], f_tmp[:, j * P:(j + 1) * P], ones[:, 0:1])
                last.then_inc(ready_v, 1)
                pe.wait_ge(srep_ready, 1)
                b = V.bank("fnb")
                for j in range(4):
                    last = mm(b[:, j * P:(j + 1) * P], f_tmp[:, j * P:(j + 1) * P], ident[:, :])
                last.then_inc(ready_v, 1)
                mod_sum(2)
                pe.wait_ge(dft_in, 64)
                pe.wait_ge(filt_ready, NT)

                def dft(name, w, col, n, rhs):
                    b = V.bank(name)
                    for kt in range(NT):
                        last = mm(b[0:n, :], w[:, kt, col:col + n], rhs[:, kt, :], kt == 0, kt == NT - 1)
                    last.then_inc(ready_v, 1)

                for m in range(NT):
                    dft(f"fc{m}", cosm, m * P, P, fsum)
                dft("fcn", sin_f, 0, 1, fsum)
                for m in range(NT):
                    dft(f"fd{m}", sinm, m * P, P, fdif)

                def transpose_rows(n):
                    t = n % NT
                    pe.wait_ge(hrow_ready, n + 1)
                    src = h_tok[:, t % 2, :] if n < NT else h2_tok[:, t, :]
                    for half in range(2):
                        b = A.bank(f"hT{n}{half}")
                        for j in range(4):
                            rows = src.rearrange("p (c k) -> p k c", k=KT)[:, 4 * half + j]
                            last = nc.tensor.transpose(b[:, j * P:(j + 1) * P], rows, ident[:, :])
                        last.then_inc(ready_a, 1)

                for t in range(NT):
                    transpose_rows(t)
                taken(pe, "hT31")

                chunk_wait(pe, ("in", "d"), l)
                w = at(big, chunk_slot(("in", "d")) * SLOT, KT, D_COLS)
                for m in range(6):
                    b = V.bank(f"d{m}")
                    for k in range(KT):
                        last = mm(b[:, :], w[:, k, m * P:(m + 1) * P], hT[:, k, :], k == 0, k == KT - 1)
                    last.then_inc(ready_v, 1)

                def project(g, tiles=range(NT)):
                    c = ("in", g)
                    chunk_wait(pe, c, l)
                    n = col0[g][1]
                    w = at(big, chunk_slot(c) * SLOT, KT, n)
                    for t in tiles:
                        for lo in range(0, n, 512):
                            m = min(512, n - lo)
                            b = A.bank(f"{g}{t}{lo}")
                            for k in range(KT):
                                last = mm(b[:, 0:m], hT[:, k, t * P:(t + 1) * P], w[:, k, lo:lo + m], k == 0, k == KT - 1)
                            last.then_inc(ready_a, 1)

                project("a")
                taken(pe, "d3")
                for t in range(NT):
                    b = A.bank(f"vx{t}")
                    for c in range(4):
                        last = nc.tensor.transpose(b[:, c * P:(c + 1) * P], vxT[:, c, t * P:(t + 1) * P], ident[:, :])
                    last.then_inc(ready_a, 1)
                for o in range(2):
                    taken(pe, "vx3" if o == 0 else "y03")
                    for m in range(NT):
                        b = V.bank(f"u{o}{m}")
                        for im, w in enumerate((cosm, sin_f if m == 0 else sinm)):
                            col = 0 if im and m == 0 else m * P
                            for kt in range(NT):
                                last = mm(b[:, im * CH:(im + 1) * CH], w[:, kt, col:col + P], vx_tok[:, kt, 0:CH],
                                          kt == 0, kt == NT - 1)
                        last.then_inc(ready_v, 1)
                    if o == 0:
                        for t in range(NT):
                            b = V.bank(f"y{o}{t}")
                            for kt in range(NT):
                                if t == 0:
                                    pe.wait_ge(y_ready, kt + 1)
                                mm(b[:, 0:CH], cosm[:, kt, t * P:(t + 1) * P], yre[:, kt, :], kt == 0, False)
                                w = sin_i[:, t * P:(t + 1) * P] if kt == 0 else sinm[:, kt, t * P:(t + 1) * P]
                                last = mm(b[:, 0:CH], w, yim[:, kt, :], False, kt == NT - 1)
                            last.then_inc(ready_v, 1)
                    else:
                        for c in range(2):
                            b = V.bank(f"y{o}{c}")
                            for kt in range(NT):
                                if c == 0:
                                    pe.wait_ge(y_ready, NT + kt + 1)
                                mm(b[:, :], yre[:, kt, c * P:(c + 1) * P], cosm[:, kt, :], kt == 0, False)
                                w = sin_i if kt == 0 else sinm[:, kt, :]
                                last = mm(b[:, :], yim[:, kt, c * P:(c + 1) * P], w, False, kt == NT - 1)
                            last.then_inc(ready_v, 1)
                project("b")
                pe.wait_ge(cn_ready, 1)
                for j in range(3):
                    b = A.bank(f"ct{j}")
                    for t in range(NT):
                        last = nc.tensor.transpose(b[:, t * P:(t + 1) * P], cols_a[:, t, j * P:(j + 1) * P], ident[:, :])
                    last.then_inc(ready_a, 1)
                taken(pe, "ct2")
                pe.wait_ge(mla_w_in, 32)
                for t in range(NT):
                    b = A.bank(f"q{t}")
                    for j in range(2):
                        last = mm(b[:, 0:384], cT[:, j, t * P:(t + 1) * P], w_uq[:, j, :], j == 0, j == 1)
                    last.then_inc(ready_a, 1)
                    b = A.bank(f"kv{t}")
                    mm(b[:, :], cT[:, 2, t * P:(t + 1) * P], w_ukv).then_inc(ready_a, 1)
                project("c", range(2))
                pe.wait_ge(ktok_ready, 1)
                for h in range(NH):
                    b = A.bank(f"kTa{h}")
                    for t in range(NT):
                        last = nc.tensor.transpose(b[0:96, t * P:(t + 1) * P], k_tok[:, t, h, :], ident[:, :])
                    last.then_inc(ready_a, 1)
                project("c", range(2, NT))
                pe.wait_ge(qr_ready, NT)
                for h in range(NH):
                    b = A.bank(f"qTa{h}")
                    for t in range(NT):
                        last = nc.tensor.transpose(b[0:96, t * P:(t + 1) * P], q_tok[:, t, h * 96:(h + 1) * 96], ident[:, :])
                    last.then_inc(ready_a, 1)
                pe.wait_ge(ropeb_ready, NT)
                b = A.bank("kTb")
                for t in range(NT):
                    last = nc.tensor.transpose(b[:, t * P:(t + 1) * P], rope_b[:, t, 256:384], ident[:, :])
                last.then_inc(ready_a, 1)
                for h in range(NH):
                    b = A.bank(f"qTb{h}")
                    for t in range(NT):
                        last = nc.tensor.transpose(b[0:64, t * P:(t + 1) * P], rope_b[:, t, h * 64:(h + 1) * 64], ident[:, :])
                    last.then_inc(ready_a, 1)
                pe.wait_ge(ropec_ready, NT)
                for j in range(4):
                    b = A.bank(f"cT{j}")
                    for t in range(NT):
                        last = nc.tensor.transpose(b[:, t * P:(t + 1) * P], rope_c[:, t, j * P:(j + 1) * P], ident[:, :])
                    last.then_inc(ready_a, 1)

                taken(pe, "cT3")
                for what, n in steps:
                    if what == "S":
                        g, h, qt, m = maps[n]
                        q = slice(qt * P, (qt + 1) * P)
                        if g == "a":
                            mm(A.bank(f"S{n}")[:, :], qT_a[0:96, h, q], kT_a[0:96, h, :]).then_inc(ready_a, 1)
                        elif g == "c":
                            i = 2 * h + m
                            mm(A.bank(f"S{n}")[:, :], qT_c[:, i, q], kT_c[:, i // 4, :]).then_inc(ready_a, 1)
                        else:
                            lo, hi = band(qt)
                            keys = slice((qt - 1) * P + lo, (qt - 1) * P + hi)
                            mm(V.bank(f"S{n}")[:, lo:hi], qT_b[:, h, q], kT_b[:, keys]).then_inc(ready_v, 1)
                    elif what == "T":
                        g, h, qt, ms = outs[n]
                        if g == "a":
                            taken(pe, f"S{ms[0]}")
                        elif g == "b":
                            pe.wait_ge(prob_b, ms[0] - 15)
                        else:
                            pe.wait_ge(diff_ready, n - 2 * NH * NT + 1)
                        b = A.bank(f"T{n}")
                        nb = NT if g != "b" else (band(qt)[1] - band(qt)[0]) // P
                        for j in range(nb):
                            last = nc.tensor.transpose(b[:, j * P:(j + 1) * P], prob[:, ms[0] % 4, j * P:(j + 1) * P], ident[:, :])
                        last.then_inc(ready_a, 1)
                    elif what == "PV":
                        g, h, qt, ms = outs[n]
                        taken(pe, f"T{n}")
                        b = V.bank(f"O{n}")
                        if g == "b":
                            lo, hi = band(qt)
                            tiles = range((qt * P - P + lo) // P, (qt * P - P + hi) // P)
                        else:
                            tiles = range(NT)
                        for j, kt in enumerate(tiles):
                            v = {"a": kv_tok[:, kt, h * P:(h + 1) * P], "b": cols_b[:, kt, 384:512],
                                 "c": cols_c[:, kt, 512 + h // 2 * P:512 + (h // 2 + 1) * P]}[g]
                            last = mm(b[:, 0:P], probT[:, n % 2, j * P:(j + 1) * P], v, j == 0, j == len(tiles) - 1)
                        last.then_inc(ready_v, 1)
                    elif what == "P":
                        mod_parts_sum(n)
                    elif what == "M":
                        mod_sum(n)
                pe.wait_ge(mix_ready, 1)
                for j in range(6):
                    b = A.bank(f"xT{j}")
                    for t in range(NT):
                        last = nc.tensor.transpose(b[:, t * P:(t + 1) * P], mix_tok[:, t, j * P:(j + 1) * P], ident[:, :])
                    last.then_inc(ready_a, 1)
                taken(pe, "xT5")
                for half in range(2):
                    c = ("out", half)
                    chunk_wait(pe, c, l)
                    w = at(big, chunk_slot(c) * SLOT, KT, 512)
                    for t in range(NT):
                        b = V.bank(f"w{half}{t}")
                        for k in range(KT):
                            src = mixT[:, k, t * P:(t + 1) * P] if k < 6 else ydT[:, k - 6, t * P:(t + 1) * P]
                            last = mm(b[:, :], src, w[:, k, :], k == 0, k == KT - 1)
                        last.then_inc(ready_v, 1)
                        if half and t >= 2:
                            transpose_rows(NT + t - 2)
                transpose_rows(2 * NT - 2)
                transpose_rows(2 * NT - 1)

                taken(pe, f"hT{2 * NT - 1}1")
                pe.wait_ge(rw_in, 16 * 4)
                b = A.bank("lgT")
                for k in range(KT):
                    last = mm(b[0:36, :], r_w[:, k, :], hT[:, k, :], k == 0, k == KT - 1)
                last.then_inc(ready_a, 1)
                taken(pe, "lgT")
                b = V.bank("lg")
                for t in range(NT):
                    last = nc.tensor.transpose(b[:, t * 36:(t + 1) * 36], lgT[:, t * P:(t + 1) * P], ident[0:36, 0:36])
                last.then_inc(ready_v, 1)
                pe.wait_ge(m_ready, 1)
                ms = msum.rearrange("p t e -> p (t e)")
                b = V.bank("before")
                mm(b[:, 0:P], tri[:, :], ms)
                mm(b[:, P:2 * P], ones[:, :], ms).then_inc(ready_v, 1)
                pe.wait_ge(hot_ready, 1)
                b = V.bank("slots")
                for j, row_of_token in enumerate((lambda k, t: id_of[:, k, t], lambda k, t: (m1, m2)[k][:, t])):
                    for k in range(2):
                        for t in range(NT):
                            last = mm(b[0:CAP, j * NE:(j + 1) * NE], rank_is[:, k, t], row_of_token(k, t), k + t == 0, k + t == NT)
                last.then_inc(ready_v, 1)
                pe.wait_ge(code_ready, 1)
                b = V.bank("over")
                nc.tensor.transpose(b[0:1, 0:P], o_code[:, 0:1], ident[:, :]).then_inc(ready_v, 1)

                pe.wait_ge(taken_v, V.n)
                pe.wait_ge(taken_a, A.n)

                def x_transpose(b, count):
                    for k in range(KT):
                        rows = xg[0:CAP, b, :].rearrange("p (c k) -> p k c", k=KT)[:, k]
                        last = nc.tensor.transpose(bank[b][:, k * CAP:(k + 1) * CAP], rows, ident[0:CAP, 0:CAP])
                    return last

                def gate_up(b, s):
                    wg, wu, _ = expert_slot(s)
                    for k in range(KT):
                        xk = xT[:, b, k * CAP:(k + 1) * CAP]
                        mm(bank[2 + b][0:CAP, 0:F], xk, wg[:, k, :], k == 0, k == KT - 1)
                        last = mm(bank[2 + b][CAP:P, 0:F], xk, wu[:, k, :], k == 0, k == KT - 1)
                    return last

                def act_transpose(b):
                    for j in range(2):
                        rows = act_h[0:CAP, b, :].rearrange("p (f j) -> p j f", j=2)[:, j]
                        last = nc.tensor.transpose(bank[4 + b][:, j * CAP:(j + 1) * CAP], rows, ident[0:CAP, 0:CAP])
                    return last

                def down(b, s):
                    _, _, wd = expert_slot(s)
                    for j in range(2):
                        hk = act_T[:, b, j * CAP:(j + 1) * CAP]
                        mm(bank[6 + b][0:CAP, :], hk, wd[:, j, 0:512], j == 0, j == 1)
                        last = mm(bank[6 + b][CAP:P, :], hk, wd[:, j, 512:1024], j == 0, j == 1)
                    return last

                gathers = [NE // 2 * 16 * l, NE // 2 * 16 * l]

                def expert(i, s, more):
                    b = s % 2
                    pe.wait_ge(xt_ready, 4 * i + s + 1)
                    pe.wait_ge(slot_full[s], expert_full(s, i, l))
                    if not (isinstance(i, int) and i == 0 and s < 2):
                        pe.wait_ge(acth_ready, 4 * i + s - 1)
                    gate_up(b, s).then_inc(gu_done, 1)
                    if more:
                        nb = (s + 1) % 2
                        k = 2 * i + (s + 1) // 2
                        pe.wait_ge(gathered[nb], gathers[nb] + 16 * (k + 1))
                        if not (isinstance(i, int) and i == 0 and s < 1):
                            pe.wait_ge(xt_ready, 4 * i + s)
                        pe.sem_inc(waited, 1)
                        x_transpose(nb, k).then_inc(xt_done, 1)
                    pe.wait_ge(acth_ready, 4 * i + s + 1)
                    if not (isinstance(i, int) and i == 0 and s < 2):
                        pe.wait_ge(actT_ready, 4 * i + s - 1)
                    pe.sem_inc(waited, 1)
                    act_transpose(b).then_inc(at_done, 1)
                    pe.wait_ge(actT_ready, 4 * i + s + 1)
                    if not (isinstance(i, int) and i == 0 and s < 2):
                        pe.wait_ge(yg_lo, 4 * i + s - 1)
                        pe.wait_ge(yg_hi, 4 * i + s - 1)
                    down(b, s).then_inc(y_done, 1)

                pe.wait_ge(gathered[0], gathers[0] + 16)
                pe.sem_inc(waited, 1)
                x_transpose(0, 0).then_inc(xt_done, 1)
                for s in range(4):
                    expert(0, s, True)
                with pe.Fori(1, NE // 4 - 1) as i:
                    for s in range(4):
                        expert(i, s, True)
                for s in range(4):
                    expert(NE // 4 - 1, s, s < 3)

                pe.wait_ge(yg_lo, NE)
                pe.wait_ge(yg_hi, NE)
                n_over = pe.value_load(tot_i[0:1, 0:1], min_val=0, max_val=EXTRA)
                n_before = pe.value_load(tot_i[0:1, 1:2], min_val=0, max_val=EXTRA * DEPTH)
                with pe.If(n_over > 0):
                    with pe.Fori(0, EXTRA) as r:
                        with pe.If(r < n_over):
                            pe.wait_ge(over_gathered, (n_before + r + 1) * 16)
                            pe.sem_inc(waited, 1)
                            x_transpose(0, 0).then_inc(ov_xt, 1)
                            pe.wait_ge(ov_x, r + 1)
                            pe.wait_ge(ov_w, 48 * r + 48)
                            gate_up(0, 0).then_inc(ov_gu, 1)
                            pe.wait_ge(ov_act, r + 1)
                            pe.sem_inc(waited, 1)
                            act_transpose(0).then_inc(ov_at, 1)
                            pe.wait_ge(ov_aT, r + 1)
                            down(0, 0).then_inc(ov_y, 1)
                        with pe.Else():
                            pe.nop()
                with pe.Else():
                    pe.nop()
                pe.drain().then_inc(layer_done, 1)

            with pe.Fori(0, DEPTH) as l:
                layer(l)
                pe.wait_ge(layer_go, l + 1)

        @block.sync
        def _(sp):
            sp.dma_start(c_sb, a["c"].rearrange("b (p k) -> p (b k)", k=KT)).then_inc(first_load, 16)
            sp.dma_start(pos_i[:, :], a["positions"].rearrange("b (t p) -> p (b t)", p=P)).then_inc(first_load, 16)
            sp.dma_start(ident[:, :], a["k_ident"]).then_inc(first_load, 16)
            sp.dma_start(tri[:, :], a["k_tri"]).then_inc(first_load, 16)
            sp.dma_start(mask[:, :], a["k_mask"]).then_inc(first_load, 16)
            sp.dma_start(invf, row(a["k_inv"])).then_inc(first_load, 16)
            sp.dma_start(misc[:, :], row(a["k_misc"])).then_inc(first_load, 16)

            def load_chunk(n, l):
                kind, which = CHUNKS[n]
                s = n % 2
                if kind == "ada":
                    src = of_layer("ada_w", l)[:, which * ADA:(which + 1) * ADA]
                elif kind == "in":
                    lo, m = col0[which]
                    src = of_layer("w_in", l)[:, lo:lo + m]
                if kind == "out":
                    src = of_layer("w_out", l)[:, which * 512:(which + 1) * 512]
                    sp.dma_start(slot(s, 12, 512)[:, 0:KT], src.rearrange("(k p) n -> p k n", p=P)).then_inc(slot_full[s], 16)
                else:
                    m = src.shape[1]
                    sp.dma_start(at(big, s * SLOT, KT, m), src.rearrange("(p k) n -> p k n", k=KT)).then_inc(slot_full[s], 16)

            sp.wait_ge(hy_in, 16 * 11)
            load_chunk(0, 0)
            sp.dma_start(x_tok[:, :, :], a["x"].rearrange("b (t p) d -> p (b t) d", p=P)).then_inc(x_in, 16)
            load_chunk(1, 0)
            with sp.Fori(0, DEPTH) as l:
                for n in range(2, len(CHUNKS)):
                    chunk_used(sp, CHUNKS[n - 2])
                    load_chunk(n, l)

                def load_expert(i, s):
                    wg, wu, wd = expert_slot(s)
                    e = l * NE + 4 * i + s
                    sp.dma_start(wg, a["moe_w_gate"].rearrange("l e d f -> (l e) d f")[bass.ds(e, 1)].rearrange(
                        "a (p k) f -> (a p) k f", k=KT)).then_inc(slot_full[s], 16)
                    sp.dma_start(wu, a["moe_w_up"].rearrange("l e d f -> (l e) d f")[bass.ds(e, 1)].rearrange(
                        "a (p k) f -> (a p) k f", k=KT)).then_inc(slot_full[s], 16)
                    sp.dma_start(wd, a["moe_w_down"].rearrange("l e f d -> (l e) f d")[bass.ds(e, 1)].rearrange(
                        "a (p j) d -> (a p) j d", j=2)).then_inc(slot_full[s], 16)

                for s in (2, 3, 0, 1):
                    if s < 2:
                        chunk_used(sp, CHUNKS[-2 + s])
                    else:
                        done(sp, f"O{len(outs) - 1}")
                    load_expert(0, s)
                with sp.Fori(1, NE // 4) as i:
                    for s in range(4):
                        sp.wait_ge(y_done, 4 * i + s - 3)
                        load_expert(i, s)

                taken(sp, "over")
                n_over = sp.value_load(tot_i[0:1, 0:1], min_val=0, max_val=EXTRA)
                n_before = sp.value_load(tot_i[0:1, 1:2], min_val=0, max_val=EXTRA * DEPTH)
                table = slots_of.rearrange("(r e) o -> r (e o)", e=NE)
                sp.wait_ge(table_dma, 16 * 2 * NT * (l + 1))
                sp.sem_inc(waited, 1)
                with sp.If(n_over > 0):
                    with sp.Fori(0, EXTRA) as r:
                        with sp.If(r < n_over):
                            code = sp.value_load(over_i[0:1, bass.ds(r, 1)], min_val=1, max_val=8 * NE - 1)
                            e = sp.snap(code // 8, min_val=0, max_val=NE - 1)
                            j = sp.snap(code % 8, min_val=0, max_val=7)
                            ee = sp.snap(l * NE + e, min_val=0, max_val=DEPTH * NE - 1)
                            wg, wu, wd = expert_slot(0)
                            sp.wait_ge(ov_yv, r + 1)
                            sp.dma_start(wg, a["moe_w_gate"].rearrange("l e d f -> (l e) d f")[bass.ds(ee, 1)].rearrange(
                                "a (p k) f -> (a p) k f", k=KT)).then_inc(ov_w, 16)
                            sp.dma_start(wu, a["moe_w_up"].rearrange("l e d f -> (l e) d f")[bass.ds(ee, 1)].rearrange(
                                "a (p k) f -> (a p) k f", k=KT)).then_inc(ov_w, 16)
                            sp.dma_start(wd, a["moe_w_down"].rearrange("l e f d -> (l e) f d")[bass.ds(ee, 1)].rearrange(
                                "a (p j) d -> (a p) j d", j=2)).then_inc(ov_w, 16)
                            sp.dma_start(o_idx[0:CAP, 0:1], table[bass.ds(j * CAP, CAP), bass.ds(e, 1)]).then_inc(ov_i, 16)
                        with sp.Else():
                            sp.nop()
                with sp.Else():
                    sp.nop()

                sp.wait_ge(moe_done, 1)
                for t in range(NT):
                    sp.dma_start(pair[:, t], pair_rows.rearrange("(k t p) d -> t p k d", t=NT, p=P)[t]).then_inc(pair_in[t], 16)
                with sp.If(l < DEPTH - 1):
                    after = sp.snap((l + 1) % DEPTH, min_val=0, max_val=DEPTH - 1)
                    sp.wait_ge(hy_in, 16 * 11 * (l + 2))
                    load_chunk(0, after)
                    load_chunk(1, after)
                with sp.Else():
                    sp.nop()

                sp.wait_ge(layer_done, 4 * l + 4)
                sp.sem_inc(waited, 1)
                for s in layer_sems:
                    sp.sem_clear(s)
                sp.sem_inc(layer_go, 1)

            for t in range(NT):
                sp.wait_ge(fin_row, t + 1)
                sp.dma_start(out[0, t * P:(t + 1) * P, :], h_tok[:, t % 2, :]).then_inc(out_row[t % 2], 16)
            for i in range(2):
                sp.wait_ge(out_row[i], 16 * NT // 2)

        @block.scalar
        def _(act):
            A_ = nc.scalar.activation
            d = act.dma_start

            def load_filters(l):
                for w, name in ((hw1, "hy_w1"), (hw2, "hy_w2"), (hw3, "hy_w3")):
                    d(w, of_layer(name, l)).then_inc(hy_in, 16)
                for j, name in enumerate(("hy_b1", "hy_b2", "hy_b3")):
                    d(hb[:, j:j + 1], row_of(name, l).rearrange("a n -> n a")).then_inc(hy_in, 16)
                d(hf, of_layer("hy_sin_freq", l).rearrange("j n -> n j")).then_inc(hy_in, 16)
                d(zT, a["k_z"]).then_inc(hy_in, 16)
                d(w4, of_layer("hy_w4", l)).then_inc(hy_in, 16)
                d(window, a["k_window"].rearrange("(t p) c -> p t c", p=P)).then_inc(hy_in, 16)
                d(bias_b, a["hy_bias"].rearrange("l o c -> l (o c)")[bass.ds(l, 1)].broadcast_to([P, S])).then_inc(hy_in, 16)

            def load_vectors(l):
                d(lv, a["diff_lambda"].rearrange("l j n -> l (j n)")[bass.ds(l, 1)].broadcast_to([P, P])).then_inc(vec_in, 16)
                for j in range(3):
                    d(conv_w[:, 6 * j:6 * j + 6], of_layer("hy_conv_w", l)[j:j + 1].rearrange("a (c p) -> p (a c)", p=P)).then_inc(vec_in, 16)
                d(conv_b, row_of("hy_conv_b", l).rearrange("a (c p) -> p (a c)", p=P)).then_inc(vec_in, 16)
                d(gd, row_of("diff_norm_g", l).broadcast_to([P, 64])).then_inc(vec_in, 16)
                d(gn[:, 0:2], row_of("mla_q_norm", l).rearrange("a (j p) -> p (a j)", p=P)).then_inc(vec_in, 16)
                d(gn[:, 2:3], row_of("mla_kv_norm", l).rearrange("a (j p) -> p (a j)", p=P)).then_inc(vec_in, 16)
                d(sink, row_of("swa_sink", l).broadcast_to([P, NH])).then_inc(vec_in, 16)
                d(lam_b, a["k_lam"][bass.ds(l, 1)].broadcast_to([P, 2])).then_inc(vec_in, 16)
                d(r_b[0:NG, :], row_of("router_g_b", l).rearrange("a n -> n a")).then_inc(vec_in, 16)
                d(r_b[NG:36, :], row_of("router_e_b", l).rearrange("a n -> n a")).then_inc(vec_in, 16)

            load_filters(0)
            act.wait_ge(first_load, 16 * 7)
            A_(c_act, c_sb, ACT.Silu).then_inc(c_ready, 1)
            act.wait_ge(ang_ready, 1)
            ang = at(mix_r, 0, NT, 48)
            half = at(mix_r, 192, NT, 48)
            A_(at(mix_r, 384, NT, 48), ang, ACT.Sin)
            A_(half, ang, ACT.Sin, scale=0.5).then_inc(sines_ready, 1)
            act.wait_ge(c_ready, 1)
            load_vectors(0)
            act.wait_ge(tables_ready, 1)

            def layer(l):
                step = Steps(act, a_step)
                R = Reader(act, 4, ready_a)
                d = act.dma_start
                bias = row_of("ada_b", l)
                for j, dst in enumerate((sh1, gsc1, mod[:, 0, :], mod[:, 1, :], mod[:, 2, :], mod[:, 3, :])):
                    d(dst, bias[:, j * D:(j + 1) * D].broadcast_to([P, D])).then_inc(mod_in, 16)
                d(ln1, row_of("ln1_g", l).broadcast_to([P, D])).then_inc(mod_in, 16)
                d(cosm, a["k_cos"].rearrange("(t p) k -> p t k", p=P)).then_inc(dft_in, 16)
                d(sinm, a["k_sin"].rearrange("(t p) k -> p t k", p=P)).then_inc(dft_in, 16)
                d(sin_f, a["k_sin_f"].rearrange("(t p) k -> p t k", p=P)).then_inc(dft_in, 16)
                d(sin_i, a["k_sin_i"]).then_inc(dft_in, 16)
                d(slots_of.rearrange("(p n) o -> p (n o)", p=P), a["k_empty"]).then_inc(fill_in, 16)

                def part_evac(c):
                    for half, (lo, n) in enumerate(((0, 512), (512, 256))):
                        b = R.take(f"p{c}{half}")
                        if c:
                            done(act, f"m{c - 1}{half}")
                        A_(part[:, lo:lo + n], b[:, 0:n], ACT.Copy).then_inc(taken_a, 1)

                for j in range(3):
                    if j < 2:
                        part_evac(j)
                    act.wait_ge(sin_in, j + 1)
                    A_(mlp_h, mlp_y, ACT.Sin).then_inc(mlp_ready, 1)
                for t in range(NT):
                    act.wait_ge(filt_ready, t + 1)
                    A_(sq_sum[:, t], fsum[:, t], ACT.Square)
                    last = A_(sq_dif[:, t], fdif[:, t], ACT.Square)
                    if t == 0:
                        step(last)
                        last = A_(sq_dif[0:1, 0], sq_sum[0:1, 0], ACT.Copy)
                    last.then_inc(sq_ready, 1)
                b = R.take("fp")
                A_(f_tmp, b[:, :], ACT.Copy).then_inc(taken_a, 1)
                part_evac(2)
                act.wait_ge(x_in, 16)
                for t in range(NT):
                    if t:
                        act.wait_ge(nss_ready, t)
                    A_(ydT[:, :, :].rearrange("p c s -> p (c s)"), x_tok[:, t, :], ACT.Square,
                       accum_out=nss[:, t:t + 1]).then_inc(nss_ready, 1)
                act.wait_ge(lam_pre, 1)
                A_(lexp, lred, ACT.Exp).then_inc(lam_exp, 1)

                def evac(n):
                    t = n % NT
                    for half in range(2):
                        b = R.take(f"hT{n}{half}")
                        A_(hT[:, 4 * half:4 * half + 4, t * P:(t + 1) * P], b[:, :].rearrange("p (k c) -> p k c", k=4),
                           ACT.Copy).then_inc(taken_a, 1)
                    if n >= NT:
                        act.dma_start(h2_rows[t * P:(t + 1) * P, :], h2_tok[:, t, :]).then_inc(h2_stored[t % 2], 16)

                taken(act, "fd3")
                for t in range(NT):
                    evac(t)

                act.wait_ge(vec_in, 16 * 12 * (l + 1))
                for m in range(6):
                    done(act, f"d{m}")
                    dst = vxT[:, m, :] if m < 4 else ydT[:, m - 4, :]
                    A_(dst, bank[number[f"d{m}"][1] % 4][:, :], ACT.Identity, bias=conv_b[:, m:m + 1],
                       scale=conv_w[:, 6 + m:7 + m]).then_inc(conv_mid, 1)
                for t in range(NT):
                    b = R.take(f"a{t}0")
                    A_(cols_a[:, t, :], b[:, 0:A_COLS], ACT.Copy).then_inc(taken_a, 1)
                    taken(act, f"a{t}0")
                    A_(rp_sq[:, 0:256], cols_a[:, t, 0:256], ACT.Square, accum_out=css[:, 2 * t:2 * t + 1])
                    A_(rp_sq[:, 256:384], cols_a[:, t, 256:384], ACT.Square, accum_out=css[:, 2 * t + 1:2 * t + 2]).then_inc(css_ready, 1)
                for t in range(NT):
                    b = R.take(f"vx{t}")
                    A_(vx_tok[:, t, :], b[:, :], ACT.Copy).then_inc(taken_a, 1)
                done(act, "y11")
                d(w_uq, of_layer("mla_w_uq", l).rearrange("(j p) n -> p j n", p=P)).then_inc(mla_w_in, 16)
                d(w_ukv, of_layer("mla_w_ukv", l)).then_inc(mla_w_in, 16)
                for t in range(NT):
                    b = R.take(f"b{t}0")
                    A_(cols_b[:, t, :], b[:, :], ACT.Copy).then_inc(taken_a, 1)
                for j in range(3):
                    b = R.take(f"ct{j}")
                    A_(cT[:, j, :], b[:, :], ACT.Copy, scale=gn[:, j:j + 1]).then_inc(taken_a, 1)
                for t in range(NT):
                    b = R.take(f"q{t}")
                    A_(q_tok[:, t, :], b[:, 0:384], ACT.Copy).then_inc(taken_a, 1)
                    b = R.take(f"kv{t}")
                    A_(kv_tok[:, t, :], b[:, :], ACT.Copy).then_inc(taken_a, 1)

                def cols_c_copy(t):
                    b = R.take(f"c{t}0")
                    A_(cols_c[:, t, 0:512], b[:, :], ACT.Copy).then_inc(taken_a, 1)
                    b = R.take(f"c{t}512")
                    A_(cols_c[:, t, 512:768], b[:, 0:256], ACT.Copy).then_inc(taken_a, 1)

                cols_c_copy(0)
                cols_c_copy(1)
                for h in range(NH):
                    b = R.take(f"kTa{h}")
                    A_(kT_a[0:96, h, :], b[0:96, :], ACT.Copy).then_inc(taken_a, 1)
                cols_c_copy(2)
                cols_c_copy(3)
                for h in range(NH):
                    b = R.take(f"qTa{h}")
                    A_(qT_a[0:96, h, :], b[0:96, :], ACT.Copy, scale=MLA_SCALE).then_inc(taken_a, 1)
                act.wait_ge(padded, 2)
                b = R.take("kTb")
                A_(kT_b, b[:, :], ACT.Copy).then_inc(taken_a, 1)
                for h in range(NH):
                    b = R.take(f"qTb{h}")
                    g = h // 2
                    A_(qT_b[64 * g:64 * g + 64, h, :], b[0:64, :], ACT.Copy).then_inc(taken_a, 1)
                for j in range(2):
                    b = R.take(f"cT{j}")
                    for i in range(4):
                        last = A_(qT_c[32 * i:32 * i + 32, 4 * j + i, :], b[32 * i:32 * i + 32, :], ACT.Copy,
                                  scale=DIFF_SCALE)
                    last.then_inc(taken_a, 1)
                for j in range(2):
                    b = R.take(f"cT{2 + j}")
                    A_(kT_c[:, j, :], b[:, :], ACT.Copy).then_inc(taken_a, 1)

                for what, n in steps:
                    if what == "S":
                        g, h, qt, m = maps[n]
                        if n >= 4:
                            done(act, f"T{out_of[n - 4]}")
                        if g == "b":
                            w = band(qt)[1] - band(qt)[0]
                            act.wait_ge(swa_s, n - 16 + 1)
                            pr = prob[:, n % 4, 0:w]
                            A_(pr, pr, ACT.Exp, bias=nm[:, n:n + 1], accum_out=rs[:, n:n + 1])
                            A_(esink[:, n - 16:n - 15], sink[:, h:h + 1], ACT.Exp, bias=nm[:, n:n + 1]).then_inc(prob_b, 1)
                        else:
                            b = R.take(f"S{n}")
                            act.wait_ge(nm_ready, n + 1 if g == "a" else n - 16 + 1)
                            A_(prob[:, n % 4, :], b[:, :], ACT.Exp, bias=nm[:, n:n + 1],
                               accum_out=rs[:, n:n + 1]).then_inc(taken_a, 1)
                    elif what == "T":
                        g, h, qt, ms = outs[n]
                        w = S if g != "b" else band(qt)[1] - band(qt)[0]
                        b = R.take(f"T{n}")
                        if n >= 2:
                            done(act, f"O{n - 2}")
                        A_(probT[:, n % 2, 0:w], b[:, 0:w], ACT.Copy).then_inc(taken_a, 1)
                    elif what == "P":
                        part_evac(n)
                for j in range(6):
                    b = R.take(f"xT{j}")
                    A_(mixT[:, j, :], b[:, :], ACT.Copy).then_inc(taken_a, 1)
                done(act, f"O{len(outs) - 1}")
                d(ln2, row_of("ln2_g", l).broadcast_to([P, D])).then_inc(ln2_in, 16)
                d(r_w[:, :, 0:NG], of_layer("router_g_w", l).rearrange("(p k) g -> p k g", k=KT)).then_inc(rw_in, 16)
                d(r_w[:, :, NG:36], of_layer("router_e_w", l).rearrange("(p k) g -> p k g", k=KT)).then_inc(rw_in, 16)
                d(block_id, a["k_blocks"][0:1, :].broadcast_to([P, NE * 7])).then_inc(rw_in, 16)
                d(block_at, a["k_blocks"][1:2, :].broadcast_to([P, NE * 7])).then_inc(rw_in, 16)
                for t in range(NT):
                    act.wait_ge(x_ready, t + 1)
                    A_(h2_tok[:, t, :], x_tok[:, t, :], ACT.Square, accum_out=nss[:, t:t + 1]).then_inc(nss_ready, 1)
                    if t >= 2:
                        evac(NT + t - 2)
                evac(2 * NT - 2)
                evac(2 * NT - 1)
                b = R.take("lgT")
                A_(lgT, b[0:36, :], ACT.Identity, bias=r_b).then_inc(taken_a, 1)
                act.wait_ge(e_in, 1)
                A_(rd, rd, ACT.Exp).then_inc(e_out, 1)
                act.wait_ge(e_in, 2)
                A_(vd, vd, ACT.Exp).then_inc(e_out, 1)

                def x_evac(b):
                    return A_(xT[:, b, :], bank[b][:, :], ACT.Copy)

                def y_evac(b):
                    return A_(yg[0:CAP, b, 0:512], bank[6 + b][0:CAP, :], ACT.Copy)

                def expert(i, s, more):
                    b = s % 2
                    pre = isinstance(i, int) and i == 0 and s < 2
                    act.wait_ge(gu_done, 4 * i + s + 1)
                    if not pre:
                        act.wait_ge(acth_ready, 4 * i + s - 1)
                    A_(sil[0:CAP, b, :], bank[2 + b][0:CAP, 0:F], ACT.Silu).then_inc(silu_ready, 1)
                    if more:
                        act.wait_ge(xt_done, 4 * i + s + 2)
                        x_evac((s + 1) % 2).then_inc(xt_ready, 1)
                    act.wait_ge(y_done, 4 * i + s + 1)
                    if not pre:
                        act.wait_ge(scattered[b], NE // 2 * 16 * l + 16 * (2 * i + s // 2))
                    y_evac(b).then_inc(yg_lo, 1)

                act.wait_ge(xt_done, 1)
                x_evac(0).then_inc(xt_ready, 1)
                for s in range(4):
                    expert(0, s, True)
                with act.Fori(1, NE // 4 - 1) as i:
                    for s in range(4):
                        expert(i, s, True)
                for s in range(4):
                    expert(NE // 4 - 1, s, s < 3)

                n_over = act.value_load(tot_i[0:1, 0:1], min_val=0, max_val=EXTRA)
                with act.If(n_over > 0):
                    with act.Fori(0, EXTRA) as r:
                        with act.If(r < n_over):
                            act.wait_ge(ov_xt, r + 1)
                            x_evac(0).then_inc(ov_x, 1)
                            act.wait_ge(ov_gu, r + 1)
                            A_(sil[0:CAP, 0, :], bank[2][0:CAP, 0:F], ACT.Silu).then_inc(ov_sil, 1)
                            act.wait_ge(ov_y, r + 1)
                            y_evac(0).then_inc(ov_ya, 1)
                        with act.Else():
                            act.nop()
                with act.Else():
                    act.nop()
                act.wait_ge(moe_done, 1)
                with act.If(l < DEPTH - 1):
                    after = act.snap((l + 1) % DEPTH, min_val=0, max_val=DEPTH - 1)
                    load_filters(after)
                with act.Else():
                    act.nop()
                for t in range(NT):
                    act.wait_ge(pair_in[t], 16)
                    A_(pair[:, t, 0], pair[:, t, 0], ACT.Copy, scale=wgt[:, 0, t:t + 1]).then_inc(gated, 1)
                with act.If(l < DEPTH - 1):
                    load_vectors(after)
                with act.Else():
                    act.nop()
                act.drain().then_inc(layer_done, 1)

            rp_sq = at(pr_r, 1536, 384)
            with act.Fori(0, DEPTH) as l:
                layer(l)
                act.wait_ge(layer_go, l + 1)
            act.dma_start(gsc1, a["final_g"].rearrange("(a d) -> a d", a=1).broadcast_to([P, D])).then_inc(final_in, 16)
            for t in range(NT):
                if t >= 2:
                    act.wait_ge(out_row[t % 2], 16 * (t // 2))
                A_(h_tok[:, t % 2, :], x_tok[:, t, :], ACT.Square, accum_out=nss[:, t:t + 1]).then_inc(fin_sq, 1)

        @block.gpsimd
        def _(g):
            g.iota(tok_id, [[P, 2 * NT]], base=0, channel_multiplier=1, allow_small_or_imprecise_dtypes=True)
            g.iota(part_id, [[0, 1]], base=1, channel_multiplier=1, allow_small_or_imprecise_dtypes=True)
            g.memset(neghalf, -0.5)
            g.memset(over_tot, 0.0).then_inc(iota_ready, 1)
            g.wait_ge(iota_ready, 1)
            g.wait_ge(c_ready, 1)
            g.tensor_scalar(c_act, c_act, 1.0 / 32, None, ALU.mult).then_inc(c_ready, 1)
            g.wait_ge(c_ready, 2)
            g.tensor_copy(c_rep[:, :, :], c_act.unsqueeze(2).to_broadcast([P, KT, 32])).then_inc(rep_ready, 1)

            def layer(l):
                step = Steps(g, g_step)

                def rstd(dst, src, inv_n, mul=1.0):
                    step(g.tensor_scalar(dst, src, inv_n, EPS, ALU.mult, ALU.add))
                    last = g.tensor_tensor(dst, dst, neghalf.to_broadcast(dst.shape), ALU.pow)
                    if mul != 1.0:
                        step(last)
                        last = g.tensor_scalar(dst, dst, mul, None, ALU.mult)
                    return last

                taken(g, "fn")
                rstd(f_s, f_s, 0.5 / 32, 2.0 / (2 * S)).then_inc(fscale, 1)
                for t in range(NT):
                    g.wait_ge(nss_ready, t + 1)
                    rstd(nrs[:, t:t + 1], nss[:, t:t + 1], 1.0 / D).then_inc(nrs_ready, 1)
                for o in range(2):
                    for m in range(NT):
                        n = o * NT + m
                        taken(g, f"u{o}{m}")
                        g.tensor_tensor(yre[:, m, :], cm[:, m % 2, 0, 0:CH], cm[:, m % 2, 1, CH:S], ALU.subtract)
                        g.tensor_tensor(yim[:, m, :], cm[:, m % 2, 1, 0:CH], cm[:, m % 2, 0, CH:S], ALU.add).then_inc(y_ready, 1)
                    if o == 0:
                        g.wait_ge(css_ready, NT)
                        step(g.tensor_scalar(crs.rearrange("p (t j) -> p j t", j=2)[:, 0], css.rearrange("p (t j) -> p j t", j=2)[:, 0],
                                             1.0 / 256, EPS, ALU.mult, ALU.add))
                        step(g.tensor_scalar(crs.rearrange("p (t j) -> p j t", j=2)[:, 1], css.rearrange("p (t j) -> p j t", j=2)[:, 1],
                                             1.0 / 128, EPS, ALU.mult, ALU.add))
                        g.tensor_tensor(crs, crs, neghalf.to_broadcast(crs.shape), ALU.pow).then_inc(crs_ready, 1)
                done(g, "y11")
                g.memset(qT_b, 0.0).then_inc(padded, 1)

                taken(g, "kv3")
                g.wait_ge(kpe_ready, NT)
                for t in range(NT):
                    g.tensor_copy(k_tok[:, t, :, 0:64], kv_tok[:, t, :].rearrange("p (h c) -> p h c", h=NH)[:, :, 0:64])
                    last = g.tensor_copy(k_tok[:, t, :, 64:96], cols_a[:, t, 384:416].unsqueeze(1).to_broadcast([P, NH, 32]))
                last.then_inc(ktok_ready, 1)
                done(g, "c3512")
                g.memset(qT_c, 0.0).then_inc(padded, 1)
                g.wait_ge(dss_ready, 1)
                rstd(drs, dss, 1.0 / 64).then_inc(drs_ready, 1)
                for t in range(NT):
                    g.wait_ge(nss_ready, NT + t + 1)
                    rstd(nrs[:, t:t + 1], nss[:, t:t + 1], 1.0 / D).then_inc(nrs_ready, 1)

                def table_rows(k):
                    for t in range(NT):
                        n = k * NT + t
                        g.indirect_dma_start(out=slots_of, out_offset=bass.IndirectOffsetOnAxis(ap=dest_i[:, k, t:t + 1], axis=0),
                                             in_=tok_id[:, n:n + 1], in_offset=None, bounds_check=S * NE - 1,
                                             oob_is_err=False).then_inc(table_dma, 16)

                g.wait_ge(slots_ready, 1)
                g.wait_ge(h2_stored[0], 32)
                g.wait_ge(h2_stored[1], 32)

                def gather(i, s):
                    b = s % 2
                    e = 4 * i + s
                    if not (isinstance(i, int) and i == 0 and s < 2):
                        g.wait_ge(xt_done, e - 1)
                    g.sem_inc(waited, 1)
                    g.tensor_copy(gather_i[0:CAP, b:b + 1], gslot_i[0:CAP, bass.ds(e, 1)]).then_inc(gidx_ready, 1)
                    g.wait_ge(gidx_ready, NE * l + e + 1)
                    g.sem_inc(waited, 1)
                    g.indirect_dma_start(out=xg[0:CAP, b, :], out_offset=None, in_=h2_rows,
                                         in_offset=bass.IndirectOffsetOnAxis(ap=gather_i[0:CAP, b:b + 1], axis=0),
                                         bounds_check=S - 1, oob_is_err=False).then_inc(gathered[b], 16)

                def scatter(i, s):
                    b = s % 2
                    e = 4 * i + s
                    if not (isinstance(i, int) and i == 0 and s < 2):
                        g.wait_ge(scattered[b], NE // 2 * 16 * l + 16 * (2 * i + s // 2))
                    g.sem_inc(waited, 1)
                    g.tensor_copy(scatter_i[0:CAP, b:b + 1], slot_i[0:CAP, bass.ds(e, 1)]).then_inc(sidx_ready, 1)
                    g.wait_ge(sidx_ready, NE * l + e + 1)
                    g.wait_ge(yg_lo, e + 1)
                    g.wait_ge(yg_hi, e + 1)
                    g.sem_inc(waited, 1)
                    g.indirect_dma_start(out=pair_rows, out_offset=bass.IndirectOffsetOnAxis(ap=scatter_i[0:CAP, b:b + 1], axis=0),
                                         in_=yg[0:CAP, b, :], in_offset=None, bounds_check=2 * S - 1,
                                         oob_is_err=False).then_inc(scattered[b], 16)

                gather(0, 0)
                gather(0, 1)

                def expert(i, s, more):
                    if more:
                        gather(i + (s + 2) // 4, (s + 2) % 4)
                    scatter(i, s)

                g.wait_ge(dest_ready, 1)
                g.wait_ge(fill_in, 16)
                for s in range(4):
                    expert(0, s, True)
                    if s in (1, 2):
                        table_rows(s - 1)
                with g.Fori(1, NE // 4 - 1) as i:
                    for s in range(4):
                        expert(i, s, True)
                for s in range(4):
                    expert(NE // 4 - 1, s, s < 2)
                for b in range(2):
                    g.wait_ge(scattered[b], NE // 2 * 16 * l + NE // 2 * 16)
                g.sem_inc(waited, 1)

                n_over = g.value_load(tot_i[0:1, 0:1], min_val=0, max_val=EXTRA)
                n_before = g.value_load(tot_i[0:1, 1:2], min_val=0, max_val=EXTRA * DEPTH)
                g.drain().then_inc(ov_done, 1)
                with g.If(n_over > 0):
                    with g.Fori(0, EXTRA) as r:
                        with g.If(r < n_over):
                            g.wait_ge(ov_i2, r + 1)
                            g.sem_inc(waited, 1)
                            g.indirect_dma_start(out=xg[0:CAP, 0, :], out_offset=None, in_=h2_rows,
                                                 in_offset=bass.IndirectOffsetOnAxis(ap=gather_i[0:CAP, 0:1], axis=0),
                                                 bounds_check=S - 1, oob_is_err=False).then_inc(over_gathered, 16)
                            g.wait_ge(ov_ya, r + 1)
                            g.wait_ge(ov_yv, r + 2)
                            g.sem_inc(waited, 1)
                            g.indirect_dma_start(out=pair_rows, out_offset=bass.IndirectOffsetOnAxis(ap=scatter_i[0:CAP, 0:1], axis=0),
                                                 in_=yg[0:CAP, 0, :], in_offset=None, bounds_check=2 * S - 1,
                                                 oob_is_err=False).then_inc(over_scattered, 16)
                            g.wait_ge(over_scattered, (n_before + r + 1) * 16)
                            g.sem_inc(waited, 1)
                            g.drain().then_inc(ov_done, 1)
                        with g.Else():
                            g.nop()
                with g.Else():
                    g.nop()
                g.drain().then_inc(moe_done, 1)
                for t in range(NT):
                    g.wait_ge(summed, t + 1)
                    g.tensor_tensor(comb[:, t % 2], comb[:, t % 2], mod[:, 3, :], ALU.mult).then_inc(scaled, 1)
                g.drain().then_inc(layer_done, 1)

            with g.Fori(0, DEPTH) as l:
                layer(l)
                g.wait_ge(layer_go, l + 1)
            for t in range(NT):
                g.wait_ge(fin_sq, t + 1)
                g.tensor_scalar(nrs[:, t:t + 1], nss[:, t:t + 1], 1.0 / D, EPS, ALU.mult, ALU.add).then_inc(fin_mid, 1)
                g.wait_ge(fin_mid, t + 1)
                g.tensor_tensor(nrs[:, t:t + 1], nrs[:, t:t + 1], neghalf, ALU.pow).then_inc(fin_rs, 1)

        @block.vector
        def _(v):
            TS, TT, STT = nc.vector.tensor_scalar, nc.vector.tensor_tensor, nc.vector.scalar_tensor_tensor
            INV2PI = 1.0 / (2 * math.pi)
            C1 = 6.28125
            C2 = float(np.float32(round((2 * math.pi - C1) * 2 ** 21)) / 2 ** 21)
            C3 = float(np.float32(2 * math.pi - C1 - C2))
            PI = 3.1415925

            def reduce_angle(step, y, k):
                step(TS(k, y, INV2PI, MAGIC, ALU.mult, ALU.add))
                step(TS(k, k, MAGIC, None, ALU.subtract))
                for c in (C1, C2, C3):
                    step(STT(out=y, in0=k, scalar=-c, in1=y, op0=ALU.mult, op1=ALU.add))
                return TS(y, y, PI, -PI, ALU.min, ALU.max)

            nc.vector.memset(ones[:, :], 1.0).then_inc(ones_set, 1)
            v.wait_ge(first_load, 16 * 7)
            setup = Steps(v, rope_ready)
            setup(nc.vector.tensor_copy(pos_f, pos_i[:, :]))
            ang, turns = at(mix_r, 0, NT, 48), at(mix_r, 192, NT, 48)
            for t in range(NT):
                setup(TS(ang[:, t, :], invf, pos_f[:, t:t + 1], None, ALU.mult))
            reduce_angle(setup, at(mix_r, 0, NT * 48), at(mix_r, 192, NT * 48)).then_inc(ang_ready, 1)
            v.wait_ge(sines_ready, 1)
            sines, halves = at(mix_r, 384, NT, 48), at(mix_r, 192, NT, 48)
            setup(TT(halves, halves, halves, ALU.mult))
            setup(TS(rope_t[:, :, 0:16], halves[:, :, 0:16], -2.0, 1.0, ALU.mult, ALU.add))
            setup(nc.vector.tensor_copy(rope_t[:, :, 16:32], sines[:, :, 0:16]))
            setup(TS(rope_t[:, :, 32:64], halves[:, :, 16:48], -2.0, 1.0, ALU.mult, ALU.add))
            nc.vector.tensor_copy(rope_t[:, :, 64:96], sines[:, :, 16:48]).then_inc(tables_ready, 1)
            v.wait_ge(tables_ready, 1)
            v.wait_ge(iota_ready, 1)

            def layer(l):
                step = Steps(v, v_step)
                V = Reader(v, 0, ready_v)

                def took(ins):
                    ins.then_inc(taken_v, 1)
                    v.wait_ge(taken_v, V.n)

                dest = {0: sh1, 1: gsc1, 2: mod[:, 0, :], 3: mod[:, 1, :], 4: mod[:, 2, :], 5: mod[:, 3, :]}

                def mod_take(c):
                    parts = mod_parts(c)
                    for half in range(2):
                        b = V.take(f"m{c}{half}")
                        mine = [p for p in parts if p[0] == half]
                        for _, lo, hi, vec, d0, d1 in mine:
                            dst = dest[vec][:, d0:d1]
                            last = STT(out=dst, in0=b[:, lo:hi], scalar=1.0 if vec in (1, 4) else 0.0, in1=dst,
                                       op0=ALU.add, op1=ALU.add)
                        took(last)

                v.wait_ge(hy_in, 16 * 11 * (l + 1))
                step(TS(bias_b, bias_b, 2.0 / (2 * S), None, ALU.mult))
                for j in range(3):
                    b = V.take(f"f{j}")
                    took(TS(mlp_y, b[0:64, :], hb[:, j:j + 1], hf[:, j:j + 1], ALU.add, ALU.mult))
                    reduce_angle(step, mlp_y, mlp_k).then_inc(sin_in, 1)
                    if j:
                        v.wait_ge(mod_in, 16 * 7)
                        mod_take(j - 1)
                v.wait_ge(vec_in, 16 * 12 * (l + 1))
                lvv = lv.rearrange("p (a b n) -> p a b n", a=2, b=2)
                lp = f_tmp[:, 0:64].rearrange("p (a n) -> p a n", a=2)
                step(TT(lp, lvv[:, :, 0], lvv[:, :, 1], ALU.mult))
                nc.vector.tensor_reduce(lred, lp, X, ALU.add).then_inc(lam_pre, 1)
                step(TS(gd, gd, lam_b[:, 1:2], None, ALU.mult))
                win = lambda t: window[:, t].unsqueeze(1).to_broadcast([P, 2, CH])
                two = lambda ap: ap.rearrange("p (o c) -> p o c", o=2)
                for t in range(NT):
                    b = V.take(f"h{t}0")
                    took(TT(two(fsum[:, t]), two(b[:, :]), win(t), ALU.mult))
                    b = V.take(f"h{t}1")
                    took(TT(two(f_tmp), two(b[:, :]), win(t), ALU.mult))
                    step(TT(fdif[:, t], fsum[:, t], f_tmp, ALU.subtract))
                    TT(fsum[:, t], fsum[:, t], f_tmp, ALU.add).then_inc(filt_ready, 1)
                b = V.take("fn")
                took(nc.vector.tensor_copy(f_s, b[:, 0:4]))
                v.wait_ge(fscale, 1)
                TT(f_tmp.rearrange("p (j n) -> p j n", j=4), ones[:, :].unsqueeze(1).to_broadcast([P, 4, P]),
                   f_s.unsqueeze(2).to_broadcast([P, 4, P]), ALU.mult).then_inc(srep_ready, 1)
                b = V.take("fnb")
                took(nc.vector.tensor_copy(s_b, b[:, :]))
                mod_take(2)
                step(TT(gsc1, gsc1, ln1, ALU.mult))

                def rows(n, gsc, sh):
                    t = n % NT
                    v.wait_ge(nrs_ready, n + 1)
                    h = h_tok[:, t % 2, :] if n < NT else h2_tok[:, t, :]
                    step(STT(out=h, in0=x_tok[:, t, :], scalar=nrs[:, t:t + 1], in1=gsc, op0=ALU.mult, op1=ALU.mult))
                    TT(h, h, sh, ALU.add).then_inc(hrow_ready, 1)

                rows(0, gsc1, sh1)
                rows(1, gsc1, sh1)
                for m in range(NT):
                    b = V.take(f"fc{m}")
                    took(TT(fc[:, m], b[:, :], s_b, ALU.mult))
                    step(TT(fc[:, m], fc[:, m], bias_b, ALU.add))
                b = V.take("fcn")
                took(TT(f_tmp[0:1, :], b[0:1, :], s_b[0:1, :], ALU.mult))
                step(TT(f_tmp[0:1, :], f_tmp[0:1, :], bias_b[0:1, :], ALU.add))
                step(nc.vector.tensor_copy(fcn, fc[:, 0]))
                step(TS(fcn[0:1, :], f_tmp[0:1, :], 0.5, None, ALU.mult))
                step(TS(fc[0:1, 0], fc[0:1, 0], 0.5, None, ALU.mult))
                for m in range(NT):
                    b = V.take(f"fd{m}")
                    took(TT(fd[:, m], b[:, :], s_b, ALU.mult))


                for t in range(2, NT):
                    done(v, f"hT{t - 2}1")
                    rows(t, gsc1, sh1)
                v.wait_ge(lam_exp, 1)
                step(TT(neglam, lexp[:, 1:2], lexp[:, 0:1], ALU.subtract))
                step(TT(neglam, neglam, lam_b[:, 0:1], ALU.subtract))
                for m in range(6):
                    b = V.take(f"d{m}")
                    v.wait_ge(conv_mid, m + 1)
                    dst = vxT[:, m, :] if m < 4 else ydT[:, m - 4, :]
                    step(STT(out=dst[:, 1:S], in0=b[:, 0:S - 1], scalar=conv_w[:, m:m + 1], in1=dst[:, 1:S],
                             op0=ALU.mult, op1=ALU.add))
                    took(STT(out=dst[:, 0:S - 1], in0=b[:, 1:S], scalar=conv_w[:, 12 + m:13 + m], in1=dst[:, 0:S - 1],
                             op0=ALU.mult, op1=ALU.add))

                rope_before = []

                def rope(src, dst, heads, half, t, sig):
                    base = 0 if half == 16 else 32
                    cos = rope_t[:, t, base:base + half].unsqueeze(1).to_broadcast([P, heads, half])
                    sin = rope_t[:, t, base + half:base + 2 * half].unsqueeze(1).to_broadcast([P, heads, half])
                    if rope_before:
                        v.wait_ge(*rope_before.pop())
                    rope_before.append((sig, t + 1))
                    tmp = [r[:, 0:heads * half].rearrange("p (h c) -> p h c", h=heads) for r in rp]
                    TT(tmp[0], src[:, :, 0], cos, ALU.mult)
                    TT(tmp[1], src[:, :, 1], sin, ALU.mult)
                    TT(tmp[2], src[:, :, 0], sin, ALU.mult)
                    step(TT(tmp[3], src[:, :, 1], cos, ALU.mult))
                    TT(dst[:, :, 0], tmp[0], tmp[1], ALU.subtract)
                    TT(dst[:, :, 1], tmp[2], tmp[3], ALU.add).then_inc(sig, 1)

                for o in range(2):
                    for m in range(NT):
                        b = V.take(f"u{o}{m}")
                        n = o * NT + m
                        if n >= 2:
                            v.wait_ge(y_ready, n - 1)
                        col = slice(o * CH, (o + 1) * CH)
                        if m == 0:
                            TT(cm[:, 0, 0, 0:CH], b[:, 0:CH], fc[:, 0, col], ALU.mult)
                            TT(cm[:, 0, 0, CH:S], b[:, CH:S], fcn[:, col], ALU.mult)
                        else:
                            TT(two(cm[:, m % 2, 0]), two(b[:, :]), fc[:, m, col].unsqueeze(1).to_broadcast([P, 2, CH]), ALU.mult)
                        took(TT(two(cm[:, m % 2, 1]), two(b[:, :]), fd[:, m, col].unsqueeze(1).to_broadcast([P, 2, CH]), ALU.mult))
                    if o == 0:
                        for t in range(NT):
                            b = V.take(f"y0{t}")
                            took(TT(vx_tok[:, t, 0:CH], b[:, 0:CH], vx_tok[:, t, CH:S], ALU.mult))
                        v.wait_ge(crs_ready, 1)
                        for t in range(NT):
                            TS(cols_a[:, t, 0:256], cols_a[:, t, 0:256], crs[:, 2 * t:2 * t + 1], None, ALU.mult)
                            last = TS(cols_a[:, t, 256:384], cols_a[:, t, 256:384], crs[:, 2 * t + 1:2 * t + 2], None, ALU.mult)
                        last.then_inc(cn_ready, 1)
                        for t in range(NT):
                            kpe = cols_a[:, t, 384:416].rearrange("p (h a c) -> p h a c", h=1, a=2)
                            rope(kpe, kpe, 1, 16, t, kpe_ready)
                    else:
                        for c in range(2):
                            b = V.take(f"y1{c}")
                            took(TT(ydT[:, c], b[:, :], ydT[:, c], ALU.mult))
                for t in range(NT):
                    taken(v, f"q{t}")
                    q = q_tok[:, t, :].rearrange("p (h c) -> p h c", h=NH)[:, :, 64:96].rearrange("p h (a c) -> p h a c", a=2)
                    rope(q, q, NH, 16, t, qr_ready)
                done(v, "kv3")
                for t in range(NT):
                    rope(cols_b[:, t, 0:384].rearrange("p (h a c) -> p h a c", h=6, a=2),
                         rope_b[:, t, :].rearrange("p (h a c) -> p h a c", h=6, a=2), 6, 32, t, ropeb_ready)
                done(v, "kTa3")
                for t in range(NT):
                    taken(v, f"c{t}512")
                    rope(cols_c[:, t, 0:512].rearrange("p (h a c) -> p h a c", h=16, a=2),
                         rope_c[:, t, :].rearrange("p (h a c) -> p h a c", h=16, a=2), 16, 16, t, ropec_ready)

                for what, n in steps:
                    if what == "S":
                        g, h, qt, m = maps[n]
                        if g == "b":
                            b = V.take(f"S{n}")
                            lo, hi = band(qt)
                            done(v, f"T{out_of[n - 4]}")
                            pr = prob[:, n % 4, 0:hi - lo]
                            took(STT(out=pr, in0=b[:, lo:hi], scalar=SWA_SCALE, in1=mask[:, lo:hi], op0=ALU.mult, op1=ALU.add))
                            step(nc.vector.tensor_reduce(mx[:, n:n + 1], pr, X, ALU.max))
                            TS(nm[:, n:n + 1], mx[:, n:n + 1], sink[:, h:h + 1], -1.0, ALU.max, ALU.mult).then_inc(swa_s, 1)
                        else:
                            done(v, f"S{n}")
                            nc.vector.tensor_reduce(nm[:, n:n + 1], bank[4 + number[f"S{n}"][1] % 4][:, :], X, ALU.max,
                                                    negate=True).then_inc(nm_ready, 1)
                    elif what == "K":
                            g, h, qt, ms = outs[n]
                            o = n - 2 * NH * NT
                            taken(v, f"S{ms[1]}")
                            m1_, m2_ = ms
                            step(nc.vector.reciprocal(mx[:, m2_:m2_ + 1], rs[:, m2_:m2_ + 1]))
                            step(TS(kap[:, o:o + 1], rs[:, m1_:m1_ + 1], neglam, mx[:, m2_:m2_ + 1], ALU.mult, ALU.mult))
                            STT(out=prob[:, m1_ % 4, :], in0=prob[:, m2_ % 4, :], scalar=kap[:, o:o + 1],
                                in1=prob[:, m1_ % 4, :], op0=ALU.mult, op1=ALU.add).then_inc(diff_ready, 1)
                    elif what == "PV":
                        g, h, qt, ms = outs[n]
                        m0 = ms[0]
                        b = V.take(f"O{n}")
                        if g == "b":
                            v.wait_ge(prob_b, m0 - 15)
                            step(TT(den[:, m0 - 16:m0 - 15], rs[:, m0:m0 + 1], esink[:, m0 - 16:m0 - 15], ALU.add))
                            step(nc.vector.reciprocal(mx[:, m0:m0 + 1], den[:, m0 - 16:m0 - 15]))
                        else:
                            taken(v, f"S{m0}")
                            step(nc.vector.reciprocal(mx[:, m0:m0 + 1], rs[:, m0:m0 + 1]))
                        lo = {"a": 64, "b": h // 2 * 64, "c": h % 2 * 64}[g]
                        c = {"a": 0, "b": 256, "c": 512}[g] + 64 * h
                        took(TS(mix_tok[:, qt, c:c + 64], b[:, lo:lo + 64], mx[:, m0:m0 + 1], None, ALU.mult))
                    elif what == "M":
                        mod_take(n)
                c_out = [mix_tok[:, t, 512:768].rearrange("p (h c) -> p h c", h=NH) for t in range(NT)]
                sq = at(pr_r, 0, NT, NH, 64)
                for t in range(NT):
                    last = TT(sq[:, t], c_out[t], c_out[t], ALU.mult)
                step(last)
                nc.vector.tensor_reduce(dss.rearrange("p (t h) -> p t h", t=NT), sq, X, ALU.add).then_inc(dss_ready, 1)
                v.wait_ge(drs_ready, 1)
                for t in range(NT):
                    last = TT(c_out[t], c_out[t], drs[:, 4 * t:4 * t + 4].unsqueeze(2).to_broadcast([P, NH, 64]), ALU.mult)
                step(last)
                for t in range(NT):
                    last = TT(c_out[t], c_out[t], gd.unsqueeze(1).to_broadcast([P, NH, 64]), ALU.mult)
                last.then_inc(mix_ready, 1)
                for half in range(2):
                    cols = slice(512 * half, 512 * half + 512)
                    for t in range(NT):
                        b = V.take(f"w{half}{t}")
                        tmp = (part[:, 0:512], f_tmp)[t % 2]
                        took(TT(tmp, b[:, :], mod[:, 0, cols], ALU.mult))
                        last = TT(x_tok[:, t, cols], x_tok[:, t, cols], tmp, ALU.add)
                        if half:
                            last.then_inc(x_ready, 1)
                            if t:
                                rows(NT + t - 1, mod[:, 2, :], mod[:, 1, :])
                    if half == 0:
                        v.wait_ge(ln2_in, 16)
                        step(TT(mod[:, 2, :], mod[:, 2, :], ln2, ALU.mult))
                rows(2 * NT - 1, mod[:, 2, :], mod[:, 1, :])

                RED = nc.vector.tensor_reduce
                b = V.take("lg")
                took(nc.vector.tensor_copy(lg, b[:, 0:NT * 36].rearrange("p (t e) -> p t e", t=NT)))
                up = lambda ap, n: ap.unsqueeze(2).to_broadcast([P, NT, n])

                def first_max(src, best, sel, n):
                    step(RED(best, src, X, ALU.max))
                    step(TT(sel, src, up(best, n), ALU.is_equal))
                    step(TT(sel, sel, desc8[:, EPG - n:EPG].unsqueeze(1).to_broadcast([P, NT, n]), ALU.mult))
                    step(RED(pg, sel, X, ALU.max))
                    step(TT(sel, sel, up(pg, n), ALU.is_equal))

                first_max(lg[:, :, 0:NG], gmax, og, NG)
                TT(rd, lg[:, :, 0:NG], up(gmax, NG), ALU.subtract).then_inc(e_in, 1)
                for t in range(NT):
                    last = TT(r_tmp[:, t, :].rearrange("p (g x) -> p g x", g=NG), lg[:, t, NG:36].rearrange("p (g x) -> p g x", g=NG),
                              og[:, t, :].unsqueeze(2).to_broadcast([P, NG, EPG]), ALU.mult)
                step(last)
                step(RED(le, r_tmp.rearrange("p t (g x) -> p t x g", g=NG), X, ALU.add))
                first_max(le, v1, o1, EPG)
                step(STT(out=r_tmp2, in0=o1, scalar=NEG, in1=le, op0=ALU.mult, op1=ALU.add))
                first_max(r_tmp2, v2, o2, EPG)
                TT(vd, v2, v1, ALU.subtract).then_inc(e_in, 1)
                for o, mk in ((o1, m1), (o2, m2)):
                    for t in range(NT):
                        last = TT(mk[:, t, :].rearrange("p (g x) -> p g x", g=NG), o[:, t, :].unsqueeze(1).to_broadcast([P, NG, EPG]),
                                  og[:, t, :].unsqueeze(2).to_broadcast([P, NG, EPG]), ALU.mult)
                step(last)
                TT(msum, m1, m2, ALU.add).then_inc(m_ready, 1)
                v.wait_ge(e_out, 2)
                step(RED(gmax, rd, X, ALU.add))
                step(nc.vector.reciprocal(pg, gmax))
                step(TS(v1, vd, 1.0, None, ALU.add))
                step(nc.vector.reciprocal(v2, v1))
                step(TT(wgt[:, 0], pg, v2, ALU.mult))
                step(TT(wgt[:, 1], wgt[:, 0], vd, ALU.mult))
                b = V.take("before")
                low = b[:, 0:P].rearrange("p (t e) -> p t e", t=NT)
                tot = b[:, P:2 * P].rearrange("p (t e) -> p t e", t=NT)
                step(nc.vector.tensor_copy(cum, low))
                step(RED(cnt, b[:, P:2 * P].rearrange("p (t e) -> p e t", t=NT), X, ALU.add))
                for k in (3, 2, 1):
                    last = TT(cum[:, NT - k:NT], cum[:, NT - k:NT], tot[:, 0:k], ALU.add)
                    if k > 1:
                        step(last)
                took(last)
                for k, mk in ((0, m1), (1, m2)):
                    step(TT(r_tmp, mk, cum, ALU.mult))
                    step(RED(rank_f[:, k], r_tmp, X, ALU.add))
                for k, mk in ((0, m1), (1, m2)):
                    for t in range(NT):
                        TS(rank_is[:, k, t, 0:NE], iota_e, rank_f[:, k, t:t + 1], None, ALU.is_equal)
                        TS(rank_is[:, k, t, NE:CAP], iota_e, float(NE), rank_f[:, k, t:t + 1], ALU.add, ALU.is_equal)
                        last = TS(id_of[:, k, t], mk[:, t, :], tok_id[:, k * NT + t:k * NT + t + 1], None, ALU.mult)
                last.then_inc(hot_ready, 1)
                step(STT(out=cum, in0=cum, scalar=float(NE), in1=iota_e.unsqueeze(1).to_broadcast([P, NT, NE]), op0=ALU.mult, op1=ALU.add))
                for k, mk in ((0, m1), (1, m2)):
                    step(TT(r_tmp, mk, cum, ALU.mult))
                    step(RED(dest_f[:, k], r_tmp, X, ALU.add))
                nc.vector.tensor_copy(dest_i[:, :, :], dest_f).then_inc(dest_ready, 1)

                def indices(src, hi, low, gather, scatter):
                    step(TS(hi, src, float(S), -float(S), ALU.is_ge, ALU.mult))
                    step(TT(low, src, hi, ALU.add))
                    nc.vector.tensor_copy(gather, low)
                    return nc.vector.tensor_copy(scatter, src)

                b = V.take("slots")
                sl = slot_f[0:CAP]
                step(TS(sl, b[0:CAP, NE:2 * NE], -EMPTY, EMPTY, ALU.mult, ALU.add))
                took(TT(sl, sl, b[0:CAP, 0:NE], ALU.add))
                indices(sl, hi_f[0:CAP], gidx_f[0:CAP], gslot_i[0:CAP, :], slot_i[0:CAP, :]).then_inc(slots_ready, 1)
                v.wait_ge(rw_in, 16 * 4)
                e7 = lambda ap: ap.rearrange("p (e j) -> p e j", j=7)
                step(TT(e7(flag), cnt.unsqueeze(2).to_broadcast([P, NE, 7]), e7(block_at), ALU.is_gt))
                step(nc.vector.tensor_tensor_scan(pos, flag, flag, 0.0, ALU.add, ALU.max))
                step(STT(out=pick, in0=pos, scalar=part_id, in1=flag, op0=ALU.is_equal, op1=ALU.mult))
                step(TT(pick, pick, block_id, ALU.mult))
                RED(o_code[:, 0:1], pick, X, ALU.add).then_inc(code_ready, 1)
                step(nc.vector.tensor_copy(tot_i[0:1, 0:1], pos[0:1, NE * 7 - 1:NE * 7]))
                step(nc.vector.tensor_copy(tot_i[0:1, 1:2], over_tot[0:1, 0:1]))
                step(TT(over_tot[0:1, 0:1], over_tot[0:1, 0:1], pos[0:1, NE * 7 - 1:NE * 7], ALU.add))
                b = V.take("over")
                took(nc.vector.tensor_copy(over_i[0:1, :], b[0:1, 0:16]))

                def times_up(b):
                    return TT(act_h[0:CAP, b, :], sil[0:CAP, b, :], bank[2 + b][CAP:P, 0:F], ALU.mult)

                def act_evac(b):
                    return nc.vector.tensor_copy(act_T[:, b, 0:2 * CAP], bank[4 + b][:, 0:2 * CAP])

                def y_evac(b):
                    return nc.vector.tensor_copy(yg[0:CAP, b, 512:1024], bank[6 + b][CAP:P, :])

                def expert(i, s):
                    b = s % 2
                    pre = isinstance(i, int) and i == 0 and s < 2
                    v.wait_ge(silu_ready, 4 * i + s + 1)
                    if not pre:
                        v.wait_ge(at_done, 4 * i + s - 1)
                    times_up(b).then_inc(acth_ready, 1)
                    v.wait_ge(at_done, 4 * i + s + 1)
                    if not pre:
                        v.wait_ge(y_done, 4 * i + s - 1)
                    act_evac(b).then_inc(actT_ready, 1)
                    v.wait_ge(y_done, 4 * i + s + 1)
                    if not pre:
                        v.wait_ge(scattered[b], NE // 2 * 16 * l + 16 * (2 * i + s // 2))
                    y_evac(b).then_inc(yg_hi, 1)

                for s in range(4):
                    expert(0, s)
                with v.Fori(1, NE // 4) as i:
                    for s in range(4):
                        expert(i, s)
                for b in range(2):
                    v.wait_ge(scattered[b], NE // 2 * 16 * l + NE // 2 * 16)
                nc.vector.tensor_copy(part_id, part_id).then_inc(ov_yv, 1)
                n_over = v.value_load(tot_i[0:1, 0:1], min_val=0, max_val=EXTRA)
                with v.If(n_over > 0):
                    with v.Fori(0, EXTRA) as r:
                        with v.If(r < n_over):
                            v.wait_ge(ov_i, 16 * r + 16)
                            v.wait_ge(ov_done, r + 1)
                            TS(hi_f[0:CAP, 0:1], o_idx[0:CAP, 0:1], float(S), -float(S), ALU.is_ge, ALU.mult).then_inc(ov_t, 1)
                            v.wait_ge(ov_t, 2 * r + 1)
                            TT(gidx_f[0:CAP, 0:1], o_idx[0:CAP, 0:1], hi_f[0:CAP, 0:1], ALU.add).then_inc(ov_t, 1)
                            v.wait_ge(ov_t, 2 * r + 2)
                            nc.vector.tensor_copy(gather_i[0:CAP, 0:1], gidx_f[0:CAP, 0:1])
                            nc.vector.tensor_copy(scatter_i[0:CAP, 0:1], o_idx[0:CAP, 0:1]).then_inc(ov_i2, 1)
                            v.wait_ge(ov_sil, r + 1)
                            times_up(0).then_inc(ov_act, 1)
                            v.wait_ge(ov_at, r + 1)
                            act_evac(0).then_inc(ov_aT, 1)
                            v.wait_ge(ov_y, r + 1)
                            y_evac(0).then_inc(ov_yv, 1)
                        with v.Else():
                            v.nop()
                with v.Else():
                    v.nop()
                def residual(t):
                    v.wait_ge(scaled, t + 1)
                    TT(x_tok[:, t, :], x_tok[:, t, :], comb[:, t % 2], ALU.add).then_inc(x_new, 1)

                for t in range(NT):
                    v.wait_ge(gated, t + 1)
                    if t >= 2:
                        v.wait_ge(x_new, t - 1)
                    STT(out=comb[:, t % 2], in0=pair[:, t, 1], scalar=wgt[:, 1, t:t + 1], in1=pair[:, t, 0],
                        op0=ALU.mult, op1=ALU.add).then_inc(summed, 1)
                    if t:
                        residual(t - 1)
                residual(NT - 1)
                v.drain().then_inc(layer_done, 1)

            with v.Fori(0, DEPTH) as l:
                layer(l)
                v.wait_ge(layer_go, l + 1)
            v.wait_ge(final_in, 16)
            for t in range(NT):
                v.wait_ge(fin_rs, t + 1)
                h = h_tok[:, t % 2, :]
                STT(out=h, in0=x_tok[:, t, :], scalar=nrs[:, t:t + 1], in1=gsc1, op0=ALU.mult, op1=ALU.mult).then_inc(fin_row, 1)


_INS = ["x", "c", "positions", "ln1_g", "ln2_g", "ada_w", "ada_b", "w_in", "mla_q_norm", "mla_kv_norm",
        "mla_w_uq", "mla_w_ukv", "swa_sink", "diff_lambda", "diff_norm_g", "hy_conv_w", "hy_conv_b",
        "hy_w1", "hy_b1", "hy_w2", "hy_b2", "hy_w3", "hy_b3", "hy_w4", "hy_sin_freq", "hy_bias", "w_out",
        "router_g_w", "router_g_b", "router_e_w", "router_e_b", "moe_w_gate", "moe_w_up", "moe_w_down",
        "final_g"]


def kernel(**inputs):
    import concourse.bacc as bacc
    from concourse.bass_utils import run_bass_kernel_spmd

    nc = bacc.Bacc("TRN2", target_bir_lowering=False, num_devices=1)
    arrays, aps = {}, {}
    for name, arr in [(n, np.ascontiguousarray(inputs[n])) for n in _INS] + list(host_constants().items()):
        arrays[f"in_{name}_dram"] = arr
        aps[name] = nc.dram_tensor(f"in_{name}_dram", arr.shape, mybir.dt.from_np(arr.dtype), kind="ExternalInput").ap()
    out = nc.dram_tensor("out_0_dram", (1, S, D), F32, kind="ExternalOutput").ap()
    trunk(nc, aps, out)
    r = run_bass_kernel_spmd(nc, [arrays], core_ids=[0])
    return r.results[0]["out_0_dram"]
```
